# Optimizing a Trainium2 kernel written in Bass

```python
import jax, jax.numpy as jnp
from jax import lax
import numpy as np

D_MODEL = 1024
BATCH = 1
SEQ = 256
DEPTH = 2

N_MEM = 256
BRANCH_WIDTH = 512
N_BRANCH = 3
MLA_HEADS = 8
MLA_NOPE = 64
MLA_ROPE = 32
MLA_QK = MLA_NOPE + MLA_ROPE
MLA_V = BRANCH_WIDTH // MLA_HEADS
Q_RANK = 384
KV_RANK = 256
ROPE_THETA = 10000.0
Q_BLOCK = 128
SG_CHUNK = 128
SG_GROUPS = 4
SG_WIDTH = BRANCH_WIDTH
X_HEADS = 4
X_HEAD_DIM = BRANCH_WIDTH // X_HEADS
D_FF = 2688
N_EXPERTS = 8
TOP_K = 2
D_FF_EXPERT = 3584
N_DENSE = (DEPTH + 1) // 2
N_MOE = DEPTH // 2
EPS = 1e-6

P_DQ = Q_RANK
P_DKV = KV_RANK
P_KR = MLA_ROPE
P_SG = 2 * SG_WIDTH
P_XQ = X_HEADS * X_HEAD_DIM
P_GATE = N_BRANCH * D_MODEL
P_TOTAL = P_DQ + P_DKV + P_KR + P_SG + P_XQ + P_GATE
SPLITS = [P_DQ, P_DQ + P_DKV, P_DQ + P_DKV + P_KR, P_DQ + P_DKV + P_KR + P_SG,
          P_DQ + P_DKV + P_KR + P_SG + P_XQ]

kernel_name = 'hybrid_mla_sgmlp_mem_moe_encoder'

def rmsnorm(x, g):
    xf = x.astype(jnp.float32)
    y = xf * lax.rsqrt(jnp.mean(xf * xf, axis=-1, keepdims=True) + EPS)
    return (y * g.astype(jnp.float32)).astype(x.dtype)

def rope(t, positions):
    r = t.shape[-1]
    inv_freq = 1.0 / (ROPE_THETA ** (jnp.arange(0, r, 2, dtype=jnp.float32) / r))
    ang = positions.astype(jnp.float32)[..., None] * inv_freq
    cos = jnp.cos(ang)[:, :, None, :]
    sin = jnp.sin(ang)[:, :, None, :]
    tf = t.astype(jnp.float32)
    t1, t2 = tf[..., : r // 2], tf[..., r // 2:]
    out = jnp.concatenate([t1 * cos - t2 * sin, t1 * sin + t2 * cos], axis=-1)
    return out.astype(t.dtype)

def mla_branch(c_q_raw, c_kv_raw, k_r_raw, positions, g_q, g_kv, w_uq, w_uk, w_uv):
    b, s, _ = c_q_raw.shape
    c_q = rmsnorm(c_q_raw, g_q)
    q = (c_q @ w_uq).reshape(b, s, MLA_HEADS, MLA_QK)
    q = jnp.concatenate([q[..., :MLA_NOPE], rope(q[..., MLA_NOPE:], positions)], axis=-1)
    q = q * (MLA_QK ** -0.5)
    c_kv = rmsnorm(c_kv_raw, g_kv)
    k_nope = (c_kv @ w_uk).reshape(b, s, MLA_HEADS, MLA_NOPE)
    v = (c_kv @ w_uv).reshape(b, s, MLA_HEADS, MLA_V)
    k_rope = rope(k_r_raw[:, :, None, :], positions)
    k = jnp.concatenate([k_nope, jnp.broadcast_to(k_rope, (b, s, MLA_HEADS, MLA_ROPE))], axis=-1)
    qb = q.reshape(b, s // Q_BLOCK, Q_BLOCK, MLA_HEADS, MLA_QK).transpose(1, 0, 2, 3, 4)

    def attend(q_blk):
        sc = jnp.einsum('bqhd,bkhd->bhqk', q_blk, k).astype(jnp.float32)
        pr = jax.nn.softmax(sc, axis=-1).astype(v.dtype)
        return jnp.einsum('bhqk,bkhd->bqhd', pr, v)

    o = lax.map(attend, qb)
    return o.transpose(1, 0, 2, 3, 4).reshape(b, s, MLA_HEADS * MLA_V)

def spatial_gating_branch(z, g_v, w_s, b_s):
    b, s, _ = z.shape
    z = jax.nn.gelu(z)
    u, v = z[..., :SG_WIDTH], z[..., SG_WIDTH:]
    v = rmsnorm(v, g_v)
    vc = v.reshape(b, s // SG_CHUNK, SG_CHUNK, SG_GROUPS, SG_WIDTH // SG_GROUPS)
    sg = jnp.einsum('gij,bnjgc->bnigc', w_s, vc) + b_s.T[None, None, :, :, None]
    return u * sg.reshape(b, s, SG_WIDTH)

def memory_branch(q_raw, mem_n, w_mkv):
    b, s, _ = q_raw.shape
    q = q_raw.reshape(b, s, X_HEADS, X_HEAD_DIM) * (X_HEAD_DIM ** -0.5)
    kv = mem_n @ w_mkv
    m = kv.shape[1]
    k = kv[..., :BRANCH_WIDTH].reshape(b, m, X_HEADS, X_HEAD_DIM)
    v = kv[..., BRANCH_WIDTH:].reshape(b, m, X_HEADS, X_HEAD_DIM)
    sc = jnp.einsum('bshd,bmhd->bhsm', q, k).astype(jnp.float32)
    pr = jax.nn.softmax(sc, axis=-1).astype(v.dtype)
    return jnp.einsum('bhsm,bmhd->bshd', pr, v).reshape(b, s, BRANCH_WIDTH)

def swiglu(h, w1, w3, w2):
    return (jax.nn.silu(h @ w1) * (h @ w3)) @ w2

def moe_swiglu(h, w_router, w1, w3, w2):
    logits = (h @ w_router).astype(jnp.float32)
    top_v, top_i = lax.top_k(logits, TOP_K)
    wts = jax.nn.softmax(top_v, axis=-1)
    combine = jnp.sum(jax.nn.one_hot(top_i, N_EXPERTS, dtype=jnp.float32) * wts[..., None], axis=-2)
    combine = combine.astype(h.dtype)
    out = jnp.zeros_like(h)
    for e in range(N_EXPERTS):
        out = out + combine[..., e:e + 1] * swiglu(h, w1[e], w3[e], w2[e])
    return out

def setup_inputs(seed: int = 0) -> dict:
    key = jax.random.key(seed)
    ks = iter(jax.random.split(key, 40))
    f32 = jnp.float32

    def nrm(shape, fan_in):
        return jax.random.normal(next(ks), shape, f32) * (fan_in ** -0.5)

    def gain(shape):
        return 1.0 + 0.02 * jax.random.normal(next(ks), shape, f32)

    x = jax.random.normal(next(ks), (BATCH, SEQ, D_MODEL), f32)
    mem = jax.random.normal(next(ks), (BATCH, N_MEM, D_MODEL), f32)
    positions = jnp.broadcast_to(jnp.arange(SEQ, dtype=jnp.int32), (BATCH, SEQ))
    return {
        'x': x,
        'mem': mem,
        'positions': positions,
        'g_mix': gain((DEPTH, D_MODEL)),
        'w_in': nrm((DEPTH, D_MODEL, P_TOTAL), D_MODEL),
        'g_q': gain((DEPTH, Q_RANK)),
        'g_kv': gain((DEPTH, KV_RANK)),
        'w_uq': nrm((DEPTH, Q_RANK, MLA_HEADS * MLA_QK), Q_RANK),
        'w_uk': nrm((DEPTH, KV_RANK, MLA_HEADS * MLA_NOPE), KV_RANK),
        'w_uv': nrm((DEPTH, KV_RANK, MLA_HEADS * MLA_V), KV_RANK),
        'g_sg': gain((DEPTH, SG_WIDTH)),
        'w_s': nrm((DEPTH, SG_GROUPS, SG_CHUNK, SG_CHUNK), SG_CHUNK),
        'b_s': gain((DEPTH, SG_GROUPS, SG_CHUNK)),
        'g_mem': gain((D_MODEL,)),
        'w_mkv': nrm((DEPTH, D_MODEL, 2 * BRANCH_WIDTH), D_MODEL),
        'w_br': nrm((DEPTH, N_BRANCH, BRANCH_WIDTH, D_MODEL), BRANCH_WIDTH),
        'b_gate': 0.02 * jax.random.normal(next(ks), (DEPTH, N_BRANCH, D_MODEL), f32),
        'w_out': nrm((DEPTH, D_MODEL, D_MODEL), D_MODEL),
        'g_ffn': gain((DEPTH, D_MODEL)),
        'dense_w1': nrm((N_DENSE, D_MODEL, D_FF), D_MODEL),
        'dense_w3': nrm((N_DENSE, D_MODEL, D_FF), D_MODEL),
        'dense_w2': nrm((N_DENSE, D_FF, D_MODEL), D_FF),
        'w_router': nrm((N_MOE, D_MODEL, N_EXPERTS), D_MODEL),
        'moe_w1': nrm((N_MOE, N_EXPERTS, D_MODEL, D_FF_EXPERT), D_MODEL),
        'moe_w3': nrm((N_MOE, N_EXPERTS, D_MODEL, D_FF_EXPERT), D_MODEL),
        'moe_w2': nrm((N_MOE, N_EXPERTS, D_FF_EXPERT, D_MODEL), D_FF_EXPERT),
        'g_final': gain((D_MODEL,)),
    }

def reference(x, mem, positions, g_mix, w_in, g_q, g_kv, w_uq, w_uk, w_uv, g_sg, w_s, b_s,
              g_mem, w_mkv, w_br, b_gate, w_out, g_ffn, dense_w1, dense_w3, dense_w2,
              w_router, moe_w1, moe_w3, moe_w2, g_final):
    b, s, d = x.shape
    mem_n = rmsnorm(mem, g_mem)
    for l in range(DEPTH):
        h = rmsnorm(x, g_mix[l])
        p = h @ w_in[l]
        c_q, c_kv, k_r, z_sg, q_x, gate_logits = jnp.split(p, SPLITS, axis=-1)
        y_a = mla_branch(c_q, c_kv, k_r, positions, g_q[l], g_kv[l], w_uq[l], w_uk[l], w_uv[l])
        y_b = spatial_gating_branch(z_sg, g_sg[l], w_s[l], b_s[l])
        y_c = memory_branch(q_x, mem_n, w_mkv[l])
        ys = jnp.stack([y_a, y_b, y_c], axis=2)
        yd = jnp.einsum('bsnw,nwd->bsnd', ys, w_br[l])
        gates = jax.nn.sigmoid(gate_logits.reshape(b, s, N_BRANCH, d) + b_gate[l])
        x = x + jnp.sum(gates * yd, axis=2) @ w_out[l]
        h = rmsnorm(x, g_ffn[l])
        if l % 2 == 0:
            j = l // 2
            x = x + swiglu(h, dense_w1[j], dense_w3[j], dense_w2[j])
        else:
            j = l // 2
            x = x + moe_swiglu(h, w_router[j], moe_w1[j], moe_w3[j], moe_w2[j])
    return rmsnorm(x, g_final)


_drawn_inputs = setup_inputs


def setup_inputs(seed=0):
    import zlib

    import numpy as np

    out = dict(_drawn_inputs(seed))
    spreads = {}
    factors = {'g_q': 6.596,
     'g_kv': 5.954,
     'g_sg': 9.946,
     'g_mem': 8.0,
     'b_gate': 4.501,
     'g_final': 7.881,
     'b_s': 7.286,
     'g_ffn': 3.768}
    for name, (base, spread) in spreads.items():
        noise = np.random.default_rng([zlib.crc32(name.encode()), seed]).standard_normal(out[name].shape)
        drawn = base * np.exp(spread * noise) if base else spread * noise
        out[name] = __import__('jax').numpy.asarray(drawn.astype(out[name].dtype))
    for name, factor in factors.items():
        out[name] = (out[name] * factor).astype(out[name].dtype)
    return out
```

```python
from contextlib import ExitStack

import numpy as np

import concourse.bass as bass
from concourse import mybir

F32 = mybir.dt.float32
I32 = mybir.dt.int32
U32 = mybir.dt.uint32
ALU = mybir.AluOpType
ACT = mybir.ActivationFunctionType
AX_X = mybir.AxisListType.X

P = 128
CAP = 96
RING = 7
SLOT = 4096
MIX_RING = 5
HALF = 512
EPS = 1e-6
TWO_PI = 6.283185307179586


class Group:

    def __init__(self, bank, use, per=0):
        self.bank, self.use, self.per = bank, use, per


def plan_psum(depth, heads, x_heads, fcd, fbd, fbm, fcm):
    groups, used, turn = {}, [0] * 8, [0]

    def take(name, bank=None, among=(0, 1, 2, 3, 6, 7)):
        if bank is None:
            bank = among[turn[0] % len(among)]
            turn[0] += 1
        used[bank] += 1
        groups[name] = Group(bank, used[bank])

    take("vecs")
    for l in range(depth):
        take(("wsT", l))
    for n in range(4):
        take(("nT", 0, n))
    for l in range(depth):
        for n in range(2):
            take(("mk", l, n))
        for t in range(2):
            take(("mv", l, t))
        for n in range(4):
            take(("nT", 1 + 2 * l, n))
        for name in ("cq", "ckv", "sv"):
            for t in range(2):
                take((name, l, t))
        for name in ("su", "qx"):
            for n in range(2):
                take((name, l, n))
        for n in range(3):
            take(("cT", l, n))
        for t in range(2):
            for n in range(2):
                take(("q", l, t, n))
        for name in ("k", "v", "sg"):
            for t in range(2):
                take((name, l, t))
        for step in mixer_steps(heads, x_heads):
            if step[0] == "O":
                continue
            take((step[0], l) + step[1:])
        for t in range(2):
            take(("o", l, t), bank=4 + t)
        for n in range(2):
            take(("oT", l, n))
        for d in range(8):
            take(("unit", l, 0, d))
        for t in range(2):
            for n in range(2):
                take(("out", l, t, n))
        for n in range(4):
            take(("nT", 2 + 2 * l, n))
        if l % 2 == 0:
            turn[0] = 0
            for c in range(fcd):
                take(("up", l, c), among=(0, 1, 2, 3))
            for n in range(4):
                take(("y", l, n), bank=4 + n)
            turn[0] = 0
        else:
            take(("logits", l), bank=6)
            take(("rank", l), bank=7)
            take(("gather0", l, 0), bank=7)
            take(("gather0", l, 1), bank=6)
            start = list(used)
            turn[0] = 0
            inside = []
            for c in range(fcm):
                inside.append(("eup", c, c % 4))
                if c == 3:
                    inside.append(("selT", 0, 0))
            inside += [("gather", 0, 7), ("gather", 1, 6), ("ey", 0, 4), ("ey", 1, 5)]
            inside += [("scatter", n, n) for n in range(4)]
            for name, n, bank in inside:
                used[bank] += 1
                groups[name, n] = Group(bank, used[bank])
            for name, n, bank in inside:
                groups[name, n].per = used[bank] - start[bank]
    return groups


def mixer_steps(heads, x_heads):
    steps = []
    fill = [(n, d) for n in (1, 2) for d in range(8)]
    for i in range(x_heads + 2):
        if i < x_heads:
            steps.append(("ms", i))
        if 1 <= i <= x_heads:
            steps.append(("mpT", i - 1))
        if i >= 2:
            steps.append(("mo", i - 2))
        steps.append(("unit", *fill.pop(0)))
    for i in range(4):
        steps += [("qT", i // 2, i % 2), ("kT", i // 2, i % 2)]
    for i in range(heads + 2):
        if i < heads:
            steps.append(("as", i))
        if 1 <= i <= heads:
            steps.append(("apT", i - 1))
        if i >= 2:
            steps.append(("O", i - 2))
        steps.append(("unit", *fill.pop(0)))
    assert not fill
    return steps


def build(nc, x, mem, positions, g_mix, w_in, g_q, g_kv, w_uq, w_uk, w_uv, g_sg, w_s, b_s, g_mem,
          w_mkv, w_br, b_gate, w_out, g_ffn, dense_w1, dense_w3, dense_w2, w_router, moe_w1, moe_w3,
          moe_w2, g_final, out):
    DEPTH, D, PT = w_in.shape
    SEQ = x.shape[1]
    QR, KVR = g_q.shape[1], g_kv.shape[1]
    SG = g_sg.shape[1]
    G = w_s.shape[1]
    NBR, BW = w_br.shape[1], w_br.shape[2]
    NOPE, ROPE, H, XH = 64, 32, 8, 4
    QK = NOPE + ROPE
    FD, FE, NE = dense_w1.shape[2], moe_w1.shape[3], moe_w1.shape[1]
    T, KD = SEQ // P, D // P
    KB = BW // P
    FCD, FCM = FD // P, FE // P
    BD, BM = 3, 4
    NBLK = FCD // BD
    assert T == 2 and KD == 8 and NBLK * BD == FCD and NBLK * BM == FCM and FCM % 4 == 0
    C_KV, C_SG = QR, QR + KVR + ROPE
    C_XQ = C_SG + 2 * SG
    C_GATE = C_XQ + BW
    JOBS = NE * (-(-SEQ // CAP))
    QS, XS = QK ** -0.5, (BW // XH) ** -0.5
    steps = mixer_steps(H, XH)
    groups = plan_psum(DEPTH, H, XH, FCD, BD, BM, FCM)

    with ExitStack() as ctx:
        def sb(name, shape, dt=F32):
            return ctx.enter_context(nc.sbuf_tensor(name, shape, dt))

        def sem(name):
            return ctx.enter_context(nc.semaphore(name))

        banks = [ctx.enter_context(nc.psum_tensor(f"bank{i}", [P, HALF], F32)) for i in range(8)]
        bank_full = [sem(f"bank_full{i}") for i in range(8)]
        bank_free = [sem(f"bank_free{i}") for i in range(8)]

        ring = sb("ring", [P, RING * SLOT])
        x_sb = sb("x_sb", [P, T, D])
        hn = sb("hn", [P, T, D])
        hT = sb("hT", [P, KD, SEQ])
        memT = sb("memT", [P, KD, SEQ])
        mixT = sb("mixT", [P, KD, SEQ])
        cqkv = sb("cqkv", [P, T, QR + KVR + ROPE])
        cT = sb("cT", [P, 5, SEQ])
        sgv = sb("sgv", [P, T * SG])
        uT = sb("uT", [P, G, SEQ])
        qxT = sb("qxT", [P, XH, SEQ])
        mkT = sb("mkT", [P, XH, SEQ])
        mv = sb("mv", [P, T, BW])
        prob = sb("prob", [P, 2, T, SEQ])
        probT = sb("probT", [P, 2, T, SEQ])
        wsT = sb("wsT", [P, DEPTH, G, P])
        bs_row = sb("bs_row", [P, DEPTH, G * P])
        ident = sb("ident", [P, P])
        lower = sb("lower", [P, P])
        ones = sb("ones", [P, P])
        sig = sb("sig", [P, 2, SEQ])
        iota_cap = sb("iota_cap", [P, CAP])
        iota_e = sb("iota_e", [P, NE])
        n_vec = 2 * DEPTH * KD + KD + DEPTH * (3 + 2 + G) + DEPTH * NBR * KD
        vec_rows = uT[0:n_vec, 0, 0:P]
        cols = sb("cols", [P, n_vec])
        half_gate = sb("half_gate", [P, DEPTH * NBR * KD])
        inv_freq = sb("inv_freq", [P, ROPE // 2])
        pos_i = sb("pos_i", [P, T], I32)
        pos_f = sb("pos_f", [P, T])
        ang = sb("ang", [P, 4, T, ROPE // 2])
        gated_tmp = sb("gated_tmp", [P, 2, SEQ])
        cos_t = sb("cos_t", [P, T, ROPE // 2])
        sin_t = sb("sin_t", [P, T, ROPE // 2])
        sumsq = sb("sumsq", [P, 8])
        rin = sb("rin", [P, 8])
        nr = sb("nr", [P, 3, 8])
        rmax = sb("rmax", [P, 2, T])
        nmax = sb("nmax", [P, 2, T])
        rsum = sb("rsum", [P, 2, T])
        rrec = sb("rrec", [P, 2, T])
        asum = sb("asum", [P, T, H])
        arec = sb("arec", [P, T, H])
        wrt = sb("wrt", [P, KD, NE])
        logits = sb("logits", [P, T, NE])
        top_v = sb("top_v", [P, T, 8])
        top_i = sb("top_i", [P, T, 8], U32)
        top_f = sb("top_f", [P, T, 8])
        gap = sb("gap", [P, 4, T])
        hot = sb("hot", [P, 2, T, NE])
        mask = sb("mask", [P, T, NE])
        comb = sb("comb", [P, T, JOBS + 8])
        rank = sb("rank", [P, T, JOBS + 8])
        cur = sb("cur", [P, 2, T])
        most = sb("most", [P, 2])
        more = sb("more", [P, 1], I32)

        scratch = ring[:, MIX_RING * SLOT:]
        q_sb = scratch[:, 0:T * H * QK].rearrange("p (t h d) -> p t h d", t=T, h=H)
        k_sb = scratch[:, 1536:1536 + T * H * QK].rearrange("p (t h d) -> p t h d", t=T, h=H)
        v_sb = scratch[:, 3072:3072 + T * BW].rearrange("p (t c) -> p t c", t=T)
        qT = scratch[:, 4096:4096 + H * SEQ].rearrange("p (h s) -> p h s", h=H)
        kT = scratch[:, 6144:6144 + H * SEQ].rearrange("p (h s) -> p h s", h=H)
        ws_raw = probT[:, :, :, :].rearrange("p a b c -> p (a b c)").rearrange(
            "p (l g j) -> p l g j", l=DEPTH, g=G)
        junk = prob[:, :, :, :].rearrange("p a b c -> p (a b c)")
        mem_sb = mixT[:, :, :].rearrange("p k s -> p (k s)").rearrange("p (t c) -> p t c", t=T)
        gf_row = mixT[:, :, :].rearrange("p k s -> p (k s)")[:, 0:D]
        o_sb = cqkv[:, :, :].rearrange("p t c -> p (t c)")[:, 0:T * BW].rearrange(
            "p (t c) -> p t c", t=T)
        sv = sgv[:, :].rearrange("p (t c) -> p t c", t=T)
        yaT = sgv[:, :].rearrange("p (k s) -> p k s", s=SEQ)
        mk_flat = mkT[:, :, :].rearrange("p k s -> p (k s)")
        mv_flat = mv[:, :, :].rearrange("p k s -> p (k s)")
        gated_d = [v[:, 0:BD * SEQ].rearrange("p (c s) -> p c s", c=BD) for v in (mk_flat, mv_flat)]
        gated_m = [v[:, 0:BM * CAP].rearrange("p (c s) -> p c s", c=BM) for v in (mk_flat, mv_flat)]
        silu_d = junk[:, 0:4 * SEQ].rearrange("p (n s) -> p n s", n=4)
        silu_m = junk[:, 0:4 * CAP].rearrange("p (n s) -> p n s", n=4)
        hselT = sgv[:, 0:KD * CAP].rearrange("p (k s) -> p k s", k=KD)
        y_sb = qxT[:, :, :].rearrange("p k s -> p (k s)")
        pT_flat = probT[:, :, :, :].rearrange("p a b c -> p (a b c)")
        sel = pT_flat[:, 0:T * CAP].rearrange("p (t s) -> p t s", t=T)
        selT = pT_flat[:, 256:256 + T * P].rearrange("p (t s) -> p t s", t=T)

        at, c_of = 0, {}
        for name, n in (("mix", DEPTH * KD), ("ffn", DEPTH * KD), ("mem", KD), ("q", DEPTH * 3),
                        ("kv", DEPTH * 2), ("sg", DEPTH * G), ("gate", DEPTH * NBR * KD)):
            c_of[name] = at
            at += n

        vecs_in = sem("vecs_in")
        x_in = sem("x_in")
        mem_in = sem("mem_in")
        ws_in = sem("ws_in")
        row_in = sem("row_in")
        pos_in = sem("pos_in")
        router_in = sem("router_in")
        gf_in = sem("gf_in")
        stored = sem("stored")
        slot_in = [sem(f"slot_in{i}") for i in range(RING)]
        down_done = sem("down_done")
        pool_step = sem("pool_step")
        consts = sem("consts")
        dve_step = sem("dve_step")
        angles = sem("angles")
        trig = sem("trig")
        squares = sem("squares")
        hn_ready = sem("hn_ready")
        lat_inv = sem("lat_inv")
        vn_ready = sem("vn_ready")
        yb_ready = sem("yb_ready")
        q_ready = sem("q_ready")
        k_ready = sem("k_ready")
        max_ready = sem("max_ready")
        prob_ready = sem("prob_ready")
        tanh_ready = sem("tanh_ready")
        merged = sem("merged")
        silu_ready = sem("silu_ready")
        gap_ready = sem("gap_ready")
        gap_exp = sem("gap_exp")
        mask_ready = sem("mask_ready")
        flag_ready = sem("flag_ready")
        e_silu = sem("e_silu")
        cur_ready = sem("cur_ready")
        sel_ready = sem("sel_ready")
        y_final = sem("y_final")

        def rows(w, c0, c1, r0=0, r1=None):
            r1 = w.shape[0] if r1 is None else r1
            return w[r0:r1, c0:c1].rearrange("(k p) c -> p k c", p=P)

        loads, slot_of, number = [], {}, {}

        def load(name, slot, *parts):
            number[name], slot_of[name] = len(loads), slot
            loads.append((name, slot, parts))

        for l in range(DEPTH):
            wi, i0 = w_in[l], len(loads)

            def mixer_load(name, *parts):
                load((name, l), (len(loads) - i0) % MIX_RING, *parts)

            mixer_load("mk", rows(w_mkv[l], 0, BW))
            mixer_load("mv", rows(w_mkv[l], BW, 2 * BW))
            mixer_load("cq", rows(wi, 0, C_KV))
            mixer_load("ckv", rows(wi, C_KV, C_SG))
            mixer_load("sv", rows(wi, C_SG + SG, C_XQ))
            mixer_load("su", rows(wi, C_SG, C_SG + SG))
            mixer_load("qx", rows(wi, C_XQ, C_GATE))
            mixer_load("uq", rows(w_uq[l], 0, H * QK))
            mixer_load("ukv", rows(w_uk[l], 0, H * NOPE), rows(w_uv[l], 0, BW))
            for n in (1, 2, 0):
                for f in range(2):
                    mixer_load(f"gate{n}{f}", rows(wi, C_GATE + n * D + f * HALF,
                                                   C_GATE + n * D + (f + 1) * HALF))
                mixer_load(f"br{n}", rows(w_br[l, n], 0, D))
            for f in range(2):
                mixer_load(f"out{f}", rows(w_out[l], f * HALF, (f + 1) * HALF))
            if l % 2 == 0:
                i1, j = len(loads), l // 2
                for b in range(NBLK + 1):
                    if b < NBLK:
                        for name, w in (("w1", dense_w1), ("w3", dense_w3)):
                            load((name, l, b), (len(loads) - i1) % RING,
                                 rows(w[j], b * BD * P, (b + 1) * BD * P))
                    if b:
                        load(("w2", l, b - 1), (len(loads) - i1) % RING,
                             rows(dense_w2[j], 0, D, (b - 1) * BD * P, b * BD * P))
        E0 = len(loads)
        e_loads = []
        for b in range(NBLK):
            e_loads += [("w1", b), ("w3", b)]
            if b and b < NBLK - 1:
                e_loads.append(("w2", b - 1))
        e_loads += [("w2", NBLK - 2), ("w2", NBLK - 1)]
        PER_E = len(e_loads)
        assert PER_E % RING == 0
        e_at = {key: i for i, key in enumerate(e_loads)}

        def slot_count(name):
            n, s = number[name], slot_of[name]
            return s, 16 * sum(len(parts) for _, t, parts in loads[:n + 1] if t == s)

        e_base = [16 * sum(len(parts) for _, t, parts in loads if t == s) for s in range(RING)]

        def slot_view(slot, chunks, width, offset=0):
            a = slot * SLOT + offset
            return ring[:, a:a + chunks * width].rearrange("p (k c) -> p k c", k=chunks)

        def weight(pe, name, chunks, width, offset=0):
            s, count = slot_count(name)
            pe.wait_ge(slot_in[s], count)
            return slot_view(s, chunks, width, offset)

        def full(eng, name, j=0):
            g = groups[name]
            eng.wait_ge(bank_full[g.bank], g.use + g.per * j)
            return banks[g.bank]

        def read(eng, name, j=0):
            g = groups[name]
            eng.wait_ge(bank_free[g.bank], g.use + g.per * j)

        def claim(pe, name, j=0):
            g = groups[name]
            if g.use > 1:
                pe.wait_ge(bank_free[g.bank], g.use - 1 + g.per * j)
            return banks[g.bank]

        def done(ins, name):
            ins.then_inc(bank_full[groups[name].bank], 1)

        def free(ins, name):
            ins.then_inc(bank_free[groups[name].bank], 1)

        def last_reader(kind, l, b=None):
            if kind in ("w1", "w3"):
                return "up", l, b * BD + BD - 1
            if kind == "w2":
                return ("y", l, 3) if b == NBLK - 1 else None
            if kind in ("mv", "cq", "ckv", "sv"):
                return kind, l, T - 1
            if kind in ("mk", "su", "qx"):
                return kind, l, 1
            if kind == "uq":
                return "q", l, T - 1, 1
            if kind == "ukv":
                return "v", l, T - 1
            if kind.startswith("gate"):
                return "unit", l, int(kind[4]), 4 * int(kind[5]) + 3
            if kind.startswith("br"):
                return "unit", l, int(kind[2]), KD - 1
            return "out", l, T - 1, int(kind[3])

        unit_names = [("unit", l) + s[1:] for l in range(DEPTH)
                      for s in [s for s in steps if s[0] == "unit"] + [("unit", 0, d) for d in range(KD)]]
        N_SQ, n = [T], T
        for l in range(DEPTH):
            N_SQ += [n + T, n + 5 * T]
            n += 5 * T
        N_SQ.append(n + T)
        DOWNS = NBLK - 1

        block = ctx.enter_context(nc.Block())

        @block.sync
        def _(sp):
            last_in_slot = {}

            def until_used(key):
                name = last_reader(*key)
                if name is None:
                    sp.wait_ge(down_done, key[2] + 1)
                else:
                    full(sp, name)

            for key, slot, parts in loads:
                if slot in last_in_slot:
                    until_used(last_in_slot[slot])
                if slot >= MIX_RING:
                    read(sp, ("o", key[1], T - 1))
                offset = 0
                for src in parts:
                    chunks, width = src.shape[1], src.shape[2]
                    sp.dma_start(slot_view(slot, chunks, width, offset), src).then_inc(slot_in[slot], 16)
                    offset += chunks * width
                last_in_slot[slot] = key

            def expert_loads(j, e, first):
                for i, (kind, b) in enumerate(e_loads):
                    slot = i % RING
                    if first and i < RING:
                        until_used(last_in_slot[slot])
                        if slot >= MIX_RING:
                            read(sp, ("o", DEPTH - 1, T - 1))
                    else:
                        old, job = e_loads[i - RING], (j if i >= RING else j - 1)
                        if old[0] != "w2":
                            full(sp, ("eup", old[1] * BM + BM - 1), job)
                        elif old[1] == NBLK - 1:
                            full(sp, ("ey", 1), job)
                        else:
                            sp.wait_ge(down_done, DOWNS * (job + 1) + old[1] + 1)
                    if kind == "w2":
                        src = moe_w2[0, e, b * BM * P:(b + 1) * BM * P, :].rearrange("(k p) c -> p k c", p=P)
                        dst = slot_view(slot, BM, D)
                    else:
                        w = moe_w1 if kind == "w1" else moe_w3
                        src = w[0, e, :, b * BM * P:(b + 1) * BM * P].rearrange("(k p) c -> p k c", p=P)
                        dst = slot_view(slot, KD, BM * P)
                    sp.dma_start(dst, src).then_inc(slot_in[slot], 16)

            expert_loads(0, 0, True)
            with sp.Fori(1, NE) as e:
                expert_loads(e, e, False)
            read(sp, ("nT", 2 * DEPTH, 3))
            sp.dma_start(gf_row, g_final.partition_broadcast(P)).then_inc(gf_in, 16)
            sp.wait_ge(flag_ready, 1)
            overflow = sp.value_load(more[0:1, 0:1], min_val=0, max_val=1)
            with sp.If(overflow > 0):
                with sp.Fori(NE, JOBS, NE) as j0:
                    with sp.Fori(0, NE) as e:
                        expert_loads(j0 + e, e, False)
            for t in range(T):
                sp.wait_ge(y_final, t + 1)
                sp.dma_start(out[0, t * P:(t + 1) * P, :], hn[:, t, :]).then_inc(stored, 16)
            sp.wait_ge(stored, 16 * T)

        @block.gpsimd
        def _(pool):
            n = 0
            for tile, value in ((ident, 0.0), (lower, 1.0), (ones, 1.0)):
                nc.gpsimd.memset(tile[:, :], value).then_inc(pool_step, 1)
            for i in range(ROPE // 2):
                f = np.float32(1.0) / np.power(np.float32(10000.0), np.float32(2 * i) / np.float32(ROPE))
                nc.gpsimd.memset(inv_freq[:, i:i + 1], float(f)).then_inc(pool_step, 1)
            pool.wait_ge(pool_step, 3)
            nc.gpsimd.affine_select(out=ident[:, :], in_=ident[:, :], compare_op=ALU.not_equal, fill=1.0,
                                    base=0, pattern=[[-1, P]], channel_multiplier=1).then_inc(consts, 1)
            nc.gpsimd.affine_select(out=lower[:, :], in_=lower[:, :], compare_op=ALU.is_gt, fill=0.0,
                                    base=0, pattern=[[1, P]], channel_multiplier=-1).then_inc(consts, 1)
            nc.gpsimd.iota(iota_cap[:, :], pattern=[[1, CAP]], base=0, channel_multiplier=0,
                           allow_small_or_imprecise_dtypes=True).then_inc(consts, 1)
            nc.gpsimd.iota(iota_e[:, :], pattern=[[1, NE]], base=0, channel_multiplier=0,
                           allow_small_or_imprecise_dtypes=True).then_inc(consts, 1)
            nc.gpsimd.memset(rank[:, :, :], -1.0).then_inc(consts, 1)
            nc.gpsimd.memset(comb[:, :, :], 0.0).then_inc(consts, 1)

        N_CONST = 6

        @block.tensor
        def _(pe):
            def acc(bank, lhs, rhs, n, **kw):
                for k in range(n):
                    ins = nc.tensor.matmul(bank, lhs(k), rhs(k), start=(k == 0), stop=(k == n - 1), **kw)
                return ins

            def tok(t):
                return slice(t * P, (t + 1) * P)

            pe.wait_ge(consts, 1)
            pe.wait_ge(vecs_in, 16 * 7)
            b = claim(pe, "vecs")
            done(nc.tensor.transpose(b[:, 0:n_vec], vec_rows, ident[0:n_vec, 0:n_vec]), "vecs")
            pe.wait_ge(ws_in, 16)
            for l in range(DEPTH):
                b = claim(pe, ("wsT", l))
                for g in range(G):
                    ins = nc.tensor.transpose(b[:, g * P:(g + 1) * P], ws_raw[:, l, g, :], ident[:, :])
                done(ins, ("wsT", l))

            def transpose_norm(i):
                pe.wait_ge(hn_ready, T * (i + 1))
                for n in range(4):
                    b = claim(pe, ("nT", i, n))
                    for c in range(2):
                        for t in range(T):
                            a = c * SEQ + t * P
                            ins = nc.tensor.transpose(b[:, a:a + P], hn[:, t, (2 * n + c) * P:(2 * n + c + 1) * P],
                                                      ident[:, :])
                    done(ins, ("nT", i, n))

            transpose_norm(0)
            for l in range(DEPTH):
                def token_major(name, width):
                    w = weight(pe, (name, l), KD, width)
                    for t in range(T):
                        b = claim(pe, (name, l, t))
                        ins = acc(b[:, 0:width], lambda k: hT[:, k, tok(t)], lambda k: w[:, k, :], KD)
                        done(ins, (name, l, t))

                def transposed(name, src):
                    w = weight(pe, (name, l), KD, HALF)
                    for n in range(2):
                        b = claim(pe, (name, l, n))
                        for c in range(2):
                            a = (2 * n + c) * P
                            ins = acc(b[:, c * SEQ:(c + 1) * SEQ], lambda k: w[:, k, a:a + P],
                                      lambda k: src[:, k, :], KD)
                        done(ins, (name, l, n))

                for n in range(4):
                    read(pe, ("nT", 0, n))
                transposed("mk", memT)
                w = weight(pe, ("mv", l), KD, HALF)
                for t in range(T):
                    b = claim(pe, ("mv", l, t))
                    ins = acc(b[:, :], lambda k: memT[:, k, tok(t)], lambda k: w[:, k, :], KD)
                    done(ins, ("mv", l, t))

                transpose_norm(1 + 2 * l)
                for n in range(4):
                    read(pe, ("nT", 1 + 2 * l, n))
                token_major("cq", QR)
                token_major("ckv", KVR + ROPE)
                token_major("sv", SG)
                transposed("su", hT)
                transposed("qx", hT)

                for t in range(T):
                    read(pe, ("ckv", l, t))
                    read(pe, ("cq", l, t))
                for n in range(3):
                    b = claim(pe, ("cT", l, n))
                    for c in range(2 if n < 2 else 1):
                        for t in range(T):
                            a = c * SEQ + t * P
                            ins = nc.tensor.transpose(b[:, a:a + P], cqkv[:, t, (2 * n + c) * P:(2 * n + c + 1) * P],
                                                      ident[:, :])
                    done(ins, ("cT", l, n))
                w = weight(pe, ("uq", l), 3, H * QK)
                for n in range(3):
                    read(pe, ("cT", l, n))
                for t in range(T):
                    for n in range(2):
                        b = claim(pe, ("q", l, t, n))
                        ins = acc(b[:, 0:384], lambda k: cT[:, k, tok(t)], lambda k: w[:, k, n * 384:(n + 1) * 384], 3)
                        done(ins, ("q", l, t, n))
                wk = weight(pe, ("ukv", l), 2, BW)
                wv = slot_view(slot_of["ukv", l], 2, BW, 2 * BW)
                for name, w in (("k", wk), ("v", wv)):
                    for t in range(T):
                        b = claim(pe, (name, l, t))
                        ins = acc(b[:, :], lambda k: cT[:, 3 + k, tok(t)], lambda k: w[:, k, :], 2)
                        done(ins, (name, l, t))
                pe.wait_ge(vn_ready, T * (l + 1))
                read(pe, ("wsT", l))
                for t in range(T):
                    b = claim(pe, ("sg", l, t))
                    for g in range(G):
                        ins = nc.tensor.matmul(b[:, g * P:(g + 1) * P], sv[:, t, g * P:(g + 1) * P],
                                               wsT[:, l, g, :], start=True, stop=True)
                    done(ins, ("sg", l, t))

                def unit(n, d):
                    f, a = d // 4, d % 4 * P
                    wg = weight(pe, (f"gate{n}{f}", l), KD, HALF)
                    wb = weight(pe, (f"br{n}", l), KB, D)
                    name = ("unit", l, n, d)
                    if d == 0:
                        if n == 1:
                            pe.wait_ge(yb_ready, T * (l + 1))
                        elif n == 2:
                            for h in range(XH):
                                read(pe, ("mo", l, h))
                        else:
                            for c in range(2):
                                read(pe, ("oT", l, c))
                    y = (yaT, uT, qxT)[n]
                    b = claim(pe, name)
                    ins = acc(b[:, 0:SEQ], lambda k: wg[:, k, a:a + P], lambda k: hT[:, k, :], KD)
                    ins = acc(b[:, SEQ:2 * SEQ], lambda k: wb[:, k, d * P:(d + 1) * P], lambda k: y[:, k, :], KB)
                    done(ins, name)

                for step in steps:
                    kind = step[0]
                    name = (kind, l) + step[1:]
                    if kind == "ms":
                        h = step[1]
                        if h == 0:
                            for n in range(2):
                                read(pe, ("qx", l, n))
                                read(pe, ("mk", l, n))
                        b = claim(pe, name)
                        for t in range(T):
                            ins = nc.tensor.matmul(b[:, t * SEQ:(t + 1) * SEQ], qxT[:, h, tok(t)], mkT[:, h, :],
                                                   start=True, stop=True)
                        done(ins, name)
                    elif kind in ("mpT", "apT"):
                        h = step[1]
                        nth = l * (XH + H) + h + (XH if kind == "apT" else 0)
                        if kind == "mpT":
                            pe.wait_ge(prob_ready, l * XH + h + 1)
                        else:
                            read(pe, ("as", l, h))
                        b = claim(pe, name)
                        for kt in range(T):
                            for t in range(T):
                                a = kt * SEQ + t * P
                                ins = nc.tensor.transpose(b[:, a:a + P], prob[:, nth % 2, t, tok(kt)], ident[:, :])
                        done(ins, name)
                    elif kind == "mo":
                        h = step[1]
                        nth = l * (XH + H) + h
                        read(pe, ("mpT", l, h))
                        if h == 0:
                            for t in range(T):
                                read(pe, ("mv", l, t))
                        b = claim(pe, name)
                        ins = acc(b[:, 0:SEQ], lambda k: mv[:, k, tok(h)], lambda k: probT[:, nth % 2, k, :], T)
                        done(ins, name)
                    elif kind in ("qT", "kT"):
                        t, n = step[1:]
                        if n == 0:
                            pe.wait_ge(q_ready if kind == "qT" else k_ready, l + 1)
                        src = q_sb if kind == "qT" else k_sb
                        b = claim(pe, name)
                        for h in range(4):
                            ins = nc.tensor.transpose(b[0:QK, h * P:(h + 1) * P], src[:, t, 4 * n + h, :], ident[:, :])
                        done(ins, name)
                    elif kind == "as":
                        h = step[1]
                        if h == 0:
                            for t in range(T):
                                for n in range(2):
                                    read(pe, ("qT", l, t, n))
                                    read(pe, ("kT", l, t, n))
                        b = claim(pe, name)
                        for t in range(T):
                            ins = nc.tensor.matmul(b[:, t * SEQ:(t + 1) * SEQ], qT[0:QK, h, tok(t)], kT[0:QK, h, :],
                                                   start=True, stop=True)
                        done(ins, name)
                    elif kind == "O":
                        h = step[1]
                        nth = l * (XH + H) + XH + h
                        read(pe, ("apT", l, h))
                        for t in range(T):
                            if h == 0:
                                read(pe, ("v", l, 0))
                                read(pe, ("v", l, 1))
                                claim(pe, ("o", l, t))
                            b = banks[4 + t]
                            ins = acc(b[:, h * 64:(h + 1) * 64], lambda k: probT[:, nth % 2, k, tok(t)],
                                      lambda k: v_sb[:, k, h * 64:(h + 1) * 64], T)
                            if h == H - 1:
                                done(ins, ("o", l, t))
                    else:
                        unit(*step[1:])
                for t in range(T):
                    read(pe, ("o", l, t))
                for n in range(2):
                    b = claim(pe, ("oT", l, n))
                    for c in range(2):
                        for t in range(T):
                            a = c * SEQ + t * P
                            ins = nc.tensor.transpose(b[:, a:a + P], o_sb[:, t, (2 * n + c) * P:(2 * n + c + 1) * P],
                                                      ident[:, :])
                    done(ins, ("oT", l, n))
                for d in range(8):
                    unit(0, d)
                pe.wait_ge(merged, KD * (l + 1))
                ws = [weight(pe, (f"out{n}", l), KD, HALF) for n in range(2)]
                for t in range(T):
                    for n in range(2):
                        b = claim(pe, ("out", l, t, n))
                        ins = acc(b[:, :], lambda k: mixT[:, k, tok(t)], lambda k: ws[n][:, k, :], KD)
                        done(ins, ("out", l, t, n))
                transpose_norm(2 + 2 * l)
                for n in range(4):
                    read(pe, ("nT", 2 + 2 * l, n))
                if l % 2 == 0:
                    def up(b_):
                        w1 = weight(pe, ("w1", l, b_), KD, BD * P)
                        w3 = weight(pe, ("w3", l, b_), KD, BD * P)
                        for cc in range(BD):
                            name = ("up", l, b_ * BD + cc)
                            b = claim(pe, name)
                            a = cc * P
                            acc(b[:, 0:SEQ], lambda k: w1[:, k, a:a + P], lambda k: hT[:, k, :], KD)
                            ins = acc(b[:, SEQ:2 * SEQ], lambda k: w3[:, k, a:a + P], lambda k: hT[:, k, :], KD)
                            done(ins, name)

                    def down(b_):
                        w2 = weight(pe, ("w2", l, b_), BD, D)
                        read(pe, ("up", l, b_ * BD + BD - 1))
                        for cc in range(BD):
                            for t in range(T):
                                for n in range(2):
                                    name = ("y", l, 2 * t + n)
                                    if b_ == 0 and cc == 0:
                                        claim(pe, name)
                                    last = b_ == NBLK - 1 and cc == BD - 1
                                    ins = nc.tensor.matmul(
                                        banks[4 + 2 * t + n][:, :], gated_d[b_ % 2][:, cc, tok(t)],
                                        w2[:, cc, n * HALF:(n + 1) * HALF], start=(b_ == 0 and cc == 0), stop=last)
                                    if last:
                                        done(ins, name)
                        if b_ < NBLK - 1:
                            ins.then_inc(down_done, 1)

                    for b_ in range(NBLK + 1):
                        if b_ < NBLK:
                            up(b_)
                        if b_:
                            down(b_ - 1)

            l = DEPTH - 1
            pe.wait_ge(router_in, 16)
            b = claim(pe, ("logits", l))
            for t in range(T):
                ins = acc(b[:, t * NE:(t + 1) * NE], lambda k: hT[:, k, tok(t)], lambda k: wrt[:, k, :], KD)
            done(ins, ("logits", l))
            pe.wait_ge(consts, N_CONST)
            pe.wait_ge(mask_ready, 1)
            b = claim(pe, ("rank", l))
            nc.tensor.matmul(b[:, 0:NE], lower[:, :], mask[:, 0, :], start=True, stop=True)
            nc.tensor.matmul(b[:, NE:2 * NE], ones[:, :], mask[:, 0, :], start=True, stop=False)
            nc.tensor.matmul(b[:, NE:2 * NE], lower[:, :], mask[:, 1, :], start=False, stop=True)
            nc.tensor.matmul(b[:, 2 * NE:3 * NE], ones[:, :], mask[:, 0, :], start=True, stop=False)
            ins = nc.tensor.matmul(b[:, 2 * NE:3 * NE], ones[:, :], mask[:, 1, :], start=False, stop=True)
            done(ins, ("rank", l))

            def gather(name, n, j):
                b = claim(pe, name, j)
                for c in range(4):
                    k = 4 * n + c
                    ins = acc(b[:, c * CAP:(c + 1) * CAP], lambda t: hn[:, t, k * P:(k + 1) * P],
                              lambda t: sel[:, t, :], T)
                done(ins, name)

            pe.wait_ge(sel_ready, 1)
            for n in range(2):
                gather(("gather0", l, n), n, 0)

            def e_weight(kind, b_, j):
                i = e_at[kind, b_]
                slot, nth = i % RING, i // RING
                pe.wait_ge(slot_in[slot], e_base[slot] + 16 * (nth + 1) + 16 * (PER_E // RING) * j)
                return slot_view(slot, BM, D) if kind == "w2" else slot_view(slot, KD, BM * P)

            def expert(j):
                for n in range(2):
                    read(pe, ("gather", n), j - 1)

                def up(b_):
                    w1, w3 = e_weight("w1", b_, j), e_weight("w3", b_, j)
                    for cc in range(BM):
                        name = ("eup", b_ * BM + cc)
                        b = claim(pe, name, j)
                        a = cc * P
                        acc(b[:, 0:CAP], lambda k: w1[:, k, a:a + P], lambda k: hselT[:, k, :], KD)
                        ins = acc(b[:, CAP:2 * CAP], lambda k: w3[:, k, a:a + P], lambda k: hselT[:, k, :], KD)
                        done(ins, name)

                def down(b_, n):
                    w2 = e_weight("w2", b_, j)
                    read(pe, ("eup", b_ * BM + BM - 1), j)
                    for cc in range(BM):
                        name = ("ey", n)
                        first, last = b_ == 0 and cc == 0, b_ == NBLK - 1 and cc == BM - 1
                        if first:
                            claim(pe, name, j)
                        ins = nc.tensor.matmul(banks[4 + n][0:CAP, :], gated_m[b_ % 2][:, cc, :],
                                               w2[:, cc, n * HALF:(n + 1) * HALF], start=first, stop=last)
                    return ins

                up(0)
                b = claim(pe, ("selT", 0), j)
                for t in range(T):
                    ins = nc.tensor.transpose(b[0:CAP, t * P:(t + 1) * P], sel[:, t, :], ident[:, :])
                done(ins, ("selT", 0))
                for b_ in range(1, NBLK - 1):
                    up(b_)
                    down(b_ - 1, 0)
                    down(b_ - 1, 1).then_inc(down_done, 1)
                up(NBLK - 1)
                pe.wait_ge(sel_ready, j + 2)
                for n in range(2):
                    gather(("gather", n), n, j)
                down(NBLK - 2, 0)
                done(down(NBLK - 1, 0), ("ey", 0))
                down(NBLK - 2, 1).then_inc(down_done, 1)
                ins = down(NBLK - 1, 1)
                done(ins, ("ey", 1))
                read(pe, ("selT", 0), j)
                for n in range(2):
                    read(pe, ("ey", n), j)
                    for t in range(T):
                        name = ("scatter", 2 * n + t)
                        b = claim(pe, name, j)
                        ins = nc.tensor.matmul(b[:, :], selT[0:CAP, t, :], y_sb[0:CAP, n * HALF:(n + 1) * HALF],
                                               start=True, stop=True)
                        done(ins, name)

            with pe.Fori(0, NE) as j:
                expert(j)
            pe.wait_ge(flag_ready, 1)
            overflow = pe.value_load(more[0:1, 0:1], min_val=0, max_val=1)
            with pe.If(overflow > 0):
                with pe.Fori(NE, JOBS) as j:
                    expert(j)

        @block.scalar
        def _(act):
            act.dma_start(vec_rows[c_of["mem"]:c_of["mem"] + KD, :],
                          g_mem.rearrange("(k p) -> k p", p=P)).then_inc(vecs_in, 16)
            act.dma_start(mem_sb, mem[0].rearrange("(t p) c -> p t c", p=P)).then_inc(mem_in, 16)
            act.dma_start(x_sb[:, :, :], x[0].rearrange("(t p) c -> p t c", p=P)).then_inc(x_in, 16)
            for name, v in (("mix", g_mix), ("ffn", g_ffn), ("q", g_q), ("kv", g_kv), ("sg", g_sg)):
                n = v.shape[0] * v.shape[1] // P
                act.dma_start(vec_rows[c_of[name]:c_of[name] + n, :],
                              v.rearrange("l (k p) -> (l k) p", p=P)).then_inc(vecs_in, 16)
            act.dma_start(vec_rows[c_of["gate"]:n_vec, :],
                          b_gate.rearrange("l n (k p) -> (l n k) p", p=P)).then_inc(vecs_in, 16)
            act.dma_start(ws_raw, w_s.rearrange("l g i j -> i l g j")).then_inc(ws_in, 16)
            act.dma_start(pos_i[:, :], positions[0].rearrange("(t p) -> p t", p=P),
                          allow_slow_non_contiguous=True).then_inc(pos_in, 16)
            act.dma_start(bs_row[:, :, :], b_s.rearrange("l g i -> l (g i)").partition_broadcast(P)).then_inc(row_in, 16)
            act.dma_start(wrt[:, :, :], w_router[0].rearrange("(k p) e -> p k e", p=P)).then_inc(router_in, 16)

            n_sq = 0

            def own_squares():
                if n_sq:
                    act.wait_ge(squares, n_sq)

            def square(src, width, col):
                nonlocal n_sq
                own_squares()
                nc.scalar.activation(junk[:, 0:width], src, ACT.Square,
                                     accum_out=sumsq[:, col:col + 1]).then_inc(squares, 1)
                n_sq += 1

            def norm_stats(src):
                for t in range(T):
                    square(src[:, t, :], D, 6 + t)

            def gains_T(i, dst, gain):
                for n in (0, 2):
                    b = full(act, ("nT", i, n))
                    for c in range(2):
                        k = 2 * n + c
                        ins = nc.scalar.activation(dst[:, k, :], b[:, c * SEQ:(c + 1) * SEQ], ACT.Copy,
                                                   scale=cols[:, gain + k:gain + k + 1])
                    free(ins, ("nT", i, n))

            act.wait_ge(mem_in, 16)
            norm_stats(mem_sb)
            act.wait_ge(x_in, 16)
            act.wait_ge(hn_ready, T)
            norm_stats(x_sb)
            for l in range(DEPTH):
                full(act, ("wsT", l))
                free(nc.scalar.activation(wsT[:, l, :, :].rearrange("p g i -> p (g i)"),
                                          banks[groups["wsT", l].bank][:, :], ACT.Copy), ("wsT", l))
            read(act, "vecs")
            gains_T(0, memT, c_of["mem"])
            act.wait_ge(angles, 1)
            nc.scalar.activation(sin_t[:, :, :], ang[:, 2, :, :], ACT.Sin).then_inc(trig, 1)
            nc.scalar.activation(cos_t[:, :, :], ang[:, 3, :, :], ACT.Sin).then_inc(trig, 1)

            n_unit = 0
            for l in range(DEPTH):
                for n in range(2):
                    b = full(act, ("mk", l, n))
                    free(nc.scalar.activation(mkT[:, 2 * n:2 * n + 2, :].rearrange("p h s -> p (h s)"), b[:, :],
                                              ACT.Copy), ("mk", l, n))
                gains_T(1 + 2 * l, hT, c_of["mix"] + l * KD)
                for t in range(T):
                    b = full(act, ("cq", l, t))
                    square(b[:, 0:QR], QR, t)
                    free(nc.scalar.activation(cqkv[:, t, 0:QR], b[:, 0:QR], ACT.Copy), ("cq", l, t))
                for t in range(T):
                    b = full(act, ("ckv", l, t))
                    square(b[:, 0:KVR], KVR, 2 + t)
                    free(nc.scalar.activation(cqkv[:, t, QR:], b[:, 0:KVR + ROPE], ACT.Copy), ("ckv", l, t))
                for t in range(T):
                    b = full(act, ("sv", l, t))
                    free(nc.scalar.activation(sv[:, t, :], b[:, :], ACT.Gelu_apprx_tanh), ("sv", l, t))
                for t in range(T):
                    read(act, ("sv", l, t))
                    square(sv[:, t, :], SG, 4 + t)
                for n in range(2):
                    b = full(act, ("su", l, n))
                    free(nc.scalar.activation(uT[:, 2 * n:2 * n + 2, :].rearrange("p h s -> p (h s)"), b[:, :],
                                              ACT.Gelu_apprx_tanh), ("su", l, n))
                act.wait_ge(lat_inv, l + 1)
                for t in range(T):
                    for n in range(2):
                        b = full(act, ("q", l, t, n))
                        free(nc.scalar.activation(q_sb[:, t, 4 * n:4 * n + 4, :].rearrange("p h d -> p (h d)"),
                                                  b[:, 0:4 * QK], ACT.Copy, scale=rin[:, t:t + 1]), ("q", l, t, n))
                for t in range(T):
                    b = full(act, ("k", l, t))
                    free(nc.scalar.activation(k_sb[:, t, :, 0:NOPE], b[:, :].rearrange("p (h d) -> p h d", h=H),
                                              ACT.Copy, scale=rin[:, 2 + t:3 + t]), ("k", l, t))

                def unit_tanh(n, d):
                    nonlocal n_unit
                    u = n_unit
                    n_unit += 1
                    if u >= 2:
                        read(act, unit_names[u - 2])
                    b = full(act, ("unit", l, n, d))
                    c = (l * NBR + n) * KD + d
                    nc.scalar.activation(sig[:, u % 2, :], b[:, 0:SEQ], ACT.Tanh, scale=0.5,
                                         bias=half_gate[:, c:c + 1]).then_inc(tanh_ready, 1)

                own_squares()
                for step in steps:
                    kind = step[0]
                    name = (kind, l) + step[1:]
                    if kind in ("ms", "as"):
                        h = step[1]
                        nth = l * (XH + H) + h + (XH if kind == "as" else 0)
                        act.wait_ge(max_ready, nth + 1)
                        b = banks[groups[name].bank]
                        for t in range(T):
                            total = rsum[:, nth % 2, t:t + 1] if kind == "ms" else asum[:, t, h:h + 1]
                            ins = nc.scalar.activation(prob[:, nth % 2, t, :], b[:, t * SEQ:(t + 1) * SEQ], ACT.Exp,
                                                       scale=XS if kind == "ms" else QS,
                                                       bias=nmax[:, nth % 2, t:t + 1], accum_out=total)
                        free(ins, name)
                    elif kind in ("mpT", "apT"):
                        h = step[1]
                        nth = l * (XH + H) + h + (XH if kind == "apT" else 0)
                        b = full(act, name)
                        free(nc.scalar.activation(probT[:, nth % 2, :, :].rearrange("p k s -> p (k s)"), b[:, :],
                                                  ACT.Copy), name)
                    elif kind == "kT":
                        t, n = step[1:]
                        b = full(act, name)
                        free(nc.scalar.activation(kT[0:QK, 4 * n:4 * n + 4, t * P:(t + 1) * P],
                                                  b[0:QK, :].rearrange("p (h s) -> p h s", h=4), ACT.Copy), name)
                    elif kind == "unit":
                        unit_tanh(*step[1:])
                for n in range(2):
                    b = full(act, ("oT", l, n))
                    free(nc.scalar.activation(yaT[:, 2 * n:2 * n + 2, :].rearrange("p h s -> p (h s)"), b[:, :],
                                              ACT.Copy), ("oT", l, n))
                for d in range(KD):
                    unit_tanh(0, d)
                for t in range(T):
                    for n in range(2):
                        read(act, ("out", l, t, n))
                norm_stats(x_sb)
                gains_T(2 + 2 * l, hT, c_of["ffn"] + l * KD)
                own_squares()
                if l % 2 == 0:
                    for c in range(FCD):
                        b = full(act, ("up", l, c))
                        nc.scalar.activation(silu_d[:, c % 4, :], b[:, 0:SEQ], ACT.Silu).then_inc(silu_ready, 1)
                    for n in range(4):
                        read(act, ("y", l, n))
                    norm_stats(x_sb)

            act.wait_ge(gap_ready, 1)
            nc.scalar.activation(gap[:, 1, :], gap[:, 0, :], ACT.Exp).then_inc(gap_exp, 1)
            gain = c_of["ffn"] + (DEPTH - 1) * KD

            def rows_T(name, j):
                b = full(act, name, j)
                for c in range(4):
                    ins = nc.scalar.activation(hselT[:, c, :], b[:, c * CAP:(c + 1) * CAP], ACT.Copy,
                                               scale=cols[:, gain + c:gain + c + 1])
                free(ins, name)

            rows_T(("gather0", DEPTH - 1, 0), 0)

            def expert(j):
                for c in range(FCM):
                    b = full(act, ("eup", c), j)
                    nc.scalar.activation(silu_m[:, c % 4, :], b[:, 0:CAP], ACT.Silu).then_inc(e_silu, 1)
                    if c == 3:
                        b = full(act, ("selT", 0), j)
                        free(nc.scalar.activation(selT[0:CAP, :, :].rearrange("p t s -> p (t s)"),
                                                  b[0:CAP, 0:T * P], ACT.Copy), ("selT", 0))
                rows_T(("gather", 0), j)
                b = full(act, ("ey", 0), j)
                free(nc.scalar.activation(y_sb[0:CAP, 0:HALF], b[0:CAP, :], ACT.Copy), ("ey", 0))

            with act.Fori(0, NE) as j:
                expert(j)
            act.wait_ge(flag_ready, 1)
            overflow = act.value_load(more[0:1, 0:1], min_val=0, max_val=1)
            with act.If(overflow > 0):
                with act.Fori(NE, JOBS) as j:
                    expert(j)
            for n in range(4):
                read(act, ("scatter", n), overflow * (JOBS - NE) + (NE - 1))
            norm_stats(x_sb)

        @block.vector
        def _(dve):
            n_step = 0

            def link(ins):
                nonlocal n_step
                n_step += 1
                ins.then_inc(dve_step, 1)
                dve.wait_ge(dve_step, n_step)

            V = nc.vector

            def inv_sqrt(a, z, widths):
                v, w, y = nr[:, 0, a:z], nr[:, 1, a:z], rin[:, a:z]
                for i, width in enumerate(widths):
                    link(V.tensor_scalar(nr[:, 0, a + 2 * i:a + 2 * i + 2], sumsq[:, a + 2 * i:a + 2 * i + 2],
                                         1.0 / width, EPS, ALU.mult, ALU.add))
                link(V.tensor_scalar(y.bitcast(I32), v.bitcast(I32), -0.5, 1597463007.0, ALU.mult, ALU.add))
                for i in range(4):
                    link(V.scalar_tensor_tensor(out=w, in0=y, scalar=-0.5, in1=y, op0=ALU.mult, op1=ALU.mult))
                    link(V.tensor_tensor(w, w, v, ALU.mult))
                    link(V.scalar_tensor_tensor(out=y, in0=w, scalar=1.5, in1=y, op0=ALU.add, op1=ALU.mult))

            def normalise(i, src):
                dve.wait_ge(squares, N_SQ[i])
                inv_sqrt(6, 8, [D])
                for t in range(T):
                    V.tensor_scalar(hn[:, t, :], src[:, t, :], rin[:, 6 + t:7 + t], None,
                                    ALU.mult).then_inc(hn_ready, 1)

            def gains_T(i, dst, gain):
                for n in (1, 3):
                    b = full(dve, ("nT", i, n))
                    for c in range(2):
                        k = 2 * n + c
                        ins = V.tensor_scalar(dst[:, k, :], b[:, c * SEQ:(c + 1) * SEQ],
                                              cols[:, gain + k:gain + k + 1], None, ALU.mult)
                    free(ins, ("nT", i, n))

            b = full(dve, "vecs")
            V.tensor_copy(cols[:, :], b[:, 0:n_vec])
            free(V.tensor_scalar(half_gate[:, :], b[:, c_of["gate"]:n_vec], 0.5, None, ALU.mult), "vecs")
            read(dve, "vecs")
            normalise(0, mem_sb)
            gains_T(0, memT, c_of["mem"])
            dve.wait_ge(pos_in, 16)
            dve.wait_ge(pool_step, 3 + ROPE // 2)
            link(V.tensor_copy(pos_f[:, :], pos_i[:, :]))
            for t in range(T):
                link(V.tensor_scalar(ang[:, 0, t, :], inv_freq[:, :], pos_f[:, t:t + 1], None, ALU.mult))
            MAGIC = 12582912.0
            C1 = 6.28125
            C2 = 0.00193500518798828125
            C3 = TWO_PI - C1 - C2
            for out_, shift in ((2, 0.0), (3, 0.25)):
                k = ang[:, 1, :, :]
                r = ang[:, out_, :, :]
                link(V.tensor_scalar(k, ang[:, 0, :, :], 1.0 / TWO_PI, shift, ALU.mult, ALU.add))
                link(V.tensor_scalar(k, k, MAGIC, None, ALU.add))
                link(V.tensor_scalar(k, k, -MAGIC, None, ALU.add))
                link(V.scalar_tensor_tensor(out=r, in0=k, scalar=-C1, in1=ang[:, 0, :, :], op0=ALU.mult, op1=ALU.add))
                for c in (C2, C3):
                    link(V.scalar_tensor_tensor(out=r, in0=k, scalar=-c, in1=r, op0=ALU.mult, op1=ALU.add))
                link(V.tensor_scalar(r, r, shift * TWO_PI, None, ALU.add))
                ins = V.tensor_scalar(r, r, 3.14159250, -3.14159250, ALU.min, ALU.max)
                if out_ == 2:
                    link(ins)
            ins.then_inc(angles, 1)

            units = 0
            for l in range(DEPTH):
                if l:
                    for n in range(4):
                        read(dve, ("y", l - 1, n))
                elif l == 0:
                    dve.wait_ge(x_in, 16)
                normalise(1 + 2 * l, x_sb)
                for t in range(T):
                    b = full(dve, ("mv", l, t))
                    free(V.tensor_copy(mv[:, t, :], b[:, :]), ("mv", l, t))
                gains_T(1 + 2 * l, hT, c_of["mix"] + l * KD)
                for t in range(T):
                    read(dve, ("ckv", l, t))
                    read(dve, ("cq", l, t))
                inv_sqrt(0, 4, [QR, KVR])
                link_inv = V.tensor_copy(nr[:, 2, 0:4], rin[:, 0:4])
                link_inv.then_inc(lat_inv, 1)
                dve.wait_ge(squares, N_SQ[1 + 2 * l] + 3 * T)
                inv_sqrt(4, 6, [SG])
                for t in range(T):
                    V.tensor_scalar(sv[:, t, :], sv[:, t, :], rin[:, 4 + t:5 + t], None,
                                    ALU.mult).then_inc(vn_ready, 1)
                for n in range(2):
                    b = full(dve, ("qx", l, n))
                    free(V.tensor_copy(qxT[:, 2 * n:2 * n + 2, :].rearrange("p h s -> p (h s)"), b[:, :]), ("qx", l, n))
                for n in range(3):
                    b = full(dve, ("cT", l, n))
                    for c in range(2 if n < 2 else 1):
                        k = 2 * n + c
                        g = c_of["q"] + l * 3 + k if k < 3 else c_of["kv"] + l * 2 + k - 3
                        ins = V.tensor_scalar(cT[:, k, :], b[:, c * SEQ:(c + 1) * SEQ], cols[:, g:g + 1], None, ALU.mult)
                    free(ins, ("cT", l, n))
                for t in range(T):
                    b = full(dve, ("v", l, t))
                    free(V.tensor_scalar(v_sb[:, t, :], b[:, :], rin[:, 2 + t:3 + t], None, ALU.mult), ("v", l, t))
                if l == 0:
                    dve.wait_ge(row_in, 16)
                for n in range(2):
                    read(dve, ("su", l, n))
                for t in range(T):
                    b = full(dve, ("sg", l, t))
                    mixed = hn[:, 1, t * HALF:(t + 1) * HALF]
                    for g in range(G):
                        c = c_of["sg"] + l * G + g
                        ins = V.scalar_tensor_tensor(out=mixed[:, g * P:(g + 1) * P], in0=b[:, g * P:(g + 1) * P],
                                                     scalar=cols[:, c:c + 1], in1=bs_row[:, l, g * P:(g + 1) * P],
                                                     op0=ALU.mult, op1=ALU.add)
                    free(ins, ("sg", l, t))
                    read(dve, ("sg", l, t))
                    u = uT[:, :, t * P:(t + 1) * P]
                    V.tensor_tensor(u, u, mixed.rearrange("p (g i) -> p g i", g=G), ALU.mult).then_inc(yb_ready, 1)

                def rotate(dst, src, heads, ready):
                    h2 = ROPE // 2
                    tmp = hn[:, 0, :].rearrange("p (n t h r) -> p n t h r", n=4, t=T, h=H)[:, :, :, 0:heads, :]
                    for t in range(T):
                        shape = [P, heads, h2]
                        co = cos_t[:, t, :].unsqueeze(1).broadcast_to(shape)
                        si = sin_t[:, t, :].unsqueeze(1).broadcast_to(shape)
                        a, b_ = src(t)[:, :, 0:h2], src(t)[:, :, h2:ROPE]
                        V.tensor_tensor(tmp[:, 0, t], a, co, ALU.mult)
                        V.tensor_tensor(tmp[:, 1, t], b_, si, ALU.mult)
                        V.tensor_tensor(tmp[:, 2, t], a, si, ALU.mult)
                        link(V.tensor_tensor(tmp[:, 3, t], b_, co, ALU.mult))
                        V.tensor_tensor(dst(t)[:, :, 0:h2], tmp[:, 0, t], tmp[:, 1, t], ALU.subtract)
                        ins = V.tensor_tensor(dst(t)[:, :, h2:ROPE], tmp[:, 2, t], tmp[:, 3, t], ALU.add)
                        if t < T - 1:
                            link(ins)
                    if ready is None:
                        link(ins)
                    else:
                        ins.then_inc(ready, 1)

                def unit_merge(n, d):
                    nonlocal units
                    name = ("unit", l, n, d)
                    units += 1
                    dve.wait_ge(tanh_ready, units)
                    b = banks[groups[name].bank]
                    s_ = sig[:, (units - 1) % 2, :]
                    first = n == 1
                    dst = mixT[:, d, :] if first else gated_tmp[:, units % 2, :]
                    free(V.scalar_tensor_tensor(out=dst, in0=s_, scalar=1.0, in1=b[:, SEQ:2 * SEQ], op0=ALU.add,
                                                op1=ALU.mult), name)
                    if not first:
                        read(dve, name)
                        ins = V.tensor_tensor(mixT[:, d, :], mixT[:, d, :], dst, ALU.add)
                        if n == 0:
                            ins.then_inc(merged, 1)
                        else:
                            link(ins)

                for step in steps:
                    kind = step[0]
                    name = (kind, l) + step[1:]
                    if kind in ("ms", "as"):
                        h = step[1]
                        nth = l * (XH + H) + h + (XH if kind == "as" else 0)
                        b = full(dve, name)
                        link(V.tensor_reduce(rmax[:, nth % 2, :], b[:, :].rearrange("p (t s) -> p t s", t=T), AX_X,
                                             ALU.max))
                        V.tensor_scalar(nmax[:, nth % 2, :], rmax[:, nth % 2, :], -(XS if kind == "ms" else QS), None,
                                        ALU.mult).then_inc(max_ready, 1)
                        if kind == "ms":
                            read(dve, name)
                            link(V.reciprocal(rrec[:, nth % 2, :], rsum[:, nth % 2, :]))
                            for t in range(T):
                                ins = V.tensor_scalar(prob[:, nth % 2, t, :], prob[:, nth % 2, t, :],
                                                      rrec[:, nth % 2, t:t + 1], None, ALU.mult)
                            ins.then_inc(prob_ready, 1)
                    elif kind == "mo":
                        h = step[1]
                        b = full(dve, name)
                        free(V.tensor_copy(qxT[:, h, :], b[:, 0:SEQ]), name)
                        if h == 0:
                            if l == 0:
                                dve.wait_ge(trig, 2)
                            for t in range(T):
                                for n in range(2):
                                    read(dve, ("q", l, t, n))
                                read(dve, ("k", l, t))
                            rotate(lambda t: q_sb[:, t, :, NOPE:QK], lambda t: q_sb[:, t, :, NOPE:QK], H, q_ready)
                            kr = hn[:, 1, 0:T * ROPE].rearrange("p (t o d) -> p t o d", t=T, o=1)
                            rotate(lambda t: kr[:, t], lambda t: cqkv[:, t, QR + KVR:].unsqueeze(1), 1, None)
                            for t in range(T):
                                ins = V.tensor_copy(k_sb[:, t, :, NOPE:QK], kr[:, t].broadcast_to([P, H, ROPE]))
                            ins.then_inc(k_ready, 1)
                    elif kind == "qT":
                        t, n = step[1:]
                        b = full(dve, name)
                        free(V.tensor_copy(qT[0:QK, 4 * n:4 * n + 4, t * P:(t + 1) * P],
                                           b[0:QK, :].rearrange("p (h s) -> p h s", h=4)), name)
                    elif kind == "unit":
                        unit_merge(*step[1:])
                read(dve, ("as", l, H - 1))
                link(V.reciprocal(arec[:, :, :], asum[:, :, :]))
                for t in range(T):
                    b = full(dve, ("o", l, t))
                    w = BW // H
                    free(V.tensor_tensor(o_sb[:, t, :].rearrange("p (h d) -> p h d", h=H),
                                         b[:, :].rearrange("p (h d) -> p h d", h=H),
                                         arec[:, t, :].unsqueeze(2).broadcast_to([P, H, w]), ALU.mult), ("o", l, t))
                for d in range(KD):
                    unit_merge(0, d)
                for t in range(T):
                    for n in range(2):
                        b = full(dve, ("out", l, t, n))
                        xs = x_sb[:, t, n * HALF:(n + 1) * HALF]
                        free(V.scalar_tensor_tensor(out=xs, in0=b[:, :], scalar=0.5, in1=xs, op0=ALU.mult,
                                                    op1=ALU.add), ("out", l, t, n))
                normalise(2 + 2 * l, x_sb)
                gains_T(2 + 2 * l, hT, c_of["ffn"] + l * KD)
                if l % 2 == 0:
                    for c in range(FCD):
                        dve.wait_ge(silu_ready, c + 1)
                        b = banks[groups["up", l, c].bank]
                        free(V.tensor_tensor(gated_d[c // BD % 2][:, c % BD, :], silu_d[:, c % 4, :],
                                             b[:, SEQ:2 * SEQ], ALU.mult), ("up", l, c))
                    for t in range(T):
                        for n in range(2):
                            b = full(dve, ("y", l, 2 * t + n))
                            xs = x_sb[:, t, n * HALF:(n + 1) * HALF]
                            free(V.tensor_tensor(xs, xs, b[:, :], ALU.add), ("y", l, 2 * t + n))

            l = DEPTH - 1
            b = full(dve, ("logits", l))
            free(V.tensor_copy(logits[:, :, :].rearrange("p t e -> p (t e)"), b[:, 0:T * NE]), ("logits", l))
            read(dve, ("logits", l))
            for t in range(T):
                link(V.max(top_v[:, t, :], logits[:, t, :]))
                link(V.max_index(top_i[:, t, :], top_v[:, t, :], logits[:, t, :]))
            link(V.tensor_copy(top_f[:, :, :], top_i[:, :, :]))
            V.tensor_tensor(gap[:, 0, :], top_v[:, :, 1], top_v[:, :, 0], ALU.subtract).then_inc(gap_ready, 1)
            dve.wait_ge(consts, N_CONST)
            for n in range(2):
                for t in range(T):
                    ins = V.tensor_scalar(hot[:, n, t, :], iota_e[:, :], top_f[:, t, n:n + 1], None, ALU.is_equal)
            link(ins)
            V.tensor_tensor(mask[:, :, :], hot[:, 0, :, :], hot[:, 1, :, :], ALU.add).then_inc(mask_ready, 1)
            dve.wait_ge(mask_ready, 1)
            dve.wait_ge(gap_exp, 1)
            link(V.tensor_scalar(gap[:, 2, :], gap[:, 1, :], 1.0, None, ALU.add))
            link(V.reciprocal(gap[:, 3, :], gap[:, 2, :]))
            link(V.tensor_tensor(gap[:, 2, :], gap[:, 1, :], gap[:, 3, :], ALU.mult))
            for t in range(T):
                link(V.tensor_scalar(comb[:, t, 0:NE], hot[:, 0, t, :], gap[:, 3, t:t + 1], None, ALU.mult))
                link(V.scalar_tensor_tensor(out=comb[:, t, 0:NE], in0=hot[:, 1, t, :], scalar=gap[:, 2, t:t + 1],
                                            in1=comb[:, t, 0:NE], op0=ALU.mult, op1=ALU.add))
            for p in range(1, JOBS // NE):
                ins = V.tensor_copy(comb[:, :, p * NE:(p + 1) * NE], comb[:, :, 0:NE])
            link(ins)
            b = full(dve, ("rank", l))
            rk = logits[:, :, :]
            link(V.scalar_tensor_tensor(out=rk, in0=b[:, 0:T * NE].rearrange("p (t e) -> p t e", t=T), scalar=1.0,
                                        in1=mask[:, :, :], op0=ALU.add, op1=ALU.mult))
            free(V.tensor_reduce(most[:, 0:1], b[:, 2 * NE:3 * NE], AX_X, ALU.max), ("rank", l))
            for p in range(JOBS // NE):
                ins = V.tensor_scalar(rank[:, :, p * NE:(p + 1) * NE], rk, -1.0 - p * CAP, None, ALU.add)
            link(ins)
            read(dve, ("rank", l))
            V.tensor_scalar(more[:, :], most[:, 0:1], float(CAP), None, ALU.is_gt).then_inc(flag_ready, 1)

            def select(j):
                for t in range(T):
                    ins = V.tensor_scalar(sel[:, t, :], iota_cap[:, :], cur[:, 0, t:t + 1], None, ALU.is_equal)
                ins.then_inc(sel_ready, 1)

            gain = c_of["ffn"] + (DEPTH - 1) * KD

            def rows_T(name, j):
                b = full(dve, name, j)
                for c in range(4):
                    k = 4 + c
                    ins = V.tensor_scalar(hselT[:, k, :], b[:, c * CAP:(c + 1) * CAP], cols[:, gain + k:gain + k + 1],
                                          None, ALU.mult)
                free(ins, name)

            V.tensor_copy(cur[:, 0, :], rank[:, :, 0]).then_inc(cur_ready, 1)
            dve.wait_ge(cur_ready, 1)
            select(0)
            rows_T(("gather0", l, 1), 0)

            def expert(j):
                for c in range(FCM):
                    dve.wait_ge(e_silu, FCM * j + (c + 1))
                    b = banks[groups["eup", c].bank]
                    free(V.tensor_tensor(gated_m[c // BM % 2][:, c % BM, :], silu_m[:, c % 4, :],
                                         b[:, CAP:2 * CAP], ALU.mult), ("eup", c))
                    if c == 7:
                        full(dve, ("selT", 0), j)
                        V.tensor_copy(cur[:, 0, :], rank[:, :, bass.ds(j + 1, 1)].rearrange("p t o -> p (t o)")).then_inc(cur_ready, 1)
                        V.tensor_copy(cur[:, 1, :], comb[:, :, bass.ds(j, 1)].rearrange("p t o -> p (t o)")).then_inc(cur_ready, 1)
                        dve.wait_ge(cur_ready, 2 * j + 3)
                        select(j + 1)
                rows_T(("gather", 1), j)
                b = full(dve, ("ey", 1), j)
                free(V.tensor_copy(y_sb[0:CAP, HALF:D], b[0:CAP, :]), ("ey", 1))
                for n in range(2):
                    for t in range(T):
                        name = ("scatter", 2 * n + t)
                        read(dve, name, j - 1)
                        b = full(dve, name, j)
                        xs = x_sb[:, t, n * HALF:(n + 1) * HALF]
                        free(V.scalar_tensor_tensor(out=xs, in0=b[:, :], scalar=cur[:, 1, t:t + 1], in1=xs,
                                                    op0=ALU.mult, op1=ALU.add), name)

            with dve.Fori(0, NE) as j:
                expert(j)
            dve.wait_ge(flag_ready, 1)
            overflow = dve.value_load(more[0:1, 0:1], min_val=0, max_val=1)
            with dve.If(overflow > 0):
                with dve.Fori(NE, JOBS) as j:
                    expert(j)
            dve.wait_ge(squares, N_SQ[-1])
            dve.wait_ge(gf_in, 16)
            inv_sqrt(6, 8, [D])
            for t in range(T):
                V.scalar_tensor_tensor(out=hn[:, t, :], in0=x_sb[:, t, :], scalar=rin[:, 6 + t:7 + t], in1=gf_row,
                                       op0=ALU.mult, op1=ALU.mult).then_inc(y_final, 1)


_INS = ['x', 'mem', 'positions', 'g_mix', 'w_in', 'g_q', 'g_kv', 'w_uq', 'w_uk', 'w_uv', 'g_sg', 'w_s',
        'b_s', 'g_mem', 'w_mkv', 'w_br', 'b_gate', 'w_out', 'g_ffn', 'dense_w1', 'dense_w3', 'dense_w2',
        'w_router', 'moe_w1', 'moe_w3', 'moe_w2', 'g_final']


def kernel(**inputs):
    from concourse import bacc
    from concourse.bass_utils import run_bass_kernel_spmd

    nc = bacc.Bacc("TRN2", target_bir_lowering=False, num_devices=1)
    arrays, args = {}, []
    for name in _INS:
        a = np.ascontiguousarray(inputs[name])
        arrays[f"in_{name}"] = a
        args.append(nc.dram_tensor(f"in_{name}", a.shape, mybir.dt.from_np(a.dtype), kind="ExternalInput").ap())
    args.append(nc.dram_tensor("out", inputs["x"].shape, F32, kind="ExternalOutput").ap())
    build(nc, *args)
    return run_bass_kernel_spmd(nc, [arrays], core_ids=[0]).results[0]["out"]
```

```python
from contextlib import ExitStack

import numpy as np

import concourse.bass as bass
from concourse import mybir

F32 = mybir.dt.float32
F32R = mybir.dt.float32r
I32 = mybir.dt.int32
U32 = mybir.dt.uint32
ALU = mybir.AluOpType
ACT = mybir.ActivationFunctionType
AX_X = mybir.AxisListType.X

P = 128
CAP = 128
RAW = 6
MIX_RAW = 2
SPLIT = 3
SLOT = 2048
HALF = 512
EPS = 1e-6
TWO_PI = 6.283185307179586


class Group:

    def __init__(self, bank, use, per=0):
        self.bank, self.use, self.per = bank, use, per


def plan_psum(depth, heads, x_heads, fcd, nblk):
    groups, used, turn = {}, [0] * 8, [0]

    def take(name, bank=None, among=(0, 1, 2, 3, 6, 7)):
        if bank is None:
            bank = among[turn[0] % len(among)]
            turn[0] += 1
        used[bank] += 1
        groups[name] = Group(bank, used[bank])

    take("vecs")
    for l in range(depth):
        for n in range(4):
            take(("nT", 3 * l, n))
        for n in range(2):
            take(("mk", l, n))
        for t in range(2):
            take(("mv", l, t))
        for n in range(4):
            take(("nT", 3 * l + 1, n))
        for name in ("cq", "ckv", "sv", "su", "qx"):
            for t in range(2):
                take((name, l, t))
        take(("wsT", l))
        for n in range(3):
            take(("cT", l, n))
        for n in range(2):
            for t in range(2):
                take(("q", l, t, n))
        for name in ("k", "v", "sg"):
            for t in range(2):
                take((name, l, t))
        for step in mixer_steps(heads, x_heads):
            if step[0] != "O":
                take((step[0], l) + step[1:])
        for t in range(2):
            take(("o", l, t), bank=4 + t)
        for n in range(2):
            take(("oT", l, n))
        for d in range(8):
            take(("unit", l, 0, d))
        for n in range(2):
            for t in range(2):
                take(("out", l, t, n))
        for n in range(4):
            take(("nT", 3 * l + 2, n))
        turn[0] = 0
        if l % 2 == 0:
            for c in range(fcd):
                take(("up", l, c), among=(0, 1, 2, 3))
            for n in range(4):
                take(("y", l, n), bank=4 + n)
            turn[0] = 0
        else:
            take(("logits", l), bank=6)
            take(("rank", l), bank=7)
            take(("gather0", l, 0), bank=7)
            take(("gather0", l, 1), bank=6)
            start = list(used)
            inside = []
            for b in range(nblk):
                inside.append(("e1", b, 2 * (b % 2)))
                if b:
                    inside.append(("eT", b - 1, 2 * ((b - 1) % 2)))
                inside.append(("e3", b, 2 * (b % 2) + 1))
                if b == 0:
                    inside.append(("selT", 0, 3))
            inside += [("gather", 0, 7), ("gather", 1, 6), ("eT", nblk - 1, 0), ("ey", 0, 4), ("ey", 1, 5)]
            inside += [("scatter", n, n) for n in range(4)]
            for name, n, bank in inside:
                used[bank] += 1
                groups[name, n] = Group(bank, used[bank])
            for name, n, bank in inside:
                groups[name, n].per = used[bank] - start[bank]
    return groups


def mixer_steps(heads, x_heads):
    steps = []
    fill = [(n, d) for n in (1, 2) for d in range(8)]
    for i in range(x_heads + 2):
        if i < x_heads:
            steps.append(("ms", i))
        if 1 <= i <= x_heads:
            steps.append(("mpT", i - 1))
        if i >= 2:
            steps.append(("mo", i - 2))
        steps.append(("unit", *fill.pop(0)))
    for i in range(4):
        steps += [("qT", i // 2, i % 2), ("kT", i // 2, i % 2)]
    for i in range(heads + 2):
        if i < heads:
            steps.append(("as", i))
        if 1 <= i <= heads:
            steps.append(("apT", i - 1))
        if i >= 2:
            steps.append(("O", i - 2))
        steps.append(("unit", *fill.pop(0)))
    assert not fill
    return steps


def build(nc, x, mem, positions, g_mix, w_in, g_q, g_kv, w_uq, w_uk, w_uv, g_sg, w_s, b_s, g_mem,
          w_mkv, w_br, b_gate, w_out, g_ffn, dense_w1, dense_w3, dense_w2, w_router, moe_w1, moe_w3,
          moe_w2, g_final, out):
    DEPTH, D, PT = w_in.shape
    SEQ = x.shape[1]
    QR, KVR = g_q.shape[1], g_kv.shape[1]
    SG = g_sg.shape[1]
    G = w_s.shape[1]
    NBR, BW = w_br.shape[1], w_br.shape[2]
    NOPE, ROPE, H, XH = 64, 32, 8, 4
    QK = NOPE + ROPE
    FD, FE, NE = dense_w1.shape[2], moe_w1.shape[3], moe_w1.shape[1]
    T, KD = SEQ // P, D // P
    KB = BW // P
    FCD, FCM = FD // P, FE // P
    BD, BM = 2, 4
    ND, NM = -(-FCD // BD), FCM // BM
    W = SLOT // KD
    assert T == 2 and KD == 8 and W == 256 and NM * BM == FCM and NM % 2 == 1
    C_KV, C_SG = QR, QR + KVR + ROPE
    C_XQ = C_SG + 2 * SG
    C_GATE = C_XQ + BW
    JOBS = NE * (-(-SEQ // CAP))
    QS, XS = QK ** -0.5, (BW // XH) ** -0.5
    steps = mixer_steps(H, XH)
    groups = plan_psum(DEPTH, H, XH, FCD, NM)

    with ExitStack() as ctx:
        def sb(name, shape, dt=F32):
            return ctx.enter_context(nc.sbuf_tensor(name, shape, dt))

        def sem(name):
            return ctx.enter_context(nc.semaphore(name))

        banks = [ctx.enter_context(nc.psum_tensor(f"bank{i}", [P, HALF], F32)) for i in range(8)]
        products = sem("products")
        bank_free = [sem(f"bank_free{i}") for i in range(8)]

        raw = sb("raw", [P, RAW, SLOT])
        whi = sb("whi", [P, SPLIT, SLOT], F32R)
        wlo = sb("wlo", [P, SPLIT, SLOT], F32R)
        x_sb = sb("x_sb", [P, T, D])
        hn = sb("hn", [P, T, D])
        hT = [sb(f"hT_{i}", [P, KD, SEQ], F32R) for i in ("hi", "lo")]
        mT = [sb(f"mT_{i}", [P, KD, SEQ], F32R) for i in ("hi", "lo")]
        yT = [sb(f"yT_{i}", [P, 2, KB, SEQ], F32R) for i in ("hi", "lo")]
        cqkv = sb("cqkv", [P, T, QR + KVR + ROPE])
        cT = sb("cT", [P, 5, SEQ])
        sgv = sb("sgv", [P, T * SG])
        qxT = sb("qxT", [P, XH, SEQ])
        mkT = sb("mkT", [P, XH, SEQ])
        mv = sb("mv", [P, T, BW])
        pbuf = sb("pbuf", [P, T * D])
        ident = sb("ident", [P, P])
        lower = sb("lower", [P, P])
        ones = sb("ones", [P, P])
        iota_cap = sb("iota_cap", [P, CAP])
        iota_e = sb("iota_e", [P, NE])
        n_vec = 2 * DEPTH * KD + KD + DEPTH * (3 + 2 + G) + DEPTH * NBR * KD
        cols = sb("cols", [P, n_vec])
        half_gate = sb("half_gate", [P, DEPTH * NBR * KD])
        inv_freq = sb("inv_freq", [P, ROPE // 2])
        pos_i = sb("pos_i", [P, T], I32)
        pos_f = sb("pos_f", [P, T])
        cos_t = sb("cos_t", [P, T, ROPE // 2])
        sin_t = sb("sin_t", [P, T, ROPE // 2])
        sumsq = sb("sumsq", [P, 8])
        rin = sb("rin", [P, 8])
        nr = sb("nr", [P, 3, 8])
        rmax = sb("rmax", [P, 2, T])
        nmax = sb("nmax", [P, 2, T])
        rsum = sb("rsum", [P, 2, T])
        rrec = sb("rrec", [P, 2, T])
        asum = sb("asum", [P, T, H])
        arec = sb("arec", [P, T, H])
        wrt = sb("wrt", [P, KD, NE])
        logits = sb("logits", [P, T, NE])
        top_v = sb("top_v", [P, T, 8])
        top_i = sb("top_i", [P, T, 8], U32)
        top_f = sb("top_f", [P, T, 8])
        gap = sb("gap", [P, 4, T])
        hot = sb("hot", [P, 2, T, NE])
        mask = sb("mask", [P, T, NE])
        comb = sb("comb", [P, T, JOBS + 8])
        rank = sb("rank", [P, T, JOBS + 8])
        cur = sb("cur", [P, 2, T])
        most = sb("most", [P, 2])
        more = sb("more", [P, 1], I32)

        scratch = raw[:, MIX_RAW:, :].rearrange("p n c -> p (n c)")
        q_sb = scratch[:, 0:T * H * QK].rearrange("p (t h d) -> p t h d", t=T, h=H)
        k_sb = scratch[:, 1536:1536 + T * H * QK].rearrange("p (t h d) -> p t h d", t=T, h=H)
        v_sb = scratch[:, 3072:3072 + T * BW].rearrange("p (t c) -> p t c", t=T)
        qT = scratch[:, 4096:4096 + H * SEQ].rearrange("p (h s) -> p h s", h=H)
        kT = scratch[:, 6144:6144 + H * SEQ].rearrange("p (h s) -> p h s", h=H)
        prob = pbuf[:, 0:2 * T * SEQ].rearrange("p (n t s) -> p n t s", n=2, t=T)
        probT = pbuf[:, 2 * T * SEQ:].rearrange("p (n t s) -> p n t s", n=2, t=T)
        junk, pT_flat = pbuf[:, 0:2 * HALF], pbuf[:, 2 * HALF:]
        uT = junk.rearrange("p (g s) -> p g s", g=G)
        mixed = pT_flat.rearrange("p (t c) -> p t c", t=T)
        mem_sb = pbuf[:, :].rearrange("p (t c) -> p t c", t=T)
        mixT = hn[:, :, :].rearrange("p t c -> p (t c)").rearrange("p (k s) -> p k s", k=KD)
        o_sb = cqkv[:, :, :].rearrange("p t c -> p (t c)")[:, 0:T * BW].rearrange(
            "p (t c) -> p t c", t=T)
        sv = sgv[:, :].rearrange("p (t c) -> p t c", t=T)
        bs_row = hn[:, 0, 0:G * P]
        ws_raw = hn[:, 1, 0:G * P].rearrange("p (g j) -> p g j", g=G)
        wsT = hn[:, 1, G * P:].rearrange("p (g j) -> p g j", g=G)
        sig = cT[:, 0:2, :]
        ang = qxT[:, 0, 0:4 * T * ROPE // 2].rearrange("p (n t r) -> p n t r", n=4, t=T)
        kr = cT[:, 2, 0:T * ROPE].rearrange("p (t o d) -> p t o d", t=T, o=1)
        gated_tmp = sgv[:, 0:2 * SEQ].rearrange("p (n s) -> p n s", n=2)
        vec_rows = sgv[0:n_vec, 0:P]
        silu_d = junk.rearrange("p (n s) -> p n s", n=4)
        g32_d = pT_flat[:, 0:2 * SEQ].rearrange("p (n s) -> p n s", n=2)
        gated_d = [v[:, :, 0:BD, :] for v in yT]
        silu_m = junk.rearrange("p (n s) -> p n s", n=2)
        g32_m = pT_flat.rearrange("p (n s) -> p n s", n=2)
        gated_m = [v[:, :, 0:2, :].rearrange("p n a s -> p n (a s)") for v in yT]
        hselT = [v[:, :, 2:4, :].rearrange("p n a s -> p n (a s)") for v in yT]
        y_sb = qxT[:, :, :].rearrange("p k s -> p (k s)")
        sel = sgv[:, 0:T * CAP].rearrange("p (t s) -> p t s", t=T)
        selT = sgv[:, T * CAP:2 * T * CAP].rearrange("p (t s) -> p t s", t=T)
        gf_row = mkT[:, :, :].rearrange("p k s -> p (k s)")

        at, c_of = 0, {}
        for name, n in (("mix", DEPTH * KD), ("ffn", DEPTH * KD), ("mem", KD), ("q", DEPTH * 3),
                        ("kv", DEPTH * 2), ("sg", DEPTH * G), ("gate", DEPTH * NBR * KD)):
            c_of[name] = at
            at += n

        vecs_in = sem("vecs_in")
        x_in = sem("x_in")
        mem_in = sem("mem_in")
        ws_in = sem("ws_in")
        row_in = sem("row_in")
        pos_in = sem("pos_in")
        router_in = sem("router_in")
        gf_in = sem("gf_in")
        stored = sem("stored")
        raw_in = [sem(f"raw_in{i}") for i in range(RAW)]
        hi_ready = sem("hi_ready")
        lo_ready = sem("lo_ready")
        pool_step = sem("pool_step")
        consts = sem("consts")
        dve_step = sem("dve_step")
        angles = sem("angles")
        trig = sem("trig")
        squares = sem("squares")
        hn_ready = sem("hn_ready")
        hT_hi = sem("hT_hi")
        g_hi = sem("g_hi")
        rows_hi = sem("rows_hi")
        lat_inv = sem("lat_inv")
        vn_ready = sem("vn_ready")
        yb_ready = sem("yb_ready")
        q_ready = sem("q_ready")
        k_ready = sem("k_ready")
        max_ready = sem("max_ready")
        prob_ready = sem("prob_ready")
        tanh_ready = sem("tanh_ready")
        merged = sem("merged")
        silu_ready = sem("silu_ready")
        gap_ready = sem("gap_ready")
        gap_exp = sem("gap_exp")
        mask_ready = sem("mask_ready")
        flag_ready = sem("flag_ready")
        y_hi = sem("y_hi")
        cur_ready = sem("cur_ready")
        sel_ready = sem("sel_ready")
        y_final = sem("y_final")

        def rows(w, c0, c1, r0=0, r1=None):
            r1 = w.shape[0] if r1 is None else r1
            return w[r0:r1, c0:c1].rearrange("(k p) c -> p k c", p=P)

        pieces, nth_piece = [], {}

        def piece(key, slots, *parts, split=True):
            n_split = sum(1 for p in pieces if p[3] is not None)
            nth_piece[key] = len(pieces)
            pieces.append((key, (len(pieces) - first) % slots, parts, n_split if split else None))

        for l in range(DEPTH):
            first = len(pieces)
            wi, hk = w_in[l], D // 2

            def mixer_piece(key, *parts, split=True):
                piece(key, MIX_RAW, *parts, split=split)

            for n in range(2):
                mixer_piece(("mk", l, n), rows(w_mkv[l], n * W, (n + 1) * W))
            for k in range(2):
                mixer_piece(("mv", l, k), rows(w_mkv[l], BW, 2 * BW, k * hk, (k + 1) * hk))
            for name, c0, c1 in (("cq", 0, C_KV), ("ckv", C_KV, C_SG), ("sv", C_SG + SG, C_XQ)):
                for k in range(2):
                    mixer_piece((name, l, k), rows(wi, c0, c1, k * hk, (k + 1) * hk))
            for name, c0 in (("su", C_SG), ("qx", C_XQ)):
                for n in range(2):
                    mixer_piece((name, l, n), rows(wi, c0 + n * W, c0 + (n + 1) * W))
            for n in range(2):
                mixer_piece(("uq", l, n), rows(w_uq[l], n * H * QK // 2, (n + 1) * H * QK // 2), split=False)
            mixer_piece(("ukv", l), rows(w_uk[l], 0, H * NOPE), rows(w_uv[l], 0, BW), split=False)
            for n in (1, 2, 0):
                for f in range(4):
                    c0 = C_GATE + n * D + f * W
                    mixer_piece(("gate", l, n, f), rows(wi, c0, c0 + W))
                    if f % 2 == 0:
                        mixer_piece(("br", l, n, f // 2), rows(w_br[l, n], f * W, (f + 2) * W))
            for n in range(2):
                for k in range(2):
                    mixer_piece(("out", l, n, k), rows(w_out[l], n * HALF, (n + 1) * HALF, k * hk, (k + 1) * hk))
            first = len(pieces)
            if l % 2 == 0:
                j = l // 2
                for b in range(ND + 1):
                    if b < ND:
                        z = min((b + 1) * BD * P, FD)
                        for name, w in (("w1", dense_w1), ("w3", dense_w3)):
                            piece((name, l, b), RAW, rows(w[j], b * BD * P, z))
                    if b:
                        piece(("w2", l, b - 1), RAW,
                              rows(dense_w2[j], 0, D, (b - 1) * BD * P, min(b * BD * P, FD)))
        E0 = sum(1 for p in pieces if p[3] is not None)
        e_pieces = []
        for b in range(NM):
            e_pieces += [("w1", b, 0), ("w1", b, 1), ("w3", b, 0), ("w3", b, 1)]
            if b:
                e_pieces += [("w2", b - 1, 0), ("w2", b - 1, 1)]
        e_pieces += [("w2", NM - 1, 0), ("w2", NM - 1, 1)]
        PER_E = len(e_pieces)
        assert PER_E % RAW == 0 and PER_E % SPLIT == 0
        e_at = {key: i for i, key in enumerate(e_pieces)}
        e_base = [16 * sum(len(p[2]) for p in pieces if p[1] == s) for s in range(RAW)]

        def raw_wait(eng, n):
            s = pieces[n][1]
            eng.wait_ge(raw_in[s], 16 * sum(len(p[2]) for p in pieces[:n + 1] if p[1] == s))

        def floats(n):
            return sum(src.shape[1] * src.shape[2] for src in pieces[n][2])

        marks = {}

        def reached(eng, name, j=0):
            count, per = marks[name]
            eng.wait_ge(products, count + per * j)

        def full(eng, name, j=0):
            reached(eng, name, j)
            return banks[groups[name].bank]

        def read(eng, name, j=0):
            g = groups[name]
            eng.wait_ge(bank_free[g.bank], g.use + g.per * j)

        def free(ins, name):
            ins.then_inc(bank_free[groups[name].bank], 1)

        unit_names = [("unit", l) + s[1:] for l in range(DEPTH)
                      for s in [s for s in steps if s[0] == "unit"] + [("unit", 0, d) for d in range(KD)]]
        N_SQ, n = [], 0
        for l in range(DEPTH):
            N_SQ += [n + T, n + 2 * T, n + 6 * T]
            n += 6 * T
        N_SQ.append(n + T)

        split_order = [n for n, p in enumerate(pieces) if p[3] is not None]

        def room(name, after=0):
            limit = marks[name][0] + after
            for m, n in enumerate(split_order):
                key, slot = pieces[n][:2]
                old = [("piece",) + pieces[split_order[m - SPLIT]][0]] if m >= SPLIT else []
                for q in range(n - 1, -1, -1):
                    if pieces[q][1] == slot:
                        if pieces[q][3] is None:
                            old.append(pieces[q][0])
                        break
                if slot >= MIX_RAW:
                    old.append(("o", key[1], T - 1))
                if any(marks[o][0] >= limit for o in old):
                    return m
            return len(split_order)

        def job_room(name, after=0):
            limit = marks[name][0] + after
            return sum(1 for i in range(PER_E)
                       if i < SPLIT or marks[("e_piece",) + e_pieces[i - SPLIT]][0] < limit)

        block = ctx.enter_context(nc.Block())

        @block.gpsimd
        def _(pool):
            n = 0
            for tile, value in ((ident, 0.0), (lower, 1.0), (ones, 1.0)):
                nc.gpsimd.memset(tile[:, :], value).then_inc(pool_step, 1)
            for i in range(ROPE // 2):
                f = np.float32(1.0) / np.power(np.float32(10000.0), np.float32(2 * i) / np.float32(ROPE))
                nc.gpsimd.memset(inv_freq[:, i:i + 1], float(f)).then_inc(pool_step, 1)
            pool.wait_ge(pool_step, 3)
            nc.gpsimd.affine_select(out=ident[:, :], in_=ident[:, :], compare_op=ALU.not_equal, fill=1.0,
                                    base=0, pattern=[[-1, P]], channel_multiplier=1).then_inc(consts, 1)
            nc.gpsimd.affine_select(out=lower[:, :], in_=lower[:, :], compare_op=ALU.is_gt, fill=0.0,
                                    base=0, pattern=[[1, P]], channel_multiplier=-1).then_inc(consts, 1)
            nc.gpsimd.iota(iota_cap[:, :], pattern=[[1, CAP]], base=0, channel_multiplier=0,
                           allow_small_or_imprecise_dtypes=True).then_inc(consts, 1)
            nc.gpsimd.iota(iota_e[:, :], pattern=[[1, NE]], base=0, channel_multiplier=0,
                           allow_small_or_imprecise_dtypes=True).then_inc(consts, 1)
            nc.gpsimd.memset(rank[:, :, :], -1.0).then_inc(consts, 1)
            nc.gpsimd.memset(comb[:, :, :], 0.0).then_inc(consts, 1)

        N_CONST = 6

        @block.tensor
        def _(pe):
            count, recording = 0, True

            def mark(ins, *names):
                nonlocal count
                count += 1
                ins.then_inc(products, 1)
                if recording:
                    for name in names:
                        marks[name] = [count, 0]

            def claim(name, j=0):
                g = groups[name]
                if g.use > 1:
                    pe.wait_ge(bank_free[g.bank], g.use - 1 + g.per * j)
                return banks[g.bank]

            def acc(bank, lhs, rhs, n):
                for k in range(n):
                    ins = nc.tensor.matmul(bank, lhs(k), rhs(k), start=(k == 0), stop=(k == n - 1))
                return ins

            def acc3(bank, lhs, rhs, chunks, start, stop):
                for k in chunks:
                    for a, b in ((0, 0), (0, 1), (1, 0)):
                        ins = nc.tensor.matmul(bank, lhs(a, k), rhs(b, k), start=(start and k == chunks[0] and a + b == 0),
                                               stop=(stop and k == chunks[-1] and a == 1))
                return ins

            def weight(key, k):
                n = nth_piece[key]
                m = pieces[n][3]
                pe.wait_ge(lo_ready, m + 1)
                size = floats(n)
                return [w[:, m % SPLIT, 0:size].rearrange("p (k c) -> p k c", k=k) for w in (whi, wlo)]

            def raw_weight(key):
                n = nth_piece[key]
                raw_wait(pe, n)
                return raw[:, pieces[n][1], :]

            def tok(t):
                return slice(t * P, (t + 1) * P)

            pe.wait_ge(consts, 1)
            pe.wait_ge(vecs_in, 16 * 7)
            b = claim("vecs")
            mark(nc.tensor.transpose(b[:, 0:n_vec], vec_rows, ident[0:n_vec, 0:n_vec]), "vecs")

            def transpose_rows(name, src, n):
                b = claim(name)
                for c in range(min(2, src.shape[2] // P - 2 * n)):
                    for t in range(T):
                        a = c * SEQ + t * P
                        ins = nc.tensor.transpose(b[:, a:a + P], src[:, t, tok(2 * n + c)], ident[:, :])
                mark(ins, name)

            def transpose_norm(i):
                pe.wait_ge(hn_ready, T * (i + 1))
                for n in range(4):
                    transpose_rows(("nT", i, n), hn, n)

            for l in range(DEPTH):
                def token_major(name, src):
                    bs = None
                    for k in range(2):
                        w = weight((name, l, k), KD // 2)
                        width = w[0].shape[2]
                        for t in range(T):
                            if k == 0:
                                claim((name, l, t))
                            ins = acc3(banks[groups[name, l, t].bank][:, 0:width],
                                       lambda a, q: src[a][:, q, tok(t)], lambda a, q: w[a][:, q - 4 * k, :],
                                       range(4 * k, 4 * k + 4), k == 0, k == 1)
                            if k == 1 and t == 0:
                                mark(ins, (name, l, 0))
                        if k == 0:
                            mark(ins, ("piece", name, l, 0))
                        else:
                            mark(ins, (name, l, 1), ("piece", name, l, 1))

                def transposed(name, src):
                    for n in range(2):
                        w = weight((name, l, n), KD)
                        b = claim((name, l, n))
                        for c in range(2):
                            ins = acc3(b[:, c * SEQ:(c + 1) * SEQ], lambda a, k: w[a][:, k, tok(c)],
                                       lambda a, k: src[a][:, k, :], range(KD), True, True)
                        mark(ins, (name, l, n), ("piece", name, l, n))

                transpose_norm(3 * l)
                for n in range(4):
                    read(pe, ("nT", 3 * l, n))
                transposed("mk", mT)
                token_major("mv", mT)
                transpose_norm(3 * l + 1)
                for n in range(4):
                    read(pe, ("nT", 3 * l + 1, n))
                token_major("cq", hT)
                token_major("ckv", hT)
                token_major("sv", hT)
                transposed("su", hT)
                transposed("qx", hT)
                pe.wait_ge(ws_in, 16 * (l + 1))
                b = claim(("wsT", l))
                for g in range(G):
                    ins = nc.tensor.transpose(b[:, tok(g)], ws_raw[:, g, :], ident[:, :])
                mark(ins, ("wsT", l))
                for t in range(T):
                    read(pe, ("ckv", l, t))
                    read(pe, ("cq", l, t))
                for n in range(3):
                    transpose_rows(("cT", l, n), cqkv[:, :, 0:QR + KVR], n)
                for n in range(3):
                    read(pe, ("cT", l, n))
                for n in range(2):
                    w = raw_weight(("uq", l, n))[:, 0:3 * 384].rearrange("p (k c) -> p k c", k=3)
                    for t in range(T):
                        b = claim(("q", l, t, n))
                        ins = acc(b[:, 0:384], lambda k: cT[:, k, tok(t)], lambda k: w[:, k, :], 3)
                        mark(ins, ("q", l, t, n), *([("uq", l, n)] if t else []))
                w = raw_weight(("ukv", l)).rearrange("p (k c) -> p k c", k=4)
                for i, name in enumerate(("k", "v")):
                    for t in range(T):
                        b = claim((name, l, t))
                        ins = acc(b[:, :], lambda k: cT[:, 3 + k, tok(t)], lambda k: w[:, 2 * i + k, :], 2)
                        mark(ins, (name, l, t), *([("ukv", l)] if i and t else []))
                pe.wait_ge(vn_ready, T * (l + 1))
                read(pe, ("wsT", l))
                for t in range(T):
                    b = claim(("sg", l, t))
                    for g in range(G):
                        ins = nc.tensor.matmul(b[:, tok(g)], sv[:, t, tok(g)], wsT[:, g, :], start=True, stop=True)
                    mark(ins, ("sg", l, t))

                def unit(n, d):
                    name = ("unit", l, n, d)
                    wg = weight(("gate", l, n, d // 2), KD)
                    b = claim(name)
                    ins = acc3(b[:, 0:SEQ], lambda a, k: wg[a][:, k, tok(d % 2)], lambda a, k: hT[a][:, k, :],
                               range(KD), True, True)
                    if d % 2:
                        mark(ins, ("piece", "gate", l, n, d // 2))
                    wb = weight(("br", l, n, d // 4), KB)
                    if d == 0:
                        if n == 1:
                            pe.wait_ge(yb_ready, l + 1)
                        for i in range(XH if n == 2 else 0):
                            read(pe, ("mo", l, i))
                        for i in range(2 if n == 0 else 0):
                            read(pe, ("oT", l, i))
                    ins = acc3(b[:, SEQ:2 * SEQ], lambda a, k: wb[a][:, k, tok(d % 4)],
                               lambda a, k: yT[a][:, n // 2, k, :], range(KB), True, True)
                    mark(ins, name, *([("piece", "br", l, n, d // 4)] if d % 4 == 3 else []))

                for step in steps:
                    kind = step[0]
                    name = (kind, l) + step[1:]
                    if kind == "unit":
                        unit(*step[1:])
                        continue
                    h = step[1]
                    nth = l * (XH + H) + h + (0 if kind[0] == "m" else XH)
                    if kind == "ms":
                        if h == 0:
                            for n in range(2):
                                read(pe, ("qx", l, n))
                                read(pe, ("mk", l, n))
                        b = claim(name)
                        for t in range(T):
                            ins = nc.tensor.matmul(b[:, t * SEQ:(t + 1) * SEQ], qxT[:, h, tok(t)], mkT[:, h, :],
                                                   start=True, stop=True)
                        mark(ins, name)
                    elif kind in ("mpT", "apT"):
                        if kind == "mpT":
                            pe.wait_ge(prob_ready, l * XH + h + 1)
                        else:
                            read(pe, ("as", l, h))
                        b = claim(name)
                        for kt in range(T):
                            for t in range(T):
                                a = kt * SEQ + t * P
                                ins = nc.tensor.transpose(b[:, a:a + P], prob[:, nth % 2, t, tok(kt)], ident[:, :])
                        mark(ins, name)
                    elif kind == "mo":
                        read(pe, ("mpT", l, h))
                        if h == 0:
                            for t in range(T):
                                read(pe, ("mv", l, t))
                        b = claim(name)
                        mark(acc(b[:, 0:SEQ], lambda k: mv[:, k, tok(h)], lambda k: probT[:, nth % 2, k, :], T), name)
                    elif kind in ("qT", "kT"):
                        t, n = step[1:]
                        if n == 0:
                            pe.wait_ge(q_ready if kind == "qT" else k_ready, l + 1)
                        src = q_sb if kind == "qT" else k_sb
                        b = claim(name)
                        for i in range(4):
                            ins = nc.tensor.transpose(b[0:QK, tok(i)], src[:, t, 4 * n + i, :], ident[:, :])
                        mark(ins, name)
                    elif kind == "as":
                        if h == 0:
                            for t in range(T):
                                for n in range(2):
                                    read(pe, ("qT", l, t, n))
                                    read(pe, ("kT", l, t, n))
                        b = claim(name)
                        for t in range(T):
                            ins = nc.tensor.matmul(b[:, t * SEQ:(t + 1) * SEQ], qT[0:QK, h, tok(t)], kT[0:QK, h, :],
                                                   start=True, stop=True)
                        mark(ins, name)
                    else:
                        read(pe, ("apT", l, h))
                        w = BW // H
                        for t in range(T):
                            if h == 0:
                                read(pe, ("v", l, 0))
                                read(pe, ("v", l, 1))
                                claim(("o", l, t))
                            ins = acc(banks[4 + t][:, h * w:(h + 1) * w], lambda k: probT[:, nth % 2, k, tok(t)],
                                      lambda k: v_sb[:, k, h * w:(h + 1) * w], T)
                            if h == H - 1:
                                mark(ins, ("o", l, t))
                for t in range(T):
                    read(pe, ("o", l, t))
                for n in range(2):
                    transpose_rows(("oT", l, n), o_sb, n)
                for d in range(KD):
                    unit(0, d)
                pe.wait_ge(merged, KD * (l + 1))
                for n in range(2):
                    for k in range(2):
                        w = weight(("out", l, n, k), KD // 2)
                        for t in range(T):
                            name = ("out", l, t, n)
                            if k == 0:
                                claim(name)
                            ins = acc3(banks[groups[name].bank][:, :], lambda a, q: mT[a][:, q, tok(t)],
                                       lambda a, q: w[a][:, q - 4 * k, :], range(4 * k, 4 * k + 4), k == 0, k == 1)
                            if k:
                                mark(ins, name, *([("piece", "out", l, n, k)] if t else []))
                        if k == 0:
                            mark(ins, ("piece", "out", l, n, k))
                transpose_norm(3 * l + 2)
                for n in range(4):
                    read(pe, ("nT", 3 * l + 2, n))
                if l % 2 == 0:
                    def up(b_):
                        w1, w3 = weight(("w1", l, b_), KD), weight(("w3", l, b_), KD)
                        last = min(BD, FCD - b_ * BD) - 1
                        for cc in range(last + 1):
                            name = ("up", l, b_ * BD + cc)
                            b = claim(name)
                            ins = acc3(b[:, 0:SEQ], lambda a, k: w1[a][:, k, tok(cc)], lambda a, k: hT[a][:, k, :],
                                       range(KD), True, True)
                            if cc == last:
                                mark(ins, ("piece", "w1", l, b_))
                            ins = acc3(b[:, SEQ:2 * SEQ], lambda a, k: w3[a][:, k, tok(cc)],
                                       lambda a, k: hT[a][:, k, :], range(KD), True, True)
                            mark(ins, name, *([("piece", "w3", l, b_)] if cc == last else []))

                    def down(b_):
                        m = min(BD, FCD - b_ * BD)
                        w2 = weight(("w2", l, b_), m)
                        read(pe, ("up", l, b_ * BD + m - 1))
                        for t in range(T):
                            for n in range(2):
                                name = ("y", l, 2 * t + n)
                                if b_ == 0:
                                    claim(name)
                                ins = acc3(banks[4 + 2 * t + n][:, :], lambda a, c: gated_d[a][:, b_ % 2, c, tok(t)],
                                           lambda a, c: w2[a][:, c, n * HALF:(n + 1) * HALF], range(m),
                                           b_ == 0, b_ == ND - 1)
                                if b_ == ND - 1:
                                    mark(ins, name, *([("piece", "w2", l, b_)] if t and n else []))
                        if b_ < ND - 1:
                            mark(ins, ("piece", "w2", l, b_))

                    for b_ in range(ND + 1):
                        if b_ < ND:
                            up(b_)
                        if b_:
                            down(b_ - 1)

            l = DEPTH - 1
            pe.wait_ge(router_in, 16)
            b = claim(("logits", l))
            for t in range(T):
                for k in range(KD):
                    for a in range(2):
                        ins = nc.tensor.matmul(b[:, t * NE:(t + 1) * NE], hT[a][:, k, tok(t)].bitcast(F32), wrt[:, k, :],
                                               start=(k + a == 0), stop=(k == KD - 1 and a == 1))
            mark(ins, ("logits", l))
            pe.wait_ge(consts, N_CONST)
            pe.wait_ge(mask_ready, 1)
            b = claim(("rank", l))
            nc.tensor.matmul(b[:, 0:NE], lower[:, :], mask[:, 0, :], start=True, stop=True)
            nc.tensor.matmul(b[:, NE:2 * NE], ones[:, :], mask[:, 0, :], start=True, stop=False)
            nc.tensor.matmul(b[:, NE:2 * NE], lower[:, :], mask[:, 1, :], start=False, stop=True)
            nc.tensor.matmul(b[:, 2 * NE:3 * NE], ones[:, :], mask[:, 0, :], start=True, stop=False)
            ins = nc.tensor.matmul(b[:, 2 * NE:3 * NE], ones[:, :], mask[:, 1, :], start=False, stop=True)
            mark(ins, ("rank", l))

            def gather(name, n, j):
                b = claim(name, j)
                for c in range(4):
                    ins = acc(b[:, c * CAP:(c + 1) * CAP], lambda t: hn[:, t, tok(4 * n + c)], lambda t: sel[:, t, :], T)
                mark(ins, name)

            pe.wait_ge(sel_ready, 1)
            for n in range(2):
                gather(("gather0", l, n), n, 0)

            def job(j):
                def e_weight(kind, b_, half):
                    i = e_at[kind, b_, half]
                    pe.wait_ge(lo_ready, E0 + i + 1 + PER_E * j)
                    return [w[:, (E0 + i) % SPLIT, :].rearrange("p (k c) -> p k c", k=2 if kind == "w2" else 4)
                            for w in (whi, wlo)]

                def up(kind, name, b_):
                    b = claim((name, b_), j)
                    for half in range(2):
                        w = e_weight(kind, b_, half)
                        ins = acc3(b[:, :], lambda a, k: hselT[a][:, half, tok(k)], lambda a, k: w[a][:, k, :],
                                   range(4), half == 0, half == 1)
                        mark(ins, ("e_piece", kind, b_, half), *([(name, b_)] if half else []))

                def hidden_T(b_):
                    read(pe, ("e3", b_), j)
                    b = claim(("eT", b_), j)
                    for c in range(BM):
                        ins = nc.tensor.transpose(b[:, tok(c)], g32_m[:, b_ % 2, tok(c)], ident[:, :])
                    mark(ins, ("eT", b_))

                def down(b_):
                    read(pe, ("eT", b_), j)
                    for half in range(2):
                        w = e_weight("w2", b_, half)
                        for n in range(2):
                            if b_ == 0 and half == 0:
                                claim(("ey", n), j)
                            last = b_ == NM - 1 and half == 1
                            ins = acc3(banks[4 + n][:, :], lambda a, c: gated_m[a][:, b_ % 2, tok(2 * half + c)],
                                       lambda a, c: w[a][:, c, n * HALF:(n + 1) * HALF], range(2),
                                       b_ == 0 and half == 0, last)
                            if last and n == 0:
                                mark(ins, ("ey", 0))
                        mark(ins, ("e_piece", "w2", b_, half), *([("ey", 1)] if last else []))

                for n in range(2):
                    read(pe, ("gather", n), j - 1)
                for b_ in range(NM):
                    up("w1", "e1", b_)
                    if b_:
                        hidden_T(b_ - 1)
                    up("w3", "e3", b_)
                    if b_ == 0:
                        b = claim(("selT", 0), j)
                        for t in range(T):
                            ins = nc.tensor.transpose(b[:, tok(t)], sel[:, t, :], ident[:, :])
                        mark(ins, ("selT", 0))
                    if b_:
                        down(b_ - 1)
                pe.wait_ge(sel_ready, j + 2)
                for n in range(2):
                    gather(("gather", n), n, j)
                hidden_T(NM - 1)
                down(NM - 1)
                read(pe, ("selT", 0), j)
                for n in range(2):
                    read(pe, ("ey", n), j)
                    for t in range(T):
                        b = claim(("scatter", 2 * n + t), j)
                        ins = nc.tensor.matmul(b[:, :], selT[:, t, :], y_sb[:, n * HALF:(n + 1) * HALF],
                                               start=True, stop=True)
                        mark(ins, ("scatter", 2 * n + t))

            before, names = count, set(marks)
            with pe.Fori(0, NE) as j:
                job(j)
            recording = False
            for name in set(marks) - names:
                marks[name][1] = count - before
            pe.wait_ge(flag_ready, 1)
            overflow = pe.value_load(more[0:1, 0:1], min_val=0, max_val=1)
            with pe.If(overflow > 0):
                with pe.Fori(NE, JOBS) as j:
                    job(j)

        @block.sync
        def _(sp):
            last_in = {}
            for n, (key, slot, parts, n_split) in enumerate(pieces):
                if slot in last_in:
                    old = pieces[last_in[slot]]
                    if old[3] is None:
                        reached(sp, old[0])
                    else:
                        sp.wait_ge(lo_ready, old[3] + 1)
                if slot >= MIX_RAW:
                    read(sp, ("o", key[1], T - 1))
                offset = 0
                for src in parts:
                    chunks, width = src.shape[1], src.shape[2]
                    dst = raw[:, slot, offset:offset + chunks * width].rearrange("p (k c) -> p k c", k=chunks)
                    sp.dma_start(dst, src).then_inc(raw_in[slot], 16)
                    offset += chunks * width
                last_in[slot] = n

            def job_loads(j, e, first_job):
                for i, (kind, b, half) in enumerate(e_pieces):
                    slot = i % RAW
                    if first_job and i < RAW:
                        old = pieces[last_in[slot]]
                        sp.wait_ge(lo_ready, old[3] + 1)
                        if slot >= MIX_RAW:
                            read(sp, ("o", DEPTH - 1, T - 1))
                    else:
                        sp.wait_ge(lo_ready, E0 + i - RAW + 1 + PER_E * j)
                    if kind == "w2":
                        r0 = (b * BM + half * BM // 2) * P
                        src = moe_w2[0, e, r0:r0 + BM // 2 * P, :]
                    else:
                        src = (moe_w1 if kind == "w1" else moe_w3)[0, e, half * D // 2:(half + 1) * D // 2,
                                                                  b * BM * P:(b + 1) * BM * P]
                    src = src.rearrange("(k p) c -> p k c", p=P)
                    dst = raw[:, slot, :].rearrange("p (k c) -> p k c", k=src.shape[1])
                    sp.dma_start(dst, src).then_inc(raw_in[slot], 16)

            job_loads(0, 0, True)
            with sp.Fori(1, NE) as e:
                job_loads(e, e, False)
            read(sp, ("nT", 3 * DEPTH - 1, 3))
            sp.dma_start(gf_row, g_final.partition_broadcast(P)).then_inc(gf_in, 16)
            sp.wait_ge(flag_ready, 1)
            overflow = sp.value_load(more[0:1, 0:1], min_val=0, max_val=1)
            with sp.If(overflow > 0):
                with sp.Fori(0, JOBS - NE) as e:
                    job_loads(e + NE, e, False)
            for t in range(T):
                sp.wait_ge(y_final, t + 1)
                sp.dma_start(out[0, t * P:(t + 1) * P, :], hn[:, t, :]).then_inc(stored, 16)
            sp.wait_ge(stored, 16 * T)

        @block.scalar
        def _(act):
            act.dma_start(vec_rows[c_of["mem"]:c_of["mem"] + KD, :],
                          g_mem.rearrange("(k p) -> k p", p=P)).then_inc(vecs_in, 16)
            act.dma_start(mem_sb, mem[0].rearrange("(t p) c -> p t c", p=P)).then_inc(mem_in, 16)
            act.dma_start(x_sb[:, :, :], x[0].rearrange("(t p) c -> p t c", p=P)).then_inc(x_in, 16)
            for name, v in (("mix", g_mix), ("ffn", g_ffn), ("q", g_q), ("kv", g_kv), ("sg", g_sg)):
                n = v.shape[0] * v.shape[1] // P
                act.dma_start(vec_rows[c_of[name]:c_of[name] + n, :],
                              v.rearrange("l (k p) -> (l k) p", p=P)).then_inc(vecs_in, 16)
            act.dma_start(vec_rows[c_of["gate"]:n_vec, :],
                          b_gate.rearrange("l n (k p) -> (l n k) p", p=P)).then_inc(vecs_in, 16)
            act.dma_start(pos_i[:, :], positions[0].rearrange("(t p) -> p t", p=P),
                          allow_slow_non_contiguous=True).then_inc(pos_in, 16)
            act.dma_start(wrt[:, :, :], w_router[0].rearrange("(k p) e -> p k e", p=P)).then_inc(router_in, 16)

            n_sq = 0
            n_hi = 0

            def hi_parts(m_end):
                nonlocal n_hi
                for m in range(n_hi, m_end):
                    n = split_order[m]
                    raw_wait(act, n)
                    if m >= SPLIT:
                        reached(act, ("piece",) + pieces[split_order[m - SPLIT]][0])
                    nc.scalar.activation(whi[:, m % SPLIT, 0:floats(n)], raw[:, pieces[n][1], 0:floats(n)],
                                         ACT.Copy).then_inc(hi_ready, 1)
                n_hi = max(n_hi, m_end)

            def own_squares():
                if n_sq:
                    act.wait_ge(squares, n_sq)

            def square(src, width, col, products_to=junk):
                nonlocal n_sq
                own_squares()
                nc.scalar.activation(products_to[:, 0:width], src, ACT.Square,
                                     accum_out=sumsq[:, col:col + 1]).then_inc(squares, 1)
                n_sq += 1

            def norm_stats(src, products_to=junk):
                for t in range(T):
                    square(src[:, t, :], D, 6 + t, products_to)

            def norm_hi(i, dst, gain):
                for n in range(4):
                    b = full(act, ("nT", i, n))
                    for c in range(2):
                        k = 2 * n + c
                        ins = nc.scalar.activation(dst[0][:, k, :], b[:, c * SEQ:(c + 1) * SEQ], ACT.Copy,
                                                   scale=cols[:, gain + k:gain + k + 1])
                    ins.then_inc(hT_hi, 1)

            n_unit = 0
            for l in range(DEPTH):
                act.wait_ge(mem_in, 16 * (l + 1))
                norm_stats(mem_sb, hn[:, 0, :])
                if l == 0:
                    read(act, "vecs")
                    hi_parts(SPLIT)
                    act.wait_ge(x_in, 16)
                else:
                    hi_parts(room(("y", l - 1, 3), 1))
                    for n in range(4):
                        read(act, ("y", l - 1, n))
                act.wait_ge(hn_ready, T * (3 * l + 1))
                norm_stats(x_sb)
                norm_hi(3 * l, mT, c_of["mem"])
                if l == 0:
                    act.wait_ge(angles, 1)
                    nc.scalar.activation(sin_t[:, :, :], ang[:, 2, :, :], ACT.Sin).then_inc(trig, 1)
                    nc.scalar.activation(cos_t[:, :, :], ang[:, 3, :, :], ACT.Sin).then_inc(trig, 1)
                for n in range(2):
                    hi_parts(room(("mk", l, n)))
                    b = full(act, ("mk", l, n))
                    free(nc.scalar.activation(mkT[:, 2 * n:2 * n + 2, :].rearrange("p h s -> p (h s)"), b[:, :],
                                              ACT.Copy), ("mk", l, n))
                hi_parts(room(("mv", l, 1), 1))
                norm_hi(3 * l + 1, hT, c_of["mix"] + l * KD)
                act.dma_start(ws_raw, w_s[l].rearrange("g i j -> i g j")).then_inc(ws_in, 16)
                act.dma_start(bs_row, b_s[l].rearrange("g i -> (g i)").partition_broadcast(P)).then_inc(row_in, 16)
                for t in range(T):
                    hi_parts(room(("cq", l, t)))
                    b = full(act, ("cq", l, t))
                    square(b[:, 0:QR], QR, t)
                    free(nc.scalar.activation(cqkv[:, t, 0:QR], b[:, 0:QR], ACT.Copy), ("cq", l, t))
                for t in range(T):
                    hi_parts(room(("ckv", l, t)))
                    b = full(act, ("ckv", l, t))
                    square(b[:, 0:KVR], KVR, 2 + t)
                    free(nc.scalar.activation(cqkv[:, t, QR:], b[:, 0:KVR + ROPE], ACT.Copy), ("ckv", l, t))
                for t in range(T):
                    hi_parts(room(("sv", l, t)))
                    b = full(act, ("sv", l, t))
                    free(nc.scalar.activation(sv[:, t, :], b[:, :], ACT.Gelu_apprx_tanh), ("sv", l, t))
                for t in range(T):
                    read(act, ("sv", l, t))
                    square(sv[:, t, :], SG, 4 + t)
                own_squares()
                for n in range(2):
                    hi_parts(room(("su", l, n)))
                    b = full(act, ("su", l, n))
                    free(nc.scalar.activation(uT[:, 2 * n:2 * n + 2, :].rearrange("p h s -> p (h s)"), b[:, :],
                                              ACT.Gelu_apprx_tanh), ("su", l, n))
                for n in range(2):
                    hi_parts(room(("qx", l, n)))
                hi_parts(room(("wsT", l)))
                b = full(act, ("wsT", l))
                free(nc.scalar.activation(hn[:, 1, G * P:], b[:, :], ACT.Copy), ("wsT", l))
                act.wait_ge(lat_inv, l + 1)
                for t in range(T):
                    for n in range(2):
                        hi_parts(room(("q", l, t, n)))
                        b = full(act, ("q", l, t, n))
                        free(nc.scalar.activation(q_sb[:, t, 4 * n:4 * n + 4, :].rearrange("p h d -> p (h d)"),
                                                  b[:, 0:4 * QK], ACT.Copy, scale=rin[:, t:t + 1]), ("q", l, t, n))
                for t in range(T):
                    hi_parts(room(("k", l, t)))
                    b = full(act, ("k", l, t))
                    free(nc.scalar.activation(k_sb[:, t, :, 0:NOPE], b[:, :].rearrange("p (h d) -> p h d", h=H),
                                              ACT.Copy, scale=rin[:, 2 + t:3 + t]), ("k", l, t))

                def unit_tanh(n, d):
                    nonlocal n_unit
                    u = n_unit
                    n_unit += 1
                    if u >= 2:
                        read(act, unit_names[u - 2])
                    b = full(act, ("unit", l, n, d))
                    c = (l * NBR + n) * KD + d
                    nc.scalar.activation(sig[:, u % 2, :], b[:, 0:SEQ], ACT.Tanh, scale=0.5,
                                         bias=half_gate[:, c:c + 1]).then_inc(tanh_ready, 1)

                own_squares()
                for step in steps:
                    kind = step[0]
                    name = (kind, l) + step[1:]
                    if kind != "O":
                        hi_parts(room(name))
                    if kind in ("ms", "as"):
                        h = step[1]
                        nth = l * (XH + H) + h + (XH if kind == "as" else 0)
                        act.wait_ge(max_ready, nth + 1)
                        b = banks[groups[name].bank]
                        for t in range(T):
                            total = rsum[:, nth % 2, t:t + 1] if kind == "ms" else asum[:, t, h:h + 1]
                            ins = nc.scalar.activation(prob[:, nth % 2, t, :], b[:, t * SEQ:(t + 1) * SEQ], ACT.Exp,
                                                       scale=XS if kind == "ms" else QS,
                                                       bias=nmax[:, nth % 2, t:t + 1], accum_out=total)
                        free(ins, name)
                    elif kind in ("mpT", "apT"):
                        h = step[1]
                        nth = l * (XH + H) + h + (XH if kind == "apT" else 0)
                        b = full(act, name)
                        free(nc.scalar.activation(probT[:, nth % 2, :, :].rearrange("p k s -> p (k s)"), b[:, :],
                                                  ACT.Copy), name)
                    elif kind == "mo":
                        b = full(act, name)
                        nc.scalar.activation(yT[0][:, 1, step[1], :], b[:, 0:SEQ], ACT.Copy).then_inc(y_hi, 1)
                    elif kind == "kT":
                        t, n = step[1:]
                        b = full(act, name)
                        free(nc.scalar.activation(kT[0:QK, 4 * n:4 * n + 4, t * P:(t + 1) * P],
                                                  b[0:QK, :].rearrange("p (h s) -> p h s", h=4), ACT.Copy), name)
                    elif kind == "unit":
                        unit_tanh(*step[1:])
                for n in range(2):
                    hi_parts(room(("oT", l, n)))
                    b = full(act, ("oT", l, n))
                    nc.scalar.activation(yT[0][:, 0, 2 * n:2 * n + 2, :].rearrange("p h s -> p (h s)"), b[:, :],
                                         ACT.Copy).then_inc(y_hi, 1)
                for d in range(KD):
                    hi_parts(room(("unit", l, 0, d)))
                    unit_tanh(0, d)
                for n in range(2):
                    for t in range(T):
                        hi_parts(room(("out", l, t, n)))
                        read(act, ("out", l, t, n))
                norm_stats(x_sb)
                hi_parts(room(("out", l, 1, 1), 1))
                norm_hi(3 * l + 2, hT, c_of["ffn"] + l * KD)
                own_squares()
                if l % 2 == 0:
                    for c in range(FCD):
                        hi_parts(room(("up", l, c)))
                        b = full(act, ("up", l, c))
                        nc.scalar.activation(silu_d[:, c % 4, :], b[:, 0:SEQ], ACT.Silu).then_inc(silu_ready, 1)
                    read(act, ("up", l, FCD - 1))
                    act.dma_start(mem_sb, mem[0].rearrange("(t p) c -> p t c", p=P)).then_inc(mem_in, 16)

            act.wait_ge(gap_ready, 1)
            nc.scalar.activation(gap[:, 1, :], gap[:, 0, :], ACT.Exp).then_inc(gap_exp, 1)
            gain = c_of["ffn"] + (DEPTH - 1) * KD

            def rows_T(name, n, j):
                b = full(act, name, j)
                for c in range(4):
                    ins = nc.scalar.activation(hselT[0][:, n, c * CAP:(c + 1) * CAP], b[:, c * CAP:(c + 1) * CAP],
                                               ACT.Copy, scale=cols[:, gain + 4 * n + c:gain + 4 * n + c + 1])
                ins.then_inc(rows_hi, 1)

            for n in range(2):
                rows_T(("gather0", DEPTH - 1, n), n, 0)

            def expert(j):
                n_hi = 0

                def hi_parts(i_end):
                    nonlocal n_hi
                    for i in range(n_hi, i_end):
                        act.wait_ge(raw_in[i % RAW], 16 * (PER_E // RAW) * j + (e_base[i % RAW] + 16 * (i // RAW + 1)))
                        reached(act, ("e_piece",) + e_pieces[i - SPLIT], j if i >= SPLIT else j - 1)
                        nc.scalar.activation(whi[:, (E0 + i) % SPLIT, :], raw[:, i % RAW, :],
                                             ACT.Copy).then_inc(hi_ready, 1)
                    n_hi = max(n_hi, i_end)

                def hidden_hi(b_):
                    hi_parts(job_room(("eT", b_)))
                    b = full(act, ("eT", b_), j)
                    nc.scalar.activation(gated_m[0][:, b_ % 2, :], b[:, :], ACT.Copy).then_inc(g_hi, 1)

                for b_ in range(NM):
                    hi_parts(job_room(("e1", b_)))
                    b = full(act, ("e1", b_), j)
                    if b_ >= 2:
                        read(act, ("e3", b_ - 2), j)
                    else:
                        read(act, ("e3", NM - 1 - b_), j - 1)
                    free(nc.scalar.activation(silu_m[:, b_ % 2, :], b[:, :], ACT.Silu), ("e1", b_))
                    if b_:
                        hidden_hi(b_ - 1)
                    else:
                        hi_parts(job_room(("selT", 0)))
                        b = full(act, ("selT", 0), j)
                        free(nc.scalar.activation(selT.rearrange("p t s -> p (t s)"), b[:, 0:T * P],
                                                  ACT.Copy), ("selT", 0))
                for n in range(2):
                    hi_parts(job_room(("gather", n)))
                    rows_T(("gather", n), n, j)
                hidden_hi(NM - 1)
                hi_parts(PER_E)
                b = full(act, ("ey", 0), j)
                free(nc.scalar.activation(y_sb[:, 0:HALF], b[:, :], ACT.Copy), ("ey", 0))

            with act.Fori(0, NE) as j:
                expert(j)
            act.wait_ge(flag_ready, 1)
            overflow = act.value_load(more[0:1, 0:1], min_val=0, max_val=1)
            with act.If(overflow > 0):
                with act.Fori(NE, JOBS) as j:
                    expert(j)
            for n in range(4):
                read(act, ("scatter", n), overflow * (JOBS - NE) + (NE - 1))
            norm_stats(x_sb)

        @block.vector
        def _(dve):
            n_step = 0

            def link(ins):
                nonlocal n_step
                n_step += 1
                ins.then_inc(dve_step, 1)
                dve.wait_ge(dve_step, n_step)

            V = nc.vector

            def inv_sqrt(a, z, widths):
                v, w, y = nr[:, 0, a:z], nr[:, 1, a:z], rin[:, a:z]
                for i, width in enumerate(widths):
                    link(V.tensor_scalar(nr[:, 0, a + 2 * i:a + 2 * i + 2], sumsq[:, a + 2 * i:a + 2 * i + 2],
                                         1.0 / width, EPS, ALU.mult, ALU.add))
                link(V.tensor_scalar(y.bitcast(I32), v.bitcast(I32), -0.5, 1597463007.0, ALU.mult, ALU.add))
                for i in range(4):
                    link(V.scalar_tensor_tensor(out=w, in0=y, scalar=-0.5, in1=y, op0=ALU.mult, op1=ALU.mult))
                    link(V.tensor_tensor(w, w, v, ALU.mult))
                    link(V.scalar_tensor_tensor(out=y, in0=w, scalar=1.5, in1=y, op0=ALU.add, op1=ALU.mult))

            n_lo = 0

            def lo_parts(m_end):
                nonlocal n_lo
                for m in range(n_lo, m_end):
                    n = split_order[m]
                    size = floats(n)
                    dve.wait_ge(hi_ready, m + 1)
                    V.tensor_tensor(wlo[:, m % SPLIT, 0:size], raw[:, pieces[n][1], 0:size],
                                    whi[:, m % SPLIT, 0:size].bitcast(F32), ALU.subtract).then_inc(lo_ready, 1)
                n_lo = max(n_lo, m_end)

            def normalise(i, src):
                dve.wait_ge(squares, N_SQ[i])
                inv_sqrt(6, 8, [D])
                for t in range(T):
                    V.tensor_scalar(hn[:, t, :], src[:, t, :], rin[:, 6 + t:7 + t], None,
                                    ALU.mult).then_inc(hn_ready, 1)

            def norm_lo(i, dst, gain):
                for n in range(4):
                    b = full(dve, ("nT", i, n))
                    dve.wait_ge(hT_hi, 4 * i + n + 1)
                    for c in range(2):
                        k = 2 * n + c
                        ins = V.scalar_tensor_tensor(out=dst[1][:, k, :], in0=b[:, c * SEQ:(c + 1) * SEQ],
                                                     scalar=cols[:, gain + k:gain + k + 1],
                                                     in1=dst[0][:, k, :].bitcast(F32), op0=ALU.mult, op1=ALU.subtract)
                    free(ins, ("nT", i, n))

            b = full(dve, "vecs")
            V.tensor_copy(cols[:, :], b[:, 0:n_vec])
            free(V.tensor_scalar(half_gate[:, :], b[:, c_of["gate"]:n_vec], 0.5, None, ALU.mult), "vecs")
            read(dve, "vecs")
            normalise(0, mem_sb)
            lo_parts(SPLIT)
            norm_lo(0, mT, c_of["mem"])
            dve.wait_ge(pos_in, 16)
            dve.wait_ge(pool_step, 3 + ROPE // 2)
            link(V.tensor_copy(pos_f[:, :], pos_i[:, :]))
            for t in range(T):
                link(V.tensor_scalar(ang[:, 0, t, :], inv_freq[:, :], pos_f[:, t:t + 1], None, ALU.mult))
            MAGIC = 12582912.0
            C1 = 6.28125
            C2 = 0.00193500518798828125
            C3 = TWO_PI - C1 - C2
            for out_, shift in ((2, 0.0), (3, 0.25)):
                k = ang[:, 1, :, :]
                r = ang[:, out_, :, :]
                link(V.tensor_scalar(k, ang[:, 0, :, :], 1.0 / TWO_PI, shift, ALU.mult, ALU.add))
                link(V.tensor_scalar(k, k, MAGIC, None, ALU.add))
                link(V.tensor_scalar(k, k, -MAGIC, None, ALU.add))
                link(V.scalar_tensor_tensor(out=r, in0=k, scalar=-C1, in1=ang[:, 0, :, :], op0=ALU.mult, op1=ALU.add))
                for c in (C2, C3):
                    link(V.scalar_tensor_tensor(out=r, in0=k, scalar=-c, in1=r, op0=ALU.mult, op1=ALU.add))
                link(V.tensor_scalar(r, r, shift * TWO_PI, None, ALU.add))
                ins = V.tensor_scalar(r, r, 3.14159250, -3.14159250, ALU.min, ALU.max)
                if out_ == 2:
                    link(ins)
            ins.then_inc(angles, 1)

            units = 0
            for l in range(DEPTH):
                if l:
                    lo_parts(room(("y", l - 1, 3)))
                    normalise(3 * l, mem_sb)
                    for t in range(T):
                        for n in range(2):
                            b = full(dve, ("y", l - 1, 2 * t + n))
                            xs = x_sb[:, t, n * HALF:(n + 1) * HALF]
                            free(V.tensor_tensor(xs, xs, b[:, :], ALU.add), ("y", l - 1, 2 * t + n))
                    norm_lo(3 * l, mT, c_of["mem"])
                    lo_parts(room(("y", l - 1, 3), 1))
                dve.wait_ge(x_in, 16)
                reached(dve, ("nT", 3 * l, 3))
                for n in range(2):
                    lo_parts(room(("mk", l, n)))
                normalise(3 * l + 1, x_sb)
                for t in range(T):
                    lo_parts(room(("mv", l, t)))
                    b = full(dve, ("mv", l, t))
                    free(V.tensor_copy(mv[:, t, :], b[:, :]), ("mv", l, t))
                lo_parts(room(("mv", l, 1), 1))
                norm_lo(3 * l + 1, hT, c_of["mix"] + l * KD)
                for name in ("cq", "ckv"):
                    lo_parts(room((name, l, 1)))
                for t in range(T):
                    read(dve, ("ckv", l, t))
                    read(dve, ("cq", l, t))
                inv_sqrt(0, 4, [QR, KVR])
                V.tensor_copy(nr[:, 2, 0:4], rin[:, 0:4]).then_inc(lat_inv, 1)
                lo_parts(room(("sv", l, 1), 1))
                dve.wait_ge(squares, N_SQ[3 * l + 1] + 3 * T)
                inv_sqrt(4, 6, [SG])
                for t in range(T):
                    V.tensor_scalar(sv[:, t, :], sv[:, t, :], rin[:, 4 + t:5 + t], None,
                                    ALU.mult).then_inc(vn_ready, 1)
                for n in range(2):
                    lo_parts(room(("su", l, n)))
                for n in range(2):
                    lo_parts(room(("qx", l, n)))
                    b = full(dve, ("qx", l, n))
                    free(V.tensor_copy(qxT[:, 2 * n:2 * n + 2, :].rearrange("p h s -> p (h s)"), b[:, :]), ("qx", l, n))
                for n in range(3):
                    lo_parts(room(("cT", l, n)))
                    b = full(dve, ("cT", l, n))
                    for c in range(2 if n < 2 else 1):
                        k = 2 * n + c
                        g = c_of["q"] + l * 3 + k if k < 3 else c_of["kv"] + l * 2 + k - 3
                        ins = V.tensor_scalar(cT[:, k, :], b[:, c * SEQ:(c + 1) * SEQ], cols[:, g:g + 1], None, ALU.mult)
                    free(ins, ("cT", l, n))
                for t in range(T):
                    lo_parts(room(("v", l, t)))
                    b = full(dve, ("v", l, t))
                    free(V.tensor_scalar(v_sb[:, t, :], b[:, :], rin[:, 2 + t:3 + t], None, ALU.mult), ("v", l, t))
                dve.wait_ge(row_in, 16 * (l + 1))
                for n in range(2):
                    read(dve, ("su", l, n))
                for t in range(T):
                    lo_parts(room(("sg", l, t)))
                    b = full(dve, ("sg", l, t))
                    for g in range(G):
                        c = c_of["sg"] + l * G + g
                        ins = V.scalar_tensor_tensor(out=mixed[:, t, g * P:(g + 1) * P], in0=b[:, g * P:(g + 1) * P],
                                                     scalar=cols[:, c:c + 1], in1=bs_row[:, g * P:(g + 1) * P],
                                                     op0=ALU.mult, op1=ALU.add)
                    free(ins, ("sg", l, t))
                for t in range(T):
                    read(dve, ("sg", l, t))
                    u = uT[:, :, t * P:(t + 1) * P]
                    link(V.tensor_tensor(u, u, mixed[:, t, :].rearrange("p (g i) -> p g i", g=G), ALU.mult))
                link(V.tensor_copy(yT[0][:, 0, :, :], uT))
                V.tensor_tensor(yT[1][:, 0, :, :], uT, yT[0][:, 0, :, :].bitcast(F32), ALU.subtract).then_inc(yb_ready, 1)

                def rotate(dst, src, heads, ready):
                    h2 = ROPE // 2
                    tmp = sgv[:, :].rearrange("p (n t h r) -> p n t h r", n=4, t=T, h=H)[:, :, :, 0:heads, :]
                    for t in range(T):
                        shape = [P, heads, h2]
                        co = cos_t[:, t, :].unsqueeze(1).broadcast_to(shape)
                        si = sin_t[:, t, :].unsqueeze(1).broadcast_to(shape)
                        a, b_ = src(t)[:, :, 0:h2], src(t)[:, :, h2:ROPE]
                        V.tensor_tensor(tmp[:, 0, t], a, co, ALU.mult)
                        V.tensor_tensor(tmp[:, 1, t], b_, si, ALU.mult)
                        V.tensor_tensor(tmp[:, 2, t], a, si, ALU.mult)
                        link(V.tensor_tensor(tmp[:, 3, t], b_, co, ALU.mult))
                        V.tensor_tensor(dst(t)[:, :, 0:h2], tmp[:, 0, t], tmp[:, 1, t], ALU.subtract)
                        ins = V.tensor_tensor(dst(t)[:, :, h2:ROPE], tmp[:, 2, t], tmp[:, 3, t], ALU.add)
                        if t < T - 1:
                            link(ins)
                    if ready is None:
                        link(ins)
                    else:
                        ins.then_inc(ready, 1)

                def unit_merge(n, d):
                    nonlocal units
                    name = ("unit", l, n, d)
                    units += 1
                    dve.wait_ge(tanh_ready, units)
                    b = banks[groups[name].bank]
                    s_ = sig[:, (units - 1) % 2, :]
                    first = n == 1
                    dst = mixT[:, d, :] if first else gated_tmp[:, units % 2, :]
                    free(V.scalar_tensor_tensor(out=dst, in0=s_, scalar=1.0, in1=b[:, SEQ:2 * SEQ], op0=ALU.add,
                                                op1=ALU.mult), name)
                    if not first:
                        read(dve, name)
                        link(V.tensor_tensor(mixT[:, d, :], mixT[:, d, :], dst, ALU.add))
                    if n == 0:
                        link(V.tensor_copy(mT[0][:, d, :], mixT[:, d, :]))
                        V.tensor_tensor(mT[1][:, d, :], mixT[:, d, :], mT[0][:, d, :].bitcast(F32),
                                        ALU.subtract).then_inc(merged, 1)

                for step in steps:
                    kind = step[0]
                    name = (kind, l) + step[1:]
                    if kind != "O":
                        lo_parts(room(name))
                    if kind in ("ms", "as"):
                        h = step[1]
                        nth = l * (XH + H) + h + (XH if kind == "as" else 0)
                        b = full(dve, name)
                        link(V.tensor_reduce(rmax[:, nth % 2, :], b[:, :].rearrange("p (t s) -> p t s", t=T), AX_X,
                                             ALU.max))
                        V.tensor_scalar(nmax[:, nth % 2, :], rmax[:, nth % 2, :], -(XS if kind == "ms" else QS), None,
                                        ALU.mult).then_inc(max_ready, 1)
                        if kind == "ms":
                            read(dve, name)
                            link(V.reciprocal(rrec[:, nth % 2, :], rsum[:, nth % 2, :]))
                            for t in range(T):
                                ins = V.tensor_scalar(prob[:, nth % 2, t, :], prob[:, nth % 2, t, :],
                                                      rrec[:, nth % 2, t:t + 1], None, ALU.mult)
                            ins.then_inc(prob_ready, 1)
                    elif kind == "mo":
                        h = step[1]
                        b = full(dve, name)
                        dve.wait_ge(y_hi, l * (XH + 2) + h + 1)
                        free(V.tensor_tensor(yT[1][:, 1, h, :], b[:, 0:SEQ], yT[0][:, 1, h, :].bitcast(F32),
                                             ALU.subtract), name)
                        if h == 0:
                            if l == 0:
                                dve.wait_ge(trig, 2)
                            for t in range(T):
                                for n in range(2):
                                    read(dve, ("q", l, t, n))
                                read(dve, ("k", l, t))
                            rotate(lambda t: q_sb[:, t, :, NOPE:QK], lambda t: q_sb[:, t, :, NOPE:QK], H, q_ready)
                            rotate(lambda t: kr[:, t], lambda t: cqkv[:, t, QR + KVR:].unsqueeze(1), 1, None)
                            for t in range(T):
                                ins = V.tensor_copy(k_sb[:, t, :, NOPE:QK], kr[:, t].broadcast_to([P, H, ROPE]))
                            ins.then_inc(k_ready, 1)
                    elif kind == "qT":
                        t, n = step[1:]
                        b = full(dve, name)
                        free(V.tensor_copy(qT[0:QK, 4 * n:4 * n + 4, t * P:(t + 1) * P],
                                           b[0:QK, :].rearrange("p (h s) -> p h s", h=4)), name)
                    elif kind == "unit":
                        unit_merge(*step[1:])
                read(dve, ("as", l, H - 1))
                link(V.reciprocal(arec[:, :, :], asum[:, :, :]))
                for t in range(T):
                    b = full(dve, ("o", l, t))
                    w = BW // H
                    free(V.tensor_tensor(o_sb[:, t, :].rearrange("p (h d) -> p h d", h=H),
                                         b[:, :].rearrange("p (h d) -> p h d", h=H),
                                         arec[:, t, :].unsqueeze(2).broadcast_to([P, H, w]), ALU.mult), ("o", l, t))
                for n in range(2):
                    lo_parts(room(("oT", l, n)))
                    b = full(dve, ("oT", l, n))
                    dve.wait_ge(y_hi, l * (XH + 2) + XH + n + 1)
                    part = [v[:, 0, 2 * n:2 * n + 2, :].rearrange("p h s -> p (h s)") for v in yT]
                    free(V.tensor_tensor(part[1], b[:, :], part[0].bitcast(F32), ALU.subtract), ("oT", l, n))
                for d in range(KD):
                    lo_parts(room(("unit", l, 0, d)))
                    unit_merge(0, d)
                for n in range(2):
                    for t in range(T):
                        lo_parts(room(("out", l, t, n)))
                        b = full(dve, ("out", l, t, n))
                        xs = x_sb[:, t, n * HALF:(n + 1) * HALF]
                        free(V.scalar_tensor_tensor(out=xs, in0=b[:, :], scalar=0.5, in1=xs, op0=ALU.mult,
                                                    op1=ALU.add), ("out", l, t, n))
                normalise(3 * l + 2, x_sb)
                lo_parts(room(("out", l, 1, 1), 1))
                norm_lo(3 * l + 2, hT, c_of["ffn"] + l * KD)
                if l % 2 == 0:
                    for c in range(FCD):
                        lo_parts(room(("up", l, c)))
                        dve.wait_ge(silu_ready, c + 1)
                        b = banks[groups["up", l, c].bank]
                        g = g32_d[:, c % 2, :]
                        part = [v[:, c // BD % 2, c % BD, :] for v in gated_d]
                        link(V.tensor_tensor(g, silu_d[:, c % 4, :], b[:, SEQ:2 * SEQ], ALU.mult))
                        link(V.tensor_copy(part[0], g))
                        free(V.tensor_tensor(part[1], g, part[0].bitcast(F32), ALU.subtract), ("up", l, c))

            l = DEPTH - 1
            b = full(dve, ("logits", l))
            free(V.tensor_copy(logits[:, :, :].rearrange("p t e -> p (t e)"), b[:, 0:T * NE]), ("logits", l))
            read(dve, ("logits", l))
            for t in range(T):
                link(V.max(top_v[:, t, :], logits[:, t, :]))
                link(V.max_index(top_i[:, t, :], top_v[:, t, :], logits[:, t, :]))
            link(V.tensor_copy(top_f[:, :, :], top_i[:, :, :]))
            V.tensor_tensor(gap[:, 0, :], top_v[:, :, 1], top_v[:, :, 0], ALU.subtract).then_inc(gap_ready, 1)
            dve.wait_ge(consts, N_CONST)
            for n in range(2):
                for t in range(T):
                    ins = V.tensor_scalar(hot[:, n, t, :], iota_e[:, :], top_f[:, t, n:n + 1], None, ALU.is_equal)
            link(ins)
            V.tensor_tensor(mask[:, :, :], hot[:, 0, :, :], hot[:, 1, :, :], ALU.add).then_inc(mask_ready, 1)
            dve.wait_ge(mask_ready, 1)
            dve.wait_ge(gap_exp, 1)
            link(V.tensor_scalar(gap[:, 2, :], gap[:, 1, :], 1.0, None, ALU.add))
            link(V.reciprocal(gap[:, 3, :], gap[:, 2, :]))
            link(V.tensor_tensor(gap[:, 2, :], gap[:, 1, :], gap[:, 3, :], ALU.mult))
            for t in range(T):
                link(V.tensor_scalar(comb[:, t, 0:NE], hot[:, 0, t, :], gap[:, 3, t:t + 1], None, ALU.mult))
                link(V.scalar_tensor_tensor(out=comb[:, t, 0:NE], in0=hot[:, 1, t, :], scalar=gap[:, 2, t:t + 1],
                                            in1=comb[:, t, 0:NE], op0=ALU.mult, op1=ALU.add))
            for p in range(1, JOBS // NE):
                ins = V.tensor_copy(comb[:, :, p * NE:(p + 1) * NE], comb[:, :, 0:NE])
            link(ins)
            b = full(dve, ("rank", l))
            rk = logits[:, :, :]
            link(V.scalar_tensor_tensor(out=rk, in0=b[:, 0:T * NE].rearrange("p (t e) -> p t e", t=T), scalar=1.0,
                                        in1=mask[:, :, :], op0=ALU.add, op1=ALU.mult))
            free(V.tensor_reduce(most[:, 0:1], b[:, 2 * NE:3 * NE], AX_X, ALU.max), ("rank", l))
            for p in range(JOBS // NE):
                ins = V.tensor_scalar(rank[:, :, p * NE:(p + 1) * NE], rk, -1.0 - p * CAP, None, ALU.add)
            link(ins)
            read(dve, ("rank", l))
            V.tensor_scalar(more[:, :], most[:, 0:1], float(CAP), None, ALU.is_gt).then_inc(flag_ready, 1)

            def select(j):
                for t in range(T):
                    ins = V.tensor_scalar(sel[:, t, :], iota_cap[:, :], cur[:, 0, t:t + 1], None, ALU.is_equal)
                ins.then_inc(sel_ready, 1)

            gain = c_of["ffn"] + (DEPTH - 1) * KD

            def rows_T(name, n, j, nth):
                b = full(dve, name, j)
                dve.wait_ge(rows_hi, nth)
                for c in range(4):
                    part = [v[:, n, c * CAP:(c + 1) * CAP] for v in hselT]
                    ins = V.scalar_tensor_tensor(out=part[1], in0=b[:, c * CAP:(c + 1) * CAP],
                                                 scalar=cols[:, gain + 4 * n + c:gain + 4 * n + c + 1],
                                                 in1=part[0].bitcast(F32), op0=ALU.mult, op1=ALU.subtract)
                free(ins, name)

            V.tensor_copy(cur[:, 0, :], rank[:, :, 0]).then_inc(cur_ready, 1)
            dve.wait_ge(cur_ready, 1)
            select(0)
            for n in range(2):
                rows_T(("gather0", l, n), n, 0, n + 1)

            def expert(j):
                n_lo = 0

                def lo_parts(i_end):
                    nonlocal n_lo
                    for i in range(n_lo, i_end):
                        s = (E0 + i) % SPLIT
                        dve.wait_ge(hi_ready, PER_E * j + (E0 + i + 1))
                        V.tensor_tensor(wlo[:, s, :], raw[:, i % RAW, :], whi[:, s, :].bitcast(F32),
                                        ALU.subtract).then_inc(lo_ready, 1)
                    n_lo = max(n_lo, i_end)

                def hidden_lo(b_):
                    lo_parts(job_room(("eT", b_)))
                    b = full(dve, ("eT", b_), j)
                    dve.wait_ge(g_hi, NM * j + (b_ + 1))
                    free(V.tensor_tensor(gated_m[1][:, b_ % 2, :], b[:, :], gated_m[0][:, b_ % 2, :].bitcast(F32),
                                         ALU.subtract), ("eT", b_))

                for b_ in range(NM):
                    lo_parts(job_room(("e1", b_)))
                    if b_:
                        hidden_lo(b_ - 1)
                    lo_parts(job_room(("e3", b_)))
                    b = full(dve, ("e3", b_), j)
                    read(dve, ("e1", b_), j)
                    free(V.tensor_tensor(g32_m[:, b_ % 2, :], silu_m[:, b_ % 2, :], b[:, :], ALU.mult), ("e3", b_))
                    if b_ == 1:
                        full(dve, ("selT", 0), j)
                        V.tensor_copy(cur[:, 0, :], rank[:, :, bass.ds(j + 1, 1)].rearrange("p t o -> p (t o)")).then_inc(cur_ready, 1)
                        V.tensor_copy(cur[:, 1, :], comb[:, :, bass.ds(j, 1)].rearrange("p t o -> p (t o)")).then_inc(cur_ready, 1)
                        dve.wait_ge(cur_ready, 2 * j + 3)
                        select(j + 1)
                for n in range(2):
                    lo_parts(job_room(("gather", n)))
                    rows_T(("gather", n), n, j, 2 * j + (n + 3))
                hidden_lo(NM - 1)
                lo_parts(PER_E)
                b = full(dve, ("ey", 1), j)
                free(V.tensor_copy(y_sb[:, HALF:D], b[:, :]), ("ey", 1))
                for n in range(2):
                    for t in range(T):
                        name = ("scatter", 2 * n + t)
                        read(dve, name, j - 1)
                        b = full(dve, name, j)
                        xs = x_sb[:, t, n * HALF:(n + 1) * HALF]
                        free(V.scalar_tensor_tensor(out=xs, in0=b[:, :], scalar=cur[:, 1, t:t + 1], in1=xs,
                                                    op0=ALU.mult, op1=ALU.add), name)

            with dve.Fori(0, NE) as j:
                expert(j)
            dve.wait_ge(flag_ready, 1)
            overflow = dve.value_load(more[0:1, 0:1], min_val=0, max_val=1)
            with dve.If(overflow > 0):
                with dve.Fori(NE, JOBS) as j:
                    expert(j)
            dve.wait_ge(squares, N_SQ[-1])
            dve.wait_ge(gf_in, 16)
            inv_sqrt(6, 8, [D])
            for t in range(T):
                V.scalar_tensor_tensor(out=hn[:, t, :], in0=x_sb[:, t, :], scalar=rin[:, 6 + t:7 + t], in1=gf_row,
                                       op0=ALU.mult, op1=ALU.mult).then_inc(y_final, 1)


_INS = ['x', 'mem', 'positions', 'g_mix', 'w_in', 'g_q', 'g_kv', 'w_uq', 'w_uk', 'w_uv', 'g_sg', 'w_s',
        'b_s', 'g_mem', 'w_mkv', 'w_br', 'b_gate', 'w_out', 'g_ffn', 'dense_w1', 'dense_w3', 'dense_w2',
        'w_router', 'moe_w1', 'moe_w3', 'moe_w2', 'g_final']


def kernel(**inputs):
    from concourse import bacc
    from concourse.bass_utils import run_bass_kernel_spmd

    nc = bacc.Bacc("TRN2", target_bir_lowering=False, num_devices=1)
    arrays, args = {}, []
    for name in _INS:
        a = np.ascontiguousarray(inputs[name])
        arrays[f"in_{name}"] = a
        args.append(nc.dram_tensor(f"in_{name}", a.shape, mybir.dt.from_np(a.dtype), kind="ExternalInput").ap())
    args.append(nc.dram_tensor("out", inputs["x"].shape, F32, kind="ExternalOutput").ap())
    build(nc, *args)
    return run_bass_kernel_spmd(nc, [arrays], core_ids=[0]).results[0]["out"]
```

```python
from contextlib import ExitStack

import numpy as np

import concourse.bass as bass
from concourse import mybir

F32 = mybir.dt.float32
F32R = mybir.dt.float32r
I32 = mybir.dt.int32
U32 = mybir.dt.uint32
ALU = mybir.AluOpType
ACT = mybir.ActivationFunctionType
AX_X = mybir.AxisListType.X

P = 128
CAP = 128
RAW = 7
MIX_RAW = 3
SPLIT = 3
EARLY = 2
MEM_AT = 6
SLOT = 2048
HALF = 512
EPS = 1e-6
TWO_PI = 6.283185307179586


class Group:

    def __init__(self, bank, use, per=0):
        self.bank, self.use, self.per = bank, use, per


def plan_psum(depth, heads, x_heads, fcd, nblk):
    groups, used, turn = {}, [0] * 8, [0]

    def take(name, bank=None, among=(0, 1, 2, 3, 6, 7)):
        if bank is None:
            bank = among[turn[0] % len(among)]
            turn[0] += 1
        used[bank] += 1
        groups[name] = Group(bank, used[bank])

    take("mem_gain")
    for n in range(4):
        take(("nT", 0, n))
    for l in range(depth):
        for n in range(2):
            take(("mk", l, n))
        if l == 0:
            take("vecs")
        for t in range(2):
            take(("mv", l, t))
        for n in range(4):
            take(("nT", 3 * l + 1, n))
        for name in ("cq", "ckv", "sv", "su", "qx"):
            for t in range(2):
                take((name, l, t))
        take(("wsT", l))
        for n in range(3):
            take(("cT", l, n))
        for t in range(2):
            take(("sg", l, t))
        for n in range(2):
            for t in range(2):
                take(("q", l, t, n))
        for step in mixer_steps(heads, x_heads):
            if step[0] != "O":
                take((step[0], l) + step[1:])
        for t in range(2):
            take(("o", l, t), bank=4 + t)
        for n in range(2):
            take(("oT", l, n))
        for d in range(8):
            take(("unit", l, 0, d))
        for n in range(2):
            for t in range(2):
                take(("out", l, t, n))
        for n in range(4):
            take(("nT", 3 * l + 2, n))
        turn[0] = 0
        if l % 2 == 0:
            for c in range(fcd):
                for n in range(4 if c == MEM_AT else 0):
                    take(("nT", 3 * l + 3, n), among=(0, 1, 2, 3))
                take(("up", l, c), among=(0, 1, 2, 3))
            for n in range(4):
                take(("y", l, n), bank=4 + n)
            turn[0] = 0
        else:
            take(("logT", l), bank=6)
            take(("logits", l), bank=7)
            take(("rank", l), bank=6)
            take(("gather0", l, 0), bank=7)
            take(("gather0", l, 1), bank=6)
            start = list(used)
            inside = []
            for b in range(nblk):
                inside.append(("e1", b, 2 * (b % 2)))
                if b:
                    inside.append(("eT", b - 1, 2 * ((b - 1) % 2)))
                inside.append(("e3", b, 2 * (b % 2) + 1))
                if b == 0:
                    inside.append(("selT", 0, 3))
            inside += [("gather", 0, 7), ("eT", nblk - 1, 0), ("gather", 1, 6), ("ey", 0, 4), ("ey", 1, 5)]
            inside += [("scatter", n, n) for n in range(4)]
            for name, n, bank in inside:
                used[bank] += 1
                groups[name, n] = Group(bank, used[bank])
            for name, n, bank in inside:
                groups[name, n].per = used[bank] - start[bank]
    return groups


def mixer_steps(heads, x_heads):
    steps = []
    fill = [(n, d) for n in (1, 2) for d in range(8)]
    for i in range(x_heads + 2):
        if i < x_heads:
            steps.append(("ms", i))
        if i == 0:
            steps += [("k", 0), ("k", 1), ("v", 0), ("v", 1)]
        if 1 <= i <= x_heads:
            steps.append(("mpT", i - 1))
        if i >= 2:
            steps.append(("mo", i - 2))
        steps.append(("unit", *fill.pop(0)))
    for kind in ("qT", "kT"):
        steps += [(kind, i // 2, i % 2) for i in range(4)]
    for i in range(heads + 2):
        if i < heads:
            steps.append(("as", i))
        if 1 <= i <= heads:
            steps.append(("apT", i - 1))
        if i >= 2:
            steps.append(("O", i - 2))
        steps.append(("unit", *fill.pop(0)))
    assert not fill
    return steps


def build(nc, x, mem, positions, g_mix, w_in, g_q, g_kv, w_uq, w_uk, w_uv, g_sg, w_s, b_s, g_mem,
          w_mkv, w_br, b_gate, w_out, g_ffn, dense_w1, dense_w3, dense_w2, w_router, moe_w1, moe_w3,
          moe_w2, g_final, out):
    DEPTH, D, PT = w_in.shape
    SEQ = x.shape[1]
    QR, KVR = g_q.shape[1], g_kv.shape[1]
    SG = g_sg.shape[1]
    G = w_s.shape[1]
    NBR, BW = w_br.shape[1], w_br.shape[2]
    NOPE, ROPE, H, XH = 64, 32, 8, 4
    QK = NOPE + ROPE
    FD, FE, NE = dense_w1.shape[2], moe_w1.shape[3], moe_w1.shape[1]
    T, KD = SEQ // P, D // P
    KB = BW // P
    FCD, FCM = FD // P, FE // P
    BD, BM = 2, 4
    ND, NM = -(-FCD // BD), FCM // BM
    W = SLOT // KD
    assert T == 2 and KD == 8 and W == 256 and NM * BM == FCM and NM % 2 == 1
    C_KV, C_SG = QR, QR + KVR + ROPE
    C_XQ = C_SG + 2 * SG
    C_GATE = C_XQ + BW
    JOBS = NE * (-(-SEQ // CAP))
    QS, XS = QK ** -0.5, (BW // XH) ** -0.5
    steps = mixer_steps(H, XH)
    groups = plan_psum(DEPTH, H, XH, FCD, NM)

    with ExitStack() as ctx:
        def sb(name, shape, dt=F32):
            return ctx.enter_context(nc.sbuf_tensor(name, shape, dt))

        def sem(name):
            return ctx.enter_context(nc.semaphore(name))

        banks = [ctx.enter_context(nc.psum_tensor(f"bank{i}", [P, HALF], F32)) for i in range(8)]
        products = sem("products")
        bank_free = [sem(f"bank_free{i}") for i in range(8)]

        raw = sb("raw", [P, RAW, SLOT])
        whi = sb("whi", [P, SPLIT, SLOT], F32R)
        wlo = sb("wlo", [P, SPLIT, SLOT], F32R)
        x_sb = sb("x_sb", [P, T, D])
        hn = sb("hn", [P, T, D])
        hT = [sb(f"hT_{i}", [P, KD, SEQ], F32R) for i in ("hi", "lo")]
        mT = [sb(f"mT_{i}", [P, KD, SEQ], F32R) for i in ("hi", "lo")]
        yT = [sb(f"yT_{i}", [P, 2, KB, SEQ], F32R) for i in ("hi", "lo")]
        cqkv = sb("cqkv", [P, T, QR + KVR + ROPE])
        cT = sb("cT", [P, 5, SEQ])
        sgv = sb("sgv", [P, T * SG])
        qxT = sb("qxT", [P, XH, SEQ])
        mkT = sb("mkT", [P, XH, SEQ])
        mv = sb("mv", [P, T, BW])
        pbuf = sb("pbuf", [P, T * D])
        ident = sb("ident", [P, P])
        lower = sb("lower", [P, P])
        ones = sb("ones", [P, P])
        iota_cap = sb("iota_cap", [P, CAP])
        iota_e = sb("iota_e", [P, NE])
        n_vec = 2 * DEPTH * KD + DEPTH * (3 + 2 + G) + DEPTH * NBR * KD
        cols = sb("cols", [P, n_vec + KD])
        half_gate = sb("half_gate", [P, DEPTH * NBR * KD])
        inv_freq = sb("inv_freq", [P, ROPE // 2])
        pos_i = sb("pos_i", [P, T], I32)
        pos_f = sb("pos_f", [P, T])
        cos_t = sb("cos_t", [P, T, ROPE // 2])
        sin_t = sb("sin_t", [P, T, ROPE // 2])
        sumsq = sb("sumsq", [P, 12])
        rin = sb("rin", [P, 10])
        nr = sb("nr", [P, 2, 10])
        rmax = sb("rmax", [P, 2, T])
        nmax = sb("nmax", [P, 2, T])
        rsum = sb("rsum", [P, 2, T])
        rrec = sb("rrec", [P, 2, T])
        asum = sb("asum", [P, T, H])
        arec = sb("arec", [P, T, H])
        wrt = sb("wrt", [P, KD, NE])
        logits = sb("logits", [P, T, NE])
        top_v = sb("top_v", [P, T, 8])
        top_i = sb("top_i", [P, T, 8], U32)
        top_f = sb("top_f", [P, T, 8])
        gap = sb("gap", [P, 4, T])
        hot = sb("hot", [P, 2, T, NE])
        mask = sb("mask", [P, T, NE])
        comb = sb("comb", [P, T, JOBS + 8])
        rank = sb("rank", [P, T, JOBS + 8])
        cur = sb("cur", [P, 2, T])
        most = sb("most", [P, 2])
        more = sb("more", [P, 1], I32)

        scratch = raw[:, MIX_RAW:, :].rearrange("p n c -> p (n c)")
        q_sb = scratch[:, 0:T * H * QK].rearrange("p (t h d) -> p t h d", t=T, h=H)
        k_sb = scratch[:, 1536:1536 + T * H * QK].rearrange("p (t h d) -> p t h d", t=T, h=H)
        v_sb = scratch[:, 3072:3072 + T * BW].rearrange("p (t c) -> p t c", t=T)
        qT = scratch[:, 4096:4096 + H * SEQ].rearrange("p (h s) -> p h s", h=H)
        kT = scratch[:, 6144:6144 + H * SEQ].rearrange("p (h s) -> p h s", h=H)
        prob = pbuf[:, 0:2 * T * SEQ].rearrange("p (n t s) -> p n t s", n=2, t=T)
        probT = pbuf[:, 2 * T * SEQ:].rearrange("p (n t s) -> p n t s", n=2, t=T)
        junk, pT_flat = pbuf[:, 0:2 * HALF], pbuf[:, 2 * HALF:]
        uT = junk.rearrange("p (g s) -> p g s", g=G)
        mixed = pT_flat.rearrange("p (t c) -> p t c", t=T)
        mixT = hn[:, :, :].rearrange("p t c -> p (t c)").rearrange("p (k s) -> p k s", k=KD)
        o_sb = cqkv[:, :, :].rearrange("p t c -> p (t c)")[:, 0:T * BW].rearrange(
            "p (t c) -> p t c", t=T)
        sv = sgv[:, :].rearrange("p (t c) -> p t c", t=T)
        bs_row = hn[:, 0, 0:G * P]
        ws_raw = hn[:, 1, 0:G * P].rearrange("p (g j) -> p g j", g=G)
        wsT = hn[:, 1, G * P:].rearrange("p (g j) -> p g j", g=G)
        sig = cT[:, 0:2, :]
        ang = qxT[:, 0, 0:4 * T * ROPE // 2].rearrange("p (n t r) -> p n t r", n=4, t=T)
        kr = cT[:, 2, 0:T * ROPE].rearrange("p (t o d) -> p t o d", t=T, o=1)
        gated_tmp = sgv[:, 0:2 * SEQ].rearrange("p (n s) -> p n s", n=2)
        vec_rows = sgv[0:n_vec, 0:P]
        gain_rows = cqkv[0:KD, 0, 0:P]
        silu_d = junk.rearrange("p (n s) -> p n s", n=4)
        g32_d = pT_flat[:, 0:2 * SEQ].rearrange("p (n s) -> p n s", n=2)
        gated_d = [v[:, :, 0:BD, :] for v in yT]
        silu_m = junk.rearrange("p (n s) -> p n s", n=2)
        g32_m = pT_flat.rearrange("p (n s) -> p n s", n=2)
        gated_m = [v[:, :, 0:2, :].rearrange("p n a s -> p n (a s)") for v in yT]
        hselT = [v[:, :, 2:4, :].rearrange("p n a s -> p n (a s)") for v in yT]
        hT_flat = [v[:, :, :].rearrange("p k s -> p (k s)") for v in hT]
        y_part = [v[:, 0:D] for v in hT_flat]
        sel = hT_flat[0][:, D:D + T * CAP].rearrange("p (t s) -> p t s", t=T)
        selT = hT_flat[0][:, D + T * CAP:D + 2 * T * CAP].rearrange("p (t s) -> p t s", t=T)
        router = [v[:, :, :, :].rearrange("p n k s -> p (n k s)")[:, 0:KD * P].rearrange("p (k e) -> p k e", k=KD)
                  for v in yT]
        logT = qxT[0:NE, 0, :]
        hn_part = [v[:, :, :].rearrange("p k s -> p (k s)").rearrange("p (t c) -> p t c", t=T) for v in mT]
        gf_row = mkT[:, :, :].rearrange("p k s -> p (k s)")

        at, c_of = 0, {}
        for name, n in (("mix", DEPTH * KD), ("ffn", DEPTH * KD), ("q", DEPTH * 3),
                        ("kv", DEPTH * 2), ("sg", DEPTH * G), ("gate", DEPTH * NBR * KD)):
            c_of[name] = at
            at += n
        c_of["mem"] = n_vec

        gain_in = sem("gain_in")
        vecs_in = sem("vecs_in")
        x_in = sem("x_in")
        mem_in = [sem(f"mem_in{t}") for t in range(T)]
        ws_in = sem("ws_in")
        row_in = sem("row_in")
        pos_in = sem("pos_in")
        router_in = sem("router_in")
        gf_in = sem("gf_in")
        stored = sem("stored")
        raw_in = [sem(f"raw_in{i}") for i in range(RAW)]
        hi_ready = sem("hi_ready")
        lo_ready = sem("lo_ready")
        pool_step = sem("pool_step")
        consts = sem("consts")
        dve_step = sem("dve_step")
        angles = sem("angles")
        trig = sem("trig")
        squares = sem("squares")
        hn_ready = sem("hn_ready")
        hT_hi = sem("hT_hi")
        g_hi = sem("g_hi")
        rows_hi = sem("rows_hi")
        lat_inv = sem("lat_inv")
        vn_ready = sem("vn_ready")
        yb_ready = sem("yb_ready")
        q_ready = sem("q_ready")
        k_ready = sem("k_ready")
        max_ready = sem("max_ready")
        prob_ready = sem("prob_ready")
        tanh_ready = sem("tanh_ready")
        merged = sem("merged")
        silu_ready = sem("silu_ready")
        gap_ready = sem("gap_ready")
        gap_exp = sem("gap_exp")
        mask_ready = sem("mask_ready")
        flag_ready = sem("flag_ready")
        ey_hi = sem("ey_hi")
        router_hi = sem("router_hi")
        router_lo = sem("router_lo")
        hn_hi = sem("hn_hi")
        hn_lo = sem("hn_lo")
        y_hi = sem("y_hi")
        cur_ready = sem("cur_ready")
        sel_ready = sem("sel_ready")
        y_final = sem("y_final")

        def rows(w, c0, c1, r0=0, r1=None):
            r1 = w.shape[0] if r1 is None else r1
            return w[r0:r1, c0:c1].rearrange("(k p) c -> p k c", p=P)

        pieces, nth_piece = [], {}

        turn = 0

        def piece(key, slots, *parts, split=True, slot=None):
            nonlocal turn
            n_split = sum(1 for p in pieces if p[3] is not None)
            if slot is None:
                slot = turn % slots
                turn += 1
            nth_piece[key] = len(pieces)
            pieces.append((key, slot, parts, n_split if split else None))

        for l in range(DEPTH):
            turn = 0
            wi, hk = w_in[l], D // 2

            def mixer_piece(key, *parts, **how):
                piece(key, MIX_RAW, *parts, **how)

            for n in range(2):
                mixer_piece(("mk", l, n), rows(w_mkv[l], n * W, (n + 1) * W))
            for k in range(2):
                mixer_piece(("mv", l, k), rows(w_mkv[l], BW, 2 * BW, k * hk, (k + 1) * hk))
            half_q = H * QK // 2
            mixer_piece(("uq", l, 0), rows(w_uq[l], 0, half_q), split=False, slot=RAW - 2)
            mixer_piece(("ukv", l), rows(w_uk[l], 0, H * NOPE), rows(w_uv[l], 0, BW), split=False, slot=RAW - 1)
            for name, c0, c1 in (("cq", 0, C_KV), ("ckv", C_KV, C_SG), ("sv", C_SG + SG, C_XQ)):
                for k in range(2):
                    mixer_piece((name, l, k), rows(wi, c0, c1, k * hk, (k + 1) * hk))
            for name, c0 in (("su", C_SG), ("qx", C_XQ)):
                for n in range(2):
                    mixer_piece((name, l, n), rows(wi, c0 + n * W, c0 + (n + 1) * W))
            mixer_piece(("uq", l, 1), rows(w_uq[l], half_q, 2 * half_q), split=False)
            for n in (1, 2, 0):
                for f in range(4):
                    c0 = C_GATE + n * D + f * W
                    mixer_piece(("gate", l, n, f), rows(wi, c0, c0 + W))
                    if f % 2 == 0:
                        mixer_piece(("br", l, n, f // 2), rows(w_br[l, n], f * W, (f + 2) * W))
            for n in range(2):
                for k in range(2):
                    mixer_piece(("out", l, n, k), rows(w_out[l], n * HALF, (n + 1) * HALF, k * hk, (k + 1) * hk))
            turn = 0
            if l % 2 == 0:
                j = l // 2
                for b in range(ND + 1):
                    if b < ND:
                        z = min((b + 1) * BD * P, FD)
                        for name, w in (("w1", dense_w1), ("w3", dense_w3)):
                            piece((name, l, b), RAW, rows(w[j], b * BD * P, z))
                    if b:
                        piece(("w2", l, b - 1), RAW,
                              rows(dense_w2[j], 0, D, (b - 1) * BD * P, min(b * BD * P, FD)))
        E0 = sum(1 for p in pieces if p[3] is not None)

        def e_source(kind, b, half, e, shift=0):
            if kind == "w2":
                r0 = (b * BM + half * BM // 2) * P
                src = moe_w2[0, shift:, :, :][e, r0:r0 + BM // 2 * P, :]
            else:
                w = moe_w1 if kind == "w1" else moe_w3
                src = w[0, shift:, :, :][e, half * D // 2:(half + 1) * D // 2, b * BM * P:(b + 1) * BM * P]
            return src.rearrange("(k p) c -> p k c", p=P)

        e_pieces = []
        for b in range(NM):
            e_pieces += [("w1", b, 0), ("w1", b, 1), ("w3", b, 0), ("w3", b, 1)]
            if b:
                e_pieces += [("w2", b - 1, 0), ("w2", b - 1, 1)]
        e_pieces += [("w2", NM - 1, 0), ("w2", NM - 1, 1)]
        PER_E = len(e_pieces)
        assert PER_E % RAW == 0 and PER_E % SPLIT == 0
        e_at = {key: i for i, key in enumerate(e_pieces)}
        for i in range(EARLY):
            piece(("e", i), RAW, e_source(*e_pieces[i], 0))
        e_base = [16 * sum(len(p[2]) for p in pieces if p[1] == s and p[0][0] != "e") for s in range(RAW)]

        def raw_wait(eng, n):
            s = pieces[n][1]
            eng.wait_ge(raw_in[s], 16 * sum(len(p[2]) for p in pieces[:n + 1] if p[1] == s))

        def floats(n):
            return sum(src.shape[1] * src.shape[2] for src in pieces[n][2])

        marks = {}

        def reached(eng, name, j=0):
            count, per = marks[name]
            eng.wait_ge(products, count + per * j)

        def full(eng, name, j=0):
            reached(eng, name, j)
            return banks[groups[name].bank]

        def read(eng, name, j=0):
            g = groups[name]
            eng.wait_ge(bank_free[g.bank], g.use + g.per * j)

        def free(ins, name):
            ins.then_inc(bank_free[groups[name].bank], 1)

        unit_names = [("unit", l) + s[1:] for l in range(DEPTH)
                      for s in [s for s in steps if s[0] == "unit"] + [("unit", 0, d) for d in range(KD)]]
        N_SQ, n = [T], T
        for l in range(DEPTH):
            N_SQ += [n + 2 * T, n + 7 * T, None]
            n += 7 * T
        N_SQ[-1] = n + 2 * T

        split_order = [n for n, p in enumerate(pieces) if p[3] is not None]

        def room(name, after=0):
            limit = marks[name][0] + after
            for m, n in enumerate(split_order):
                key, slot = pieces[n][:2]
                old = [("piece",) + pieces[split_order[m - SPLIT]][0]] if m >= SPLIT else []
                for q in range(n - 1, -1, -1):
                    if pieces[q][1] == slot:
                        if pieces[q][3] is None:
                            old.append(pieces[q][0])
                        break
                if slot >= MIX_RAW:
                    old.append(("o", key[1], T - 1))
                if any(marks[o][0] >= limit for o in old):
                    return m
            return len(split_order)

        def job_room(name, after=0):
            limit = marks[name][0] + after
            return sum(1 for i in range(PER_E + EARLY)
                       if i < SPLIT or marks[("e_piece",) + e_pieces[i - SPLIT]][0] < limit)

        block = ctx.enter_context(nc.Block())

        @block.gpsimd
        def _(pool):
            nc.gpsimd.memset(ident[:, :], 0.0).then_inc(pool_step, 1)
            pool.wait_ge(pool_step, 1)
            nc.gpsimd.affine_select(out=ident[:, :], in_=ident[:, :], compare_op=ALU.not_equal, fill=1.0,
                                    base=0, pattern=[[-1, P]], channel_multiplier=1).then_inc(consts, 1)
            for name, v in (("mix", g_mix), ("ffn", g_ffn), ("q", g_q), ("kv", g_kv), ("sg", g_sg)):
                n = v.shape[0] * v.shape[1] // P
                pool.dma_start(vec_rows[c_of[name]:c_of[name] + n, :],
                               v.rearrange("l (k p) -> (l k) p", p=P)).then_inc(vecs_in, 16)
            pool.dma_start(vec_rows[c_of["gate"]:n_vec, :],
                           b_gate.rearrange("l n (k p) -> (l n k) p", p=P)).then_inc(vecs_in, 16)
            pool.dma_start(pos_i[:, :], positions[0].rearrange("(t p) -> p t", p=P),
                           allow_slow_non_contiguous=True).then_inc(pos_in, 16)
            pool.dma_start(wrt[:, :, :], w_router[0].rearrange("(k p) e -> p k e", p=P)).then_inc(router_in, 16)
            for tile in (lower, ones):
                nc.gpsimd.memset(tile[:, :], 1.0).then_inc(pool_step, 1)
            for i in range(ROPE // 2):
                f = np.float32(1.0) / np.power(np.float32(10000.0), np.float32(2 * i) / np.float32(ROPE))
                nc.gpsimd.memset(inv_freq[:, i:i + 1], float(f)).then_inc(pool_step, 1)
            pool.wait_ge(pool_step, 3)
            nc.gpsimd.affine_select(out=lower[:, :], in_=lower[:, :], compare_op=ALU.is_gt, fill=0.0,
                                    base=0, pattern=[[1, P]], channel_multiplier=-1).then_inc(consts, 1)
            nc.gpsimd.iota(iota_cap[:, :], pattern=[[1, CAP]], base=0, channel_multiplier=0,
                           allow_small_or_imprecise_dtypes=True).then_inc(consts, 1)
            nc.gpsimd.iota(iota_e[:, :], pattern=[[1, NE]], base=0, channel_multiplier=0,
                           allow_small_or_imprecise_dtypes=True).then_inc(consts, 1)
            nc.gpsimd.memset(rank[:, :, :], -1.0).then_inc(consts, 1)
            nc.gpsimd.memset(comb[:, :, :], 0.0).then_inc(consts, 1)

        N_CONST = 6

        @block.tensor
        def _(pe):
            count, recording = 0, True

            def mark(ins, *names):
                nonlocal count
                count += 1
                ins.then_inc(products, 1)
                if recording:
                    for name in names:
                        marks[name] = [count, 0]

            def claim(name, j=0):
                g = groups[name]
                if g.use > 1:
                    pe.wait_ge(bank_free[g.bank], g.use - 1 + g.per * j)
                return banks[g.bank]

            def acc(bank, lhs, rhs, n):
                for k in range(n):
                    ins = nc.tensor.matmul(bank, lhs(k), rhs(k), start=(k == 0), stop=(k == n - 1))
                return ins

            def acc3(bank, lhs, rhs, chunks, start, stop, norm=None):
                for k in chunks:
                    if norm is not None and k % 2 == 0:
                        read(pe, ("nT", norm, k // 2))
                    for a, b in ((0, 0), (0, 1), (1, 0)):
                        ins = nc.tensor.matmul(bank, lhs(a, k), rhs(b, k), start=(start and k == chunks[0] and a + b == 0),
                                               stop=(stop and k == chunks[-1] and a == 1))
                return ins

            def weight(key, k):
                n = nth_piece[key]
                m = pieces[n][3]
                pe.wait_ge(lo_ready, m + 1)
                size = floats(n)
                return [w[:, m % SPLIT, 0:size].rearrange("p (k c) -> p k c", k=k) for w in (whi, wlo)]

            def raw_weight(key):
                n = nth_piece[key]
                raw_wait(pe, n)
                return raw[:, pieces[n][1], :]

            def tok(t):
                return slice(t * P, (t + 1) * P)

            pe.wait_ge(consts, 1)
            pe.wait_ge(gain_in, 16)
            b = claim("mem_gain")
            mark(nc.tensor.transpose(b[:, 0:KD], gain_rows, ident[0:KD, 0:KD]), "mem_gain")

            def transpose_rows(name, src, n):
                b = claim(name)
                for c in range(min(2, src.shape[2] // P - 2 * n)):
                    for t in range(T):
                        a = c * SEQ + t * P
                        ins = nc.tensor.transpose(b[:, a:a + P], src[:, t, tok(2 * n + c)], ident[:, :])
                mark(ins, name)

            def transpose_norm(i):
                for t in range(T):
                    pe.wait_ge(hn_ready, T * i + t + 1)
                    for n in range(4):
                        name = ("nT", i, n)
                        b = banks[groups[name].bank] if t else claim(name)
                        for c in range(2):
                            a = c * SEQ + t * P
                            ins = nc.tensor.transpose(b[:, a:a + P], hn[:, t, tok(2 * n + c)], ident[:, :])
                        if t == T - 1:
                            mark(ins, name)

            for l in range(DEPTH):
                def token_major(name, src, norm=None):
                    bs = None
                    for k in range(2):
                        w = weight((name, l, k), KD // 2)
                        width = w[0].shape[2]
                        for t in range(T):
                            if k == 0:
                                claim((name, l, t))
                            ins = acc3(banks[groups[name, l, t].bank][:, 0:width],
                                       lambda a, q: src[a][:, q, tok(t)], lambda a, q: w[a][:, q - 4 * k, :],
                                       range(4 * k, 4 * k + 4), k == 0, k == 1, None if t else norm)
                            if k == 1 and t == 0:
                                mark(ins, (name, l, 0))
                        if k == 0:
                            mark(ins, ("piece", name, l, 0))
                        else:
                            mark(ins, (name, l, 1), ("piece", name, l, 1))

                def transposed(name, src, norm=None):
                    for n in range(2):
                        w = weight((name, l, n), KD)
                        b = claim((name, l, n))
                        for c in range(2):
                            ins = acc3(b[:, c * SEQ:(c + 1) * SEQ], lambda a, k: w[a][:, k, tok(c)],
                                       lambda a, k: src[a][:, k, :], range(KD), True, True,
                                       None if n or c else norm)
                        mark(ins, (name, l, n), ("piece", name, l, n))

                if l == 0:
                    transpose_norm(0)
                transposed("mk", mT, 3 * l)
                if l == 0:
                    pe.wait_ge(vecs_in, 16 * 6)
                    b = claim("vecs")
                    mark(nc.tensor.transpose(b[:, 0:n_vec], vec_rows, ident[0:n_vec, 0:n_vec]), "vecs")
                token_major("mv", mT)
                transpose_norm(3 * l + 1)
                token_major("cq", hT, 3 * l + 1)
                token_major("ckv", hT)
                token_major("sv", hT)
                transposed("su", hT)
                transposed("qx", hT)
                pe.wait_ge(ws_in, 16 * (l + 1))
                b = claim(("wsT", l))
                for g in range(G):
                    ins = nc.tensor.transpose(b[:, tok(g)], ws_raw[:, g, :], ident[:, :])
                mark(ins, ("wsT", l))
                for t in range(T):
                    read(pe, ("ckv", l, t))
                    read(pe, ("cq", l, t))
                for n in range(3):
                    transpose_rows(("cT", l, n), cqkv[:, :, 0:QR + KVR], n)
                pe.wait_ge(vn_ready, T * (l + 1))
                read(pe, ("wsT", l))
                for t in range(T):
                    b = claim(("sg", l, t))
                    for g in range(G):
                        ins = nc.tensor.matmul(b[:, tok(g)], sv[:, t, tok(g)], wsT[:, g, :], start=True, stop=True)
                    mark(ins, ("sg", l, t))

                for n in range(3):
                    read(pe, ("cT", l, n))
                for n in range(2):
                    w = raw_weight(("uq", l, n))[:, 0:3 * 384].rearrange("p (k c) -> p k c", k=3)
                    for t in range(T):
                        b = claim(("q", l, t, n))
                        ins = acc(b[:, 0:384], lambda k: cT[:, k, tok(t)], lambda k: w[:, k, :], 3)
                        mark(ins, ("q", l, t, n), *([("uq", l, n)] if t else []))
                def unit(n, d):
                    name = ("unit", l, n, d)
                    b = claim(name)

                    def gate():
                        w = weight(("gate", l, n, d // 2), KD)
                        return acc3(b[:, 0:SEQ], lambda a, k: w[a][:, k, tok(d % 2)], lambda a, k: hT[a][:, k, :],
                                    range(KD), True, True)

                    def project():
                        w = weight(("br", l, n, d // 4), KB)
                        return acc3(b[:, SEQ:2 * SEQ], lambda a, k: w[a][:, k, tok(d % 4)],
                                    lambda a, k: yT[a][:, n // 2, k, :], range(KB), True, True)

                    if d % 4 == 3:
                        mark(project(), ("piece", "br", l, n, d // 4))
                        mark(gate(), name, ("piece", "gate", l, n, d // 2))
                        return
                    ins = gate()
                    if d % 2:
                        mark(ins, ("piece", "gate", l, n, d // 2))
                    if d == 0:
                        if n == 1:
                            pe.wait_ge(yb_ready, l + 1)
                        for i in range(XH if n == 2 else 0):
                            read(pe, ("mo", l, i))
                        for i in range(2 if n == 0 else 0):
                            read(pe, ("oT", l, i))
                    mark(project(), name)

                for step in steps:
                    kind = step[0]
                    name = (kind, l) + step[1:]
                    if kind == "unit":
                        unit(*step[1:])
                        continue
                    h = step[1]
                    nth = l * (XH + H) + h + (0 if kind[0] == "m" else XH)
                    if kind == "ms":
                        if h == 0:
                            for n in range(2):
                                read(pe, ("qx", l, n))
                                read(pe, ("mk", l, n))
                        b = claim(name)
                        for t in range(T):
                            ins = nc.tensor.matmul(b[:, t * SEQ:(t + 1) * SEQ], qxT[:, h, tok(t)], mkT[:, h, :],
                                                   start=True, stop=True)
                        mark(ins, name)
                    elif kind in ("k", "v"):
                        w = raw_weight(("ukv", l)).rearrange("p (i k c) -> p i k c", i=2, k=2)[:, int(kind == "v")]
                        t = step[1]
                        b = claim(name)
                        ins = acc(b[:, :], lambda k: cT[:, 3 + k, tok(t)], lambda k: w[:, k, :], 2)
                        mark(ins, name, *([("ukv", l)] if kind == "v" and t else []))
                    elif kind in ("mpT", "apT"):
                        if kind == "mpT":
                            pe.wait_ge(prob_ready, l * XH + h + 1)
                        else:
                            read(pe, ("as", l, h))
                        b = claim(name)
                        for kt in range(T):
                            for t in range(T):
                                a = kt * SEQ + t * P
                                ins = nc.tensor.transpose(b[:, a:a + P], prob[:, nth % 2, t, tok(kt)], ident[:, :])
                        mark(ins, name)
                    elif kind == "mo":
                        read(pe, ("mpT", l, h))
                        if h == 0:
                            for t in range(T):
                                read(pe, ("mv", l, t))
                        b = claim(name)
                        mark(acc(b[:, 0:SEQ], lambda k: mv[:, k, tok(h)], lambda k: probT[:, nth % 2, k, :], T), name)
                    elif kind in ("qT", "kT"):
                        t, n = step[1:]
                        if n == 0:
                            if kind == "qT":
                                pe.wait_ge(q_ready, T * l + t + 1)
                            else:
                                pe.wait_ge(k_ready, l + 1)
                        src = q_sb if kind == "qT" else k_sb
                        b = claim(name)
                        for i in range(4):
                            ins = nc.tensor.transpose(b[0:QK, tok(i)], src[:, t, 4 * n + i, :], ident[:, :])
                        mark(ins, name)
                    elif kind == "as":
                        if h == 0:
                            for t in range(T):
                                for n in range(2):
                                    read(pe, ("qT", l, t, n))
                                    read(pe, ("kT", l, t, n))
                        b = claim(name)
                        for t in range(T):
                            ins = nc.tensor.matmul(b[:, t * SEQ:(t + 1) * SEQ], qT[0:QK, h, tok(t)], kT[0:QK, h, :],
                                                   start=True, stop=True)
                        mark(ins, name)
                    else:
                        read(pe, ("apT", l, h))
                        w = BW // H
                        for t in range(T):
                            if h == 0:
                                read(pe, ("v", l, 0))
                                read(pe, ("v", l, 1))
                                claim(("o", l, t))
                            ins = acc(banks[4 + t][:, h * w:(h + 1) * w], lambda k: probT[:, nth % 2, k, tok(t)],
                                      lambda k: v_sb[:, k, h * w:(h + 1) * w], T)
                            if h == H - 1:
                                mark(ins, ("o", l, t))
                for t in range(T):
                    read(pe, ("o", l, t))
                for n in range(2):
                    transpose_rows(("oT", l, n), o_sb, n)
                for d in range(KD):
                    unit(0, d)
                for n in range(2):
                    for k in range(2):
                        if n == 0:
                            pe.wait_ge(merged, KD * l + KD // 2 * (k + 1))
                        w = weight(("out", l, n, k), KD // 2)
                        for t in range(T):
                            name = ("out", l, t, n)
                            if k == 0:
                                claim(name)
                            ins = acc3(banks[groups[name].bank][:, :], lambda a, q: mT[a][:, q, tok(t)],
                                       lambda a, q: w[a][:, q - 4 * k, :], range(4 * k, 4 * k + 4), k == 0, k == 1)
                            if k:
                                mark(ins, name, *([("piece", "out", l, n, k)] if t else []))
                        if k == 0:
                            mark(ins, ("piece", "out", l, n, k))
                transpose_norm(3 * l + 2)
                if l % 2 == 0:
                    def up(b_):
                        w1 = weight(("w1", l, b_), KD)
                        last = min(BD, FCD - b_ * BD) - 1
                        for cc in range(last + 1):
                            name = ("up", l, b_ * BD + cc)
                            b = claim(name)
                            ins = acc3(b[:, 0:SEQ], lambda a, k: w1[a][:, k, tok(cc)], lambda a, k: hT[a][:, k, :],
                                       range(KD), True, True, None if b_ or cc else 3 * l + 2)
                            if cc == last:
                                mark(ins, ("piece", "w1", l, b_))
                            w3 = weight(("w3", l, b_), KD)
                            ins = acc3(b[:, SEQ:2 * SEQ], lambda a, k: w3[a][:, k, tok(cc)],
                                       lambda a, k: hT[a][:, k, :], range(KD), True, True)
                            mark(ins, name, *([("piece", "w3", l, b_)] if cc == last else []))

                    def down(b_):
                        m = min(BD, FCD - b_ * BD)
                        w2 = weight(("w2", l, b_), m)
                        read(pe, ("up", l, b_ * BD + m - 1))
                        for t in range(T):
                            for n in range(2):
                                name = ("y", l, 2 * t + n)
                                if b_ == 0:
                                    claim(name)
                                ins = acc3(banks[4 + 2 * t + n][:, :], lambda a, c: gated_d[a][:, b_ % 2, c, tok(t)],
                                           lambda a, c: w2[a][:, c, n * HALF:(n + 1) * HALF], range(m),
                                           b_ == 0, b_ == ND - 1)
                                if b_ == ND - 1:
                                    mark(ins, name, *([("piece", "w2", l, b_)] if t and n else []))
                        if b_ < ND - 1:
                            mark(ins, ("piece", "w2", l, b_))

                    for b_ in range(ND + 1):
                        if b_ * BD == MEM_AT:
                            transpose_norm(3 * l + 3)
                        if b_ < ND:
                            up(b_)
                        if b_:
                            down(b_ - 1)

            l = DEPTH - 1
            pe.wait_ge(router_lo, 1)
            b = claim(("logT", l))
            mark(acc3(b[:, 0:SEQ], lambda a, k: router[a][:, k, :], lambda a, k: hT[a][:, k, :], range(KD),
                      True, True, 3 * l + 2), ("logT", l))
            read(pe, ("logT", l))
            b = claim(("logits", l))
            for t in range(T):
                ins = nc.tensor.transpose(b[:, t * NE:(t + 1) * NE], logT[:, tok(t)], ident[0:NE, 0:NE])
            mark(ins, ("logits", l))
            pe.wait_ge(consts, N_CONST)
            pe.wait_ge(mask_ready, 1)
            b = claim(("rank", l))
            nc.tensor.matmul(b[:, 0:NE], lower[:, :], mask[:, 0, :], start=True, stop=True)
            nc.tensor.matmul(b[:, NE:2 * NE], ones[:, :], mask[:, 0, :], start=True, stop=False)
            nc.tensor.matmul(b[:, NE:2 * NE], lower[:, :], mask[:, 1, :], start=False, stop=True)
            nc.tensor.matmul(b[:, 2 * NE:3 * NE], ones[:, :], mask[:, 0, :], start=True, stop=False)
            ins = nc.tensor.matmul(b[:, 2 * NE:3 * NE], ones[:, :], mask[:, 1, :], start=False, stop=True)
            mark(ins, ("rank", l))

            def gather(name, n, j):
                b = claim(name, j)
                for c in range(4):
                    for t in range(T):
                        for a in range(2):
                            ins = nc.tensor.matmul(b[:, c * CAP:(c + 1) * CAP], hn_part[a][:, t, tok(4 * n + c)],
                                                   sel[:, t, :], start=(t + a == 0), stop=(t + a == T))
                mark(ins, name)

            pe.wait_ge(hn_lo, T)
            pe.wait_ge(sel_ready, 1)
            for n in range(2):
                gather(("gather0", l, n), n, 0)

            def job(j):
                def e_weight(kind, b_, half):
                    i = e_at[kind, b_, half]
                    pe.wait_ge(lo_ready, E0 + i + 1 + PER_E * j)
                    return [w[:, (E0 + i) % SPLIT, :].rearrange("p (k c) -> p k c", k=2 if kind == "w2" else 4)
                            for w in (whi, wlo)]

                def up(kind, name, b_):
                    b = claim((name, b_), j)
                    for half in range(2):
                        w = e_weight(kind, b_, half)
                        if name == "e1" and b_ == 0:
                            read(pe, ("gather", half), j - 1)
                        ins = acc3(b[:, :], lambda a, k: hselT[a][:, half, tok(k)], lambda a, k: w[a][:, k, :],
                                   range(4), half == 0, half == 1)
                        mark(ins, ("e_piece", kind, b_, half), *([(name, b_)] if half else []))

                def hidden_T(b_):
                    read(pe, ("e3", b_), j)
                    b = claim(("eT", b_), j)
                    for c in range(BM):
                        ins = nc.tensor.transpose(b[:, tok(c)], g32_m[:, b_ % 2, tok(c)], ident[:, :])
                    mark(ins, ("eT", b_))

                def down(b_):
                    read(pe, ("eT", b_), j)
                    for half in range(2):
                        w = e_weight("w2", b_, half)
                        for n in range(2):
                            if b_ == 0 and half == 0:
                                claim(("ey", n), j)
                            last = b_ == NM - 1 and half == 1
                            ins = acc3(banks[4 + n][:, :], lambda a, c: gated_m[a][:, b_ % 2, tok(2 * half + c)],
                                       lambda a, c: w[a][:, c, n * HALF:(n + 1) * HALF], range(2),
                                       b_ == 0 and half == 0, last)
                            if last and n == 0:
                                mark(ins, ("ey", 0))
                        mark(ins, ("e_piece", "w2", b_, half), *([("ey", 1)] if last else []))

                for b_ in range(NM):
                    up("w1", "e1", b_)
                    if b_:
                        hidden_T(b_ - 1)
                    up("w3", "e3", b_)
                    if b_ == 0:
                        b = claim(("selT", 0), j)
                        for t in range(T):
                            ins = nc.tensor.transpose(b[:, tok(t)], sel[:, t, :].bitcast(F32), ident[:, :])
                        mark(ins, ("selT", 0))
                    if b_:
                        down(b_ - 1)
                pe.wait_ge(sel_ready, j + 2)
                gather(("gather", 0), 0, j)
                hidden_T(NM - 1)
                gather(("gather", 1), 1, j)
                down(NM - 1)
                read(pe, ("selT", 0), j)
                for n in range(2):
                    read(pe, ("ey", n), j)
                    for t in range(T):
                        b = claim(("scatter", 2 * n + t), j)
                        for a in range(2):
                            ins = nc.tensor.matmul(b[:, :], selT[:, t, :], y_part[a][:, n * HALF:(n + 1) * HALF],
                                                   start=(a == 0), stop=(a == 1))
                        mark(ins, ("scatter", 2 * n + t))

            before, names = count, set(marks)
            with pe.Fori(0, NE) as j:
                job(j)
            recording = False
            for name in set(marks) - names:
                marks[name][1] = count - before
            pe.wait_ge(flag_ready, 1)
            overflow = pe.value_load(more[0:1, 0:1], min_val=0, max_val=1)
            with pe.If(overflow > 0):
                with pe.Fori(NE, JOBS) as j:
                    job(j)

        @block.sync
        def _(sp):
            last_in = {}

            def wait_slot(slot, scratch):
                if slot in last_in:
                    old = pieces[last_in[slot]]
                    if old[3] is None:
                        reached(sp, old[0])
                    else:
                        sp.wait_ge(lo_ready, old[3] + 1)
                if scratch is not None:
                    read(sp, ("o", scratch, T - 1))

            for t in range(T):
                sp.dma_start(hn[:, t, :], mem[0, t * P:(t + 1) * P, :]).then_inc(mem_in[t], 16)
            for n, (key, slot, parts, n_split) in enumerate(pieces):
                if n == MIX_RAW:
                    sp.dma_start(x_sb[:, :, :], x[0].rearrange("(t p) c -> p t c", p=P)).then_inc(x_in, 16)
                wait_slot(slot, key[1] if slot >= MIX_RAW and n_split is not None else None)
                offset = 0
                for src in parts:
                    chunks, width = src.shape[1], src.shape[2]
                    dst = raw[:, slot, offset:offset + chunks * width].rearrange("p (k c) -> p k c", k=chunks)
                    sp.dma_start(dst, src).then_inc(raw_in[slot], 16)
                    offset += chunks * width
                last_in[slot] = n

            def job_loads(j, e, last):
                for i in range(EARLY, PER_E + EARLY):
                    slot = i % RAW
                    sp.wait_ge(lo_ready, E0 + i - RAW + 1 + PER_E * j)
                    if i < PER_E:
                        src = e_source(*e_pieces[i], e)
                    else:
                        src = e_source(*e_pieces[i - PER_E], 0 if last else e, 0 if last else 1)
                    dst = raw[:, slot, :].rearrange("p (k c) -> p k c", k=src.shape[1])
                    sp.dma_start(dst, src).then_inc(raw_in[slot], 16)

            with sp.Fori(0, NE - 1) as e:
                job_loads(e, e, False)
            job_loads(NE - 1, NE - 1, True)
            read(sp, ("nT", 3 * DEPTH - 1, 3))
            sp.dma_start(gf_row, g_final.partition_broadcast(P)).then_inc(gf_in, 16)
            sp.wait_ge(flag_ready, 1)
            overflow = sp.value_load(more[0:1, 0:1], min_val=0, max_val=1)
            with sp.If(overflow > 0):
                with sp.Fori(0, NE - 1) as e:
                    job_loads(e + NE, e, False)
                job_loads(JOBS - 1, NE - 1, True)
            for t in range(T):
                sp.wait_ge(y_final, t + 1)
                sp.dma_start(out[0, t * P:(t + 1) * P, :], hn[:, t, :]).then_inc(stored, 16)
            sp.wait_ge(stored, 16 * T)

        @block.scalar
        def _(act):
            act.dma_start(gain_rows, g_mem.rearrange("(k p) -> k p", p=P)).then_inc(gain_in, 16)

            n_sq = 0
            n_hi = 0

            def hi_parts(m_end):
                nonlocal n_hi
                for m in range(n_hi, m_end):
                    n = split_order[m]
                    raw_wait(act, n)
                    if m >= SPLIT:
                        reached(act, ("piece",) + pieces[split_order[m - SPLIT]][0])
                    nc.scalar.activation(whi[:, m % SPLIT, 0:floats(n)], raw[:, pieces[n][1], 0:floats(n)],
                                         ACT.Copy).then_inc(hi_ready, 1)
                n_hi = max(n_hi, m_end)

            def own_squares():
                if n_sq:
                    act.wait_ge(squares, n_sq)

            def square(src, width, col):
                nonlocal n_sq
                own_squares()
                nc.scalar.activation(junk[:, 0:width], src, ACT.Square,
                                     accum_out=sumsq[:, col:col + 1]).then_inc(squares, 1)
                n_sq += 1

            def half_square(t, n):
                square(x_sb[:, t, n * HALF:(n + 1) * HALF], HALF, 6 + 2 * t + n)

            def norm_hi(i, dst, gain):
                for n in range(4):
                    b = full(act, ("nT", i, n))
                    for c in range(2):
                        k = 2 * n + c
                        ins = nc.scalar.activation(dst[0][:, k, :], b[:, c * SEQ:(c + 1) * SEQ], ACT.Copy,
                                                   scale=cols[:, gain + k:gain + k + 1])
                    ins.then_inc(hT_hi, 1)

            n_unit = 0
            for l in range(DEPTH):
                if l == 0:
                    for t in range(T):
                        act.wait_ge(mem_in[t], 16)
                        square(hn[:, t, :], D, 10 + t)
                    read(act, "mem_gain")
                    hi_parts(1)
                    norm_hi(0, mT, c_of["mem"])
                    hi_parts(SPLIT)
                    act.wait_ge(x_in, 16)
                for n in range(2):
                    for t in range(T):
                        if l:
                            read(act, ("y", l - 1, 2 * t + n))
                        half_square(t, n)
                if l == 0:
                    act.wait_ge(angles, 1)
                    nc.scalar.activation(sin_t[:, :, :], ang[:, 2, :, :], ACT.Sin).then_inc(trig, 1)
                    nc.scalar.activation(cos_t[:, :, :], ang[:, 3, :, :], ACT.Sin).then_inc(trig, 1)
                for n in range(2):
                    hi_parts(room(("mk", l, n)))
                    b = full(act, ("mk", l, n))
                    free(nc.scalar.activation(mkT[:, 2 * n:2 * n + 2, :].rearrange("p h s -> p (h s)"), b[:, :],
                                              ACT.Copy), ("mk", l, n))
                hi_parts(room(("mv", l, 1)))
                if l == 0:
                    read(act, "vecs")
                norm_hi(3 * l + 1, hT, c_of["mix"] + l * KD)
                hi_parts(room(("mv", l, 1), 1))
                act.dma_start(ws_raw, w_s[l].rearrange("g i j -> i g j")).then_inc(ws_in, 16)
                act.dma_start(bs_row, b_s[l].rearrange("g i -> (g i)").partition_broadcast(P)).then_inc(row_in, 16)
                for t in range(T):
                    hi_parts(room(("cq", l, t)))
                    b = full(act, ("cq", l, t))
                    square(b[:, 0:QR], QR, t)
                    free(nc.scalar.activation(cqkv[:, t, 0:QR], b[:, 0:QR], ACT.Copy), ("cq", l, t))
                for t in range(T):
                    hi_parts(room(("ckv", l, t)))
                    b = full(act, ("ckv", l, t))
                    square(b[:, 0:KVR], KVR, 2 + t)
                    free(nc.scalar.activation(cqkv[:, t, QR:], b[:, 0:KVR + ROPE], ACT.Copy), ("ckv", l, t))
                for t in range(T):
                    hi_parts(room(("sv", l, t)))
                    b = full(act, ("sv", l, t))
                    free(nc.scalar.activation(sv[:, t, :], b[:, :], ACT.Gelu_apprx_tanh), ("sv", l, t))
                for t in range(T):
                    read(act, ("sv", l, t))
                    square(sv[:, t, :], SG, 4 + t)
                own_squares()
                for n in range(2):
                    hi_parts(room(("su", l, n)))
                    b = full(act, ("su", l, n))
                    free(nc.scalar.activation(uT[:, 2 * n:2 * n + 2, :].rearrange("p h s -> p (h s)"), b[:, :],
                                              ACT.Gelu_apprx_tanh), ("su", l, n))
                for n in range(2):
                    hi_parts(room(("qx", l, n)))
                hi_parts(room(("wsT", l)))
                b = full(act, ("wsT", l))
                free(nc.scalar.activation(hn[:, 1, G * P:], b[:, :], ACT.Copy), ("wsT", l))
                act.wait_ge(lat_inv, l + 1)
                for t in range(T):
                    for n in range(2):
                        hi_parts(room(("q", l, t, n)))
                        b = full(act, ("q", l, t, n))
                        free(nc.scalar.activation(q_sb[:, t, 4 * n:4 * n + 4, :].rearrange("p h d -> p (h d)"),
                                                  b[:, 0:4 * QK], ACT.Copy, scale=rin[:, t:t + 1]), ("q", l, t, n))
                def unit_tanh(n, d):
                    nonlocal n_unit
                    u = n_unit
                    n_unit += 1
                    if u >= 2:
                        read(act, unit_names[u - 2])
                    b = full(act, ("unit", l, n, d))
                    c = (l * NBR + n) * KD + d
                    nc.scalar.activation(sig[:, u % 2, :], b[:, 0:SEQ], ACT.Tanh, scale=0.5,
                                         bias=half_gate[:, c:c + 1]).then_inc(tanh_ready, 1)

                own_squares()
                for step in steps:
                    kind = step[0]
                    name = (kind, l) + step[1:]
                    if kind not in ("O", "ms", "as", "v"):
                        hi_parts(room(name))
                    if kind in ("ms", "as"):
                        h = step[1]
                        nth = l * (XH + H) + h + (XH if kind == "as" else 0)
                        act.wait_ge(max_ready, nth + 1)
                        b = banks[groups[name].bank]
                        for t in range(T):
                            total = rsum[:, nth % 2, t:t + 1] if kind == "ms" else asum[:, t, h:h + 1]
                            ins = nc.scalar.activation(prob[:, nth % 2, t, :], b[:, t * SEQ:(t + 1) * SEQ], ACT.Exp,
                                                       scale=XS if kind == "ms" else QS,
                                                       bias=nmax[:, nth % 2, t:t + 1], accum_out=total)
                        free(ins, name)
                    elif kind in ("mpT", "apT"):
                        h = step[1]
                        nth = l * (XH + H) + h + (XH if kind == "apT" else 0)
                        b = full(act, name)
                        free(nc.scalar.activation(probT[:, nth % 2, :, :].rearrange("p k s -> p (k s)"), b[:, :],
                                                  ACT.Copy), name)
                    elif kind == "k":
                        t = step[1]
                        b = full(act, name)
                        free(nc.scalar.activation(k_sb[:, t, :, 0:NOPE], b[:, :].rearrange("p (h d) -> p h d", h=H),
                                                  ACT.Copy, scale=rin[:, 2 + t:3 + t]), name)
                    elif kind == "mo":
                        b = full(act, name)
                        nc.scalar.activation(yT[0][:, 1, step[1], :], b[:, 0:SEQ], ACT.Copy).then_inc(y_hi, 1)
                    elif kind == "kT":
                        t, n = step[1:]
                        b = full(act, name)
                        free(nc.scalar.activation(kT[0:QK, 4 * n:4 * n + 4, t * P:(t + 1) * P],
                                                  b[0:QK, :].rearrange("p (h s) -> p h s", h=4), ACT.Copy), name)
                    elif kind == "unit":
                        unit_tanh(*step[1:])
                for n in range(2):
                    b = full(act, ("oT", l, n))
                    nc.scalar.activation(yT[0][:, 0, 2 * n:2 * n + 2, :].rearrange("p h s -> p (h s)"), b[:, :],
                                         ACT.Copy).then_inc(y_hi, 1)
                for d in range(KD):
                    hi_parts(room(("unit", l, 0, d)))
                    unit_tanh(0, d)
                own_squares()
                for n in range(2):
                    for t in range(T):
                        if n * t == 0:
                            hi_parts(room(("out", l, t, n)))
                        read(act, ("out", l, t, n))
                        half_square(t, n)
                    if n == 0:
                        hi_parts(room(("out", l, 1, 0), 1))
                if l == DEPTH - 1:
                    act.wait_ge(router_in, 16)
                    nc.scalar.activation(router[0][:, :, 0:NE], wrt[:, :, :], ACT.Copy).then_inc(router_hi, 1)
                hi_parts(room(("out", l, 1, 1), 1))
                norm_hi(3 * l + 2, hT, c_of["ffn"] + l * KD)
                own_squares()
                if l % 2 == 0:
                    for t in range(T):
                        act.dma_start(hn[:, t, :], mem[0, t * P:(t + 1) * P, :]).then_inc(mem_in[t], 16)
                    for c in range(FCD):
                        if c == MEM_AT:
                            hi_parts(room(("up", l, c - 1), 1))
                            norm_hi(3 * l + 3, mT, c_of["mem"])
                        hi_parts(room(("up", l, c)))
                        b = full(act, ("up", l, c))
                        nc.scalar.activation(silu_d[:, c % 4, :], b[:, 0:SEQ], ACT.Silu).then_inc(silu_ready, 1)
                    hi_parts(room(("y", l, 0)))

            for t in range(T):
                nc.scalar.activation(hn_part[0][:, t, :], hn[:, t, :], ACT.Copy).then_inc(hn_hi, 1)
            act.wait_ge(gap_ready, 1)
            nc.scalar.activation(gap[:, 1, :], gap[:, 0, :], ACT.Exp).then_inc(gap_exp, 1)
            gain = c_of["ffn"] + (DEPTH - 1) * KD

            def rows_T(name, n, j):
                b = full(act, name, j)
                for c in range(4):
                    ins = nc.scalar.activation(hselT[0][:, n, c * CAP:(c + 1) * CAP], b[:, c * CAP:(c + 1) * CAP],
                                               ACT.Copy, scale=cols[:, gain + 4 * n + c:gain + 4 * n + c + 1])
                ins.then_inc(rows_hi, 1)

            for n in range(2):
                rows_T(("gather0", DEPTH - 1, n), n, 0)

            def expert(j):
                n_hi = EARLY

                def hi_parts(i_end):
                    nonlocal n_hi
                    for i in range(n_hi, i_end):
                        act.wait_ge(raw_in[i % RAW], 16 * (PER_E // RAW) * j + (e_base[i % RAW] + 16 * (i // RAW + 1)))
                        reached(act, ("e_piece",) + e_pieces[i - SPLIT], j if i >= SPLIT else j - 1)
                        nc.scalar.activation(whi[:, (E0 + i) % SPLIT, :], raw[:, i % RAW, :],
                                             ACT.Copy).then_inc(hi_ready, 1)
                    n_hi = max(n_hi, i_end)

                def hidden_hi(b_):
                    hi_parts(job_room(("eT", b_)))
                    b = full(act, ("eT", b_), j)
                    nc.scalar.activation(gated_m[0][:, b_ % 2, :], b[:, :], ACT.Copy).then_inc(g_hi, 1)

                for b_ in range(NM):
                    hi_parts(job_room(("e1", b_)))
                    b = full(act, ("e1", b_), j)
                    if b_ >= 2:
                        read(act, ("e3", b_ - 2), j)
                    else:
                        read(act, ("e3", NM - 1 - b_), j - 1)
                    free(nc.scalar.activation(silu_m[:, b_ % 2, :], b[:, :], ACT.Silu), ("e1", b_))
                    if b_:
                        hidden_hi(b_ - 1)
                    else:
                        hi_parts(job_room(("selT", 0)))
                        b = full(act, ("selT", 0), j)
                        free(nc.scalar.activation(selT.rearrange("p t s -> p (t s)"), b[:, 0:T * P],
                                                  ACT.Copy), ("selT", 0))
                hidden_hi(NM - 1)
                for n in range(2):
                    rows_T(("gather", n), n, j)
                hi_parts(job_room(("ey", 0)))
                for n in range(2):
                    b = full(act, ("ey", n), j)
                    nc.scalar.activation(y_part[0][:, n * HALF:(n + 1) * HALF], b[:, :], ACT.Copy).then_inc(ey_hi, 1)
                hi_parts(PER_E + EARLY)

            with act.Fori(0, NE) as j:
                expert(j)
            act.wait_ge(flag_ready, 1)
            overflow = act.value_load(more[0:1, 0:1], min_val=0, max_val=1)
            with act.If(overflow > 0):
                with act.Fori(NE, JOBS) as j:
                    expert(j)
            for n in range(4):
                read(act, ("scatter", n), overflow * (JOBS - NE) + (NE - 1))
                half_square(n % 2, n // 2)

        @block.vector
        def _(dve):
            n_step = 0

            def link(ins):
                nonlocal n_step
                n_step += 1
                ins.then_inc(dve_step, 1)
                dve.wait_ge(dve_step, n_step)

            V = nc.vector

            def inv_sqrt(a, z):
                v, w, y = nr[:, 0, a:z], nr[:, 1, a:z], rin[:, a:z]
                link(V.tensor_scalar(y.bitcast(I32), v.bitcast(I32), -0.5, 1597463007.0, ALU.mult, ALU.add))
                for i in range(3):
                    link(V.scalar_tensor_tensor(out=w, in0=y, scalar=-0.5, in1=y, op0=ALU.mult, op1=ALU.mult))
                    link(V.tensor_tensor(w, w, v, ALU.mult))
                    link(V.scalar_tensor_tensor(out=y, in0=w, scalar=1.5, in1=y, op0=ALU.add, op1=ALU.mult))

            def means(a, z, src, width):
                link(V.tensor_scalar(nr[:, 0, a:z], src, 1.0 / width, EPS, ALU.mult, ALU.add))

            def row_scales(i):
                dve.wait_ge(squares, N_SQ[i])
                halves = sumsq[:, 6:10].rearrange("p (t n) -> p t n", t=T)
                link(V.tensor_tensor(nr[:, 0, 6:8], halves[:, :, 0], halves[:, :, 1], ALU.add))
                means(6, 8, nr[:, 0, 6:8], D)
                inv_sqrt(6, 8)

            n_lo = 0

            def lo_parts(m_end):
                nonlocal n_lo
                for m in range(n_lo, m_end):
                    n = split_order[m]
                    size = floats(n)
                    dve.wait_ge(hi_ready, m + 1)
                    V.tensor_tensor(wlo[:, m % SPLIT, 0:size], raw[:, pieces[n][1], 0:size],
                                    whi[:, m % SPLIT, 0:size].bitcast(F32), ALU.subtract).then_inc(lo_ready, 1)
                n_lo = max(n_lo, m_end)

            def normalise(i):
                row_scales(i)
                for t in range(T):
                    V.tensor_scalar(hn[:, t, :], x_sb[:, t, :], rin[:, 6 + t:7 + t], None,
                                    ALU.mult).then_inc(hn_ready, 1)

            def normalise_memory(loads):
                for t in range(T):
                    dve.wait_ge(mem_in[t], 16 * loads)
                    V.tensor_scalar(hn[:, t, :], hn[:, t, :], rin[:, 8 + t:9 + t], None, ALU.mult).then_inc(hn_ready, 1)

            def norm_lo(i, dst, gain):
                for n in range(4):
                    b = full(dve, ("nT", i, n))
                    dve.wait_ge(hT_hi, 4 * i + n + 1)
                    for c in range(2):
                        k = 2 * n + c
                        ins = V.scalar_tensor_tensor(out=dst[1][:, k, :], in0=b[:, c * SEQ:(c + 1) * SEQ],
                                                     scalar=cols[:, gain + k:gain + k + 1],
                                                     in1=dst[0][:, k, :].bitcast(F32), op0=ALU.mult, op1=ALU.subtract)
                    free(ins, ("nT", i, n))

            b = full(dve, "mem_gain")
            free(V.tensor_copy(cols[:, n_vec:], b[:, 0:KD]), "mem_gain")
            read(dve, "mem_gain")
            dve.wait_ge(squares, N_SQ[0])
            means(8, 10, sumsq[:, 10:12], D)
            inv_sqrt(8, 10)
            normalise_memory(1)
            lo_parts(1)
            norm_lo(0, mT, c_of["mem"])
            lo_parts(SPLIT)
            dve.wait_ge(pos_in, 16)
            dve.wait_ge(pool_step, 3 + ROPE // 2)
            link(V.tensor_copy(pos_f[:, :], pos_i[:, :]))
            for t in range(T):
                link(V.tensor_scalar(ang[:, 0, t, :], inv_freq[:, :], pos_f[:, t:t + 1], None, ALU.mult))
            MAGIC = 12582912.0
            C1 = 6.28125
            C2 = 0.00193500518798828125
            C3 = TWO_PI - C1 - C2
            for out_, shift in ((2, 0.0), (3, 0.25)):
                k = ang[:, 1, :, :]
                r = ang[:, out_, :, :]
                link(V.tensor_scalar(k, ang[:, 0, :, :], 1.0 / TWO_PI, shift, ALU.mult, ALU.add))
                link(V.tensor_scalar(k, k, MAGIC, None, ALU.add))
                link(V.tensor_scalar(k, k, -MAGIC, None, ALU.add))
                link(V.scalar_tensor_tensor(out=r, in0=k, scalar=-C1, in1=ang[:, 0, :, :], op0=ALU.mult, op1=ALU.add))
                for c in (C2, C3):
                    link(V.scalar_tensor_tensor(out=r, in0=k, scalar=-c, in1=r, op0=ALU.mult, op1=ALU.add))
                link(V.tensor_scalar(r, r, shift * TWO_PI, None, ALU.add))
                ins = V.tensor_scalar(r, r, 3.14159250, -3.14159250, ALU.min, ALU.max)
                if out_ == 2:
                    link(ins)
            ins.then_inc(angles, 1)

            units = 0
            for l in range(DEPTH):
                if l:
                    lo_parts(room(("y", l - 1, 0)))
                    for n in range(2):
                        for t in range(T):
                            b = full(dve, ("y", l - 1, 2 * t + n))
                            xs = x_sb[:, t, n * HALF:(n + 1) * HALF]
                            free(V.tensor_tensor(xs, xs, b[:, :], ALU.add), ("y", l - 1, 2 * t + n))
                lo_parts(room(("mk", l, 0)))
                dve.wait_ge(x_in, 16)
                reached(dve, ("nT", 3 * l, 3))
                normalise(3 * l + 1)
                for n in range(2):
                    lo_parts(room(("mk", l, n)))
                if l == 0:
                    b = full(dve, "vecs")
                    V.tensor_copy(cols[:, 0:n_vec], b[:, 0:n_vec])
                    free(V.tensor_scalar(half_gate[:, :], b[:, c_of["gate"]:n_vec], 0.5, None, ALU.mult), "vecs")
                    read(dve, "vecs")
                for t in range(T):
                    lo_parts(room(("mv", l, t)))
                    b = full(dve, ("mv", l, t))
                    free(V.tensor_copy(mv[:, t, :], b[:, :]), ("mv", l, t))
                norm_lo(3 * l + 1, hT, c_of["mix"] + l * KD)
                lo_parts(room(("mv", l, 1), 1))
                for name in ("cq", "ckv"):
                    lo_parts(room((name, l, 1)))
                for t in range(T):
                    read(dve, ("ckv", l, t))
                    read(dve, ("cq", l, t))
                means(0, 2, sumsq[:, 0:2], QR)
                means(2, 4, sumsq[:, 2:4], KVR)
                inv_sqrt(0, 4)
                V.tensor_copy(nr[:, 0, 0:4], rin[:, 0:4]).then_inc(lat_inv, 1)
                lo_parts(room(("sv", l, 1), 1))
                dve.wait_ge(squares, N_SQ[3 * l + 1] + 3 * T)
                means(4, 6, sumsq[:, 4:6], SG)
                inv_sqrt(4, 6)
                for t in range(T):
                    V.tensor_scalar(sv[:, t, :], sv[:, t, :], rin[:, 4 + t:5 + t], None,
                                    ALU.mult).then_inc(vn_ready, 1)
                for n in range(2):
                    lo_parts(room(("su", l, n)))
                for n in range(2):
                    lo_parts(room(("qx", l, n)))
                    b = full(dve, ("qx", l, n))
                    free(V.tensor_copy(qxT[:, 2 * n:2 * n + 2, :].rearrange("p h s -> p (h s)"), b[:, :]), ("qx", l, n))
                for n in range(3):
                    lo_parts(room(("cT", l, n)))
                    b = full(dve, ("cT", l, n))
                    for c in range(2 if n < 2 else 1):
                        k = 2 * n + c
                        g = c_of["q"] + l * 3 + k if k < 3 else c_of["kv"] + l * 2 + k - 3
                        ins = V.tensor_scalar(cT[:, k, :], b[:, c * SEQ:(c + 1) * SEQ], cols[:, g:g + 1], None, ALU.mult)
                    free(ins, ("cT", l, n))
                dve.wait_ge(row_in, 16 * (l + 1))
                for n in range(2):
                    read(dve, ("su", l, n))
                for t in range(T):
                    lo_parts(room(("sg", l, t)))
                    b = full(dve, ("sg", l, t))
                    for g in range(G):
                        c = c_of["sg"] + l * G + g
                        ins = V.scalar_tensor_tensor(out=mixed[:, t, g * P:(g + 1) * P], in0=b[:, g * P:(g + 1) * P],
                                                     scalar=cols[:, c:c + 1], in1=bs_row[:, g * P:(g + 1) * P],
                                                     op0=ALU.mult, op1=ALU.add)
                    free(ins, ("sg", l, t))
                for t in range(T):
                    read(dve, ("sg", l, t))
                    u = uT[:, :, t * P:(t + 1) * P]
                    link(V.tensor_tensor(u, u, mixed[:, t, :].rearrange("p (g i) -> p g i", g=G), ALU.mult))
                link(V.tensor_copy(yT[0][:, 0, :, :], uT))
                V.tensor_tensor(yT[1][:, 0, :, :], uT, yT[0][:, 0, :, :].bitcast(F32), ALU.subtract).then_inc(yb_ready, 1)

                def rotate(t, dst, src, heads):
                    h2 = ROPE // 2
                    tmp = sgv[:, :].rearrange("p (t n h r) -> p t n h r", t=T, n=4, h=H)[:, t, :, 0:heads, :]
                    shape = [P, heads, h2]
                    co = cos_t[:, t, :].unsqueeze(1).broadcast_to(shape)
                    si = sin_t[:, t, :].unsqueeze(1).broadcast_to(shape)
                    a, b_ = src[:, :, 0:h2], src[:, :, h2:ROPE]
                    V.tensor_tensor(tmp[:, 0], a, co, ALU.mult)
                    V.tensor_tensor(tmp[:, 1], b_, si, ALU.mult)
                    V.tensor_tensor(tmp[:, 2], a, si, ALU.mult)
                    link(V.tensor_tensor(tmp[:, 3], b_, co, ALU.mult))
                    V.tensor_tensor(dst[:, :, 0:h2], tmp[:, 0], tmp[:, 1], ALU.subtract)
                    return V.tensor_tensor(dst[:, :, h2:ROPE], tmp[:, 2], tmp[:, 3], ALU.add)

                def unit_merge(n, d):
                    nonlocal units
                    name = ("unit", l, n, d)
                    units += 1
                    dve.wait_ge(tanh_ready, units)
                    b = banks[groups[name].bank]
                    s_ = sig[:, (units - 1) % 2, :]
                    first = n == 1
                    dst = mixT[:, d, :] if first else gated_tmp[:, units % 2, :]
                    free(V.scalar_tensor_tensor(out=dst, in0=s_, scalar=1.0, in1=b[:, SEQ:2 * SEQ], op0=ALU.add,
                                                op1=ALU.mult), name)
                    if not first:
                        read(dve, name)
                        link(V.tensor_tensor(mixT[:, d, :], mixT[:, d, :], dst, ALU.add))
                    if n == 0:
                        link(V.tensor_copy(mT[0][:, d, :], mixT[:, d, :]))
                        V.tensor_tensor(mT[1][:, d, :], mixT[:, d, :], mT[0][:, d, :].bitcast(F32),
                                        ALU.subtract).then_inc(merged, 1)

                for step in steps:
                    kind = step[0]
                    name = (kind, l) + step[1:]
                    if kind not in ("O", "ms", "as", "k"):
                        lo_parts(room(name))
                    if kind in ("ms", "as"):
                        h = step[1]
                        nth = l * (XH + H) + h + (XH if kind == "as" else 0)
                        b = full(dve, name)
                        link(V.tensor_reduce(rmax[:, nth % 2, :], b[:, :].rearrange("p (t s) -> p t s", t=T), AX_X,
                                             ALU.max))
                        V.tensor_scalar(nmax[:, nth % 2, :], rmax[:, nth % 2, :], -(XS if kind == "ms" else QS), None,
                                        ALU.mult).then_inc(max_ready, 1)
                        if kind == "ms":
                            read(dve, name)
                            link(V.reciprocal(rrec[:, nth % 2, :], rsum[:, nth % 2, :]))
                            for t in range(T):
                                ins = V.tensor_scalar(prob[:, nth % 2, t, :], prob[:, nth % 2, t, :],
                                                      rrec[:, nth % 2, t:t + 1], None, ALU.mult)
                            ins.then_inc(prob_ready, 1)
                    elif kind == "v":
                        t = step[1]
                        b = full(dve, name)
                        free(V.tensor_scalar(v_sb[:, t, :], b[:, :], rin[:, 2 + t:3 + t], None, ALU.mult), name)
                    elif kind == "mo":
                        h = step[1]
                        b = full(dve, name)
                        dve.wait_ge(y_hi, l * (XH + 2) + h + 1)
                        free(V.tensor_tensor(yT[1][:, 1, h, :], b[:, 0:SEQ], yT[0][:, 1, h, :].bitcast(F32),
                                             ALU.subtract), name)
                        if h < T:
                            if l == 0:
                                dve.wait_ge(trig, 2)
                            for n in range(2):
                                read(dve, ("q", l, h, n))
                            rotate(h, q_sb[:, h, :, NOPE:QK], q_sb[:, h, :, NOPE:QK], H).then_inc(q_ready, 1)
                        elif h == T:
                            for t in range(T):
                                read(dve, ("k", l, t))
                                link(rotate(t, kr[:, t], cqkv[:, t, QR + KVR:].unsqueeze(1), 1))
                            for t in range(T):
                                ins = V.tensor_copy(k_sb[:, t, :, NOPE:QK], kr[:, t].broadcast_to([P, H, ROPE]))
                            ins.then_inc(k_ready, 1)
                    elif kind == "qT":
                        t, n = step[1:]
                        b = full(dve, name)
                        free(V.tensor_copy(qT[0:QK, 4 * n:4 * n + 4, t * P:(t + 1) * P],
                                           b[0:QK, :].rearrange("p (h s) -> p h s", h=4)), name)
                    elif kind == "unit":
                        unit_merge(*step[1:])
                    elif kind == "O" and step[1] == H - 1:
                        read(dve, ("as", l, H - 1))
                        link(V.reciprocal(arec[:, :, :], asum[:, :, :]))
                        for t in range(T):
                            b = full(dve, ("o", l, t))
                            w = BW // H
                            free(V.tensor_tensor(o_sb[:, t, :].rearrange("p (h d) -> p h d", h=H),
                                                 b[:, :].rearrange("p (h d) -> p h d", h=H),
                                                 arec[:, t, :].unsqueeze(2).broadcast_to([P, H, w]), ALU.mult), ("o", l, t))
                for n in range(2):
                    b = full(dve, ("oT", l, n))
                    dve.wait_ge(y_hi, l * (XH + 2) + XH + n + 1)
                    part = [v[:, 0, 2 * n:2 * n + 2, :].rearrange("p h s -> p (h s)") for v in yT]
                    free(V.tensor_tensor(part[1], b[:, :], part[0].bitcast(F32), ALU.subtract), ("oT", l, n))
                for d in range(KD):
                    lo_parts(room(("unit", l, 0, d)))
                    unit_merge(0, d)
                for n in range(2):
                    for t in range(T):
                        if n == 0:
                            lo_parts(room(("out", l, t, n)))
                        b = full(dve, ("out", l, t, n))
                        xs = x_sb[:, t, n * HALF:(n + 1) * HALF]
                        free(V.scalar_tensor_tensor(out=xs, in0=b[:, :], scalar=0.5, in1=xs, op0=ALU.mult,
                                                    op1=ALU.add), ("out", l, t, n))
                    if n == 0:
                        lo_parts(room(("out", l, 1, 0), 1))
                normalise(3 * l + 2)
                if l == DEPTH - 1:
                    dve.wait_ge(router_hi, 1)
                    V.tensor_tensor(router[1][:, :, 0:NE], wrt[:, :, :], router[0][:, :, 0:NE].bitcast(F32),
                                    ALU.subtract).then_inc(router_lo, 1)
                lo_parts(room(("out", l, 0, 1)))
                norm_lo(3 * l + 2, hT, c_of["ffn"] + l * KD)
                lo_parts(room(("out", l, 1, 1), 1))
                if l % 2 == 0:
                    for c in range(FCD):
                        if c == MEM_AT - 2:
                            normalise_memory(2)
                        if c == MEM_AT:
                            lo_parts(room(("up", l, c - 1), 1))
                            norm_lo(3 * l + 3, mT, c_of["mem"])
                        lo_parts(room(("up", l, c)))
                        dve.wait_ge(silu_ready, c + 1)
                        b = banks[groups["up", l, c].bank]
                        g = g32_d[:, c % 2, :]
                        part = [v[:, c // BD % 2, c % BD, :] for v in gated_d]
                        link(V.tensor_tensor(g, silu_d[:, c % 4, :], b[:, SEQ:2 * SEQ], ALU.mult))
                        link(V.tensor_copy(part[0], g))
                        free(V.tensor_tensor(part[1], g, part[0].bitcast(F32), ALU.subtract), ("up", l, c))

            for t in range(T):
                dve.wait_ge(hn_hi, t + 1)
                V.tensor_tensor(hn_part[1][:, t, :], hn[:, t, :], hn_part[0][:, t, :].bitcast(F32),
                                ALU.subtract).then_inc(hn_lo, 1)
            l = DEPTH - 1
            b = full(dve, ("logT", l))
            free(V.tensor_copy(logT, b[0:NE, 0:SEQ]), ("logT", l))
            b = full(dve, ("logits", l))
            free(V.tensor_copy(logits[:, :, :].rearrange("p t e -> p (t e)"), b[:, 0:T * NE]), ("logits", l))
            read(dve, ("logits", l))
            for t in range(T):
                link(V.max(top_v[:, t, :], logits[:, t, :]))
                link(V.max_index(top_i[:, t, :], top_v[:, t, :], logits[:, t, :]))
            link(V.tensor_copy(top_f[:, :, :], top_i[:, :, :]))
            V.tensor_tensor(gap[:, 0, :], top_v[:, :, 1], top_v[:, :, 0], ALU.subtract).then_inc(gap_ready, 1)
            dve.wait_ge(consts, N_CONST)
            for n in range(2):
                for t in range(T):
                    ins = V.tensor_scalar(hot[:, n, t, :], iota_e[:, :], top_f[:, t, n:n + 1], None, ALU.is_equal)
            link(ins)
            V.tensor_tensor(mask[:, :, :], hot[:, 0, :, :], hot[:, 1, :, :], ALU.add).then_inc(mask_ready, 1)
            dve.wait_ge(mask_ready, 1)
            dve.wait_ge(gap_exp, 1)
            link(V.tensor_scalar(gap[:, 2, :], gap[:, 1, :], 1.0, None, ALU.add))
            link(V.reciprocal(gap[:, 3, :], gap[:, 2, :]))
            link(V.tensor_tensor(gap[:, 2, :], gap[:, 1, :], gap[:, 3, :], ALU.mult))
            for t in range(T):
                link(V.tensor_scalar(comb[:, t, 0:NE], hot[:, 0, t, :], gap[:, 3, t:t + 1], None, ALU.mult))
                link(V.scalar_tensor_tensor(out=comb[:, t, 0:NE], in0=hot[:, 1, t, :], scalar=gap[:, 2, t:t + 1],
                                            in1=comb[:, t, 0:NE], op0=ALU.mult, op1=ALU.add))
            for p in range(1, JOBS // NE):
                ins = V.tensor_copy(comb[:, :, p * NE:(p + 1) * NE], comb[:, :, 0:NE])
            link(ins)
            b = full(dve, ("rank", l))
            rk = logits[:, :, :]
            link(V.scalar_tensor_tensor(out=rk, in0=b[:, 0:T * NE].rearrange("p (t e) -> p t e", t=T), scalar=1.0,
                                        in1=mask[:, :, :], op0=ALU.add, op1=ALU.mult))
            free(V.tensor_reduce(most[:, 0:1], b[:, 2 * NE:3 * NE], AX_X, ALU.max), ("rank", l))
            for p in range(JOBS // NE):
                ins = V.tensor_scalar(rank[:, :, p * NE:(p + 1) * NE], rk, -1.0 - p * CAP, None, ALU.add)
            link(ins)
            read(dve, ("rank", l))
            V.tensor_scalar(more[:, :], most[:, 0:1], float(CAP), None, ALU.is_gt).then_inc(flag_ready, 1)

            def select(j):
                for t in range(T):
                    ins = V.tensor_scalar(sel[:, t, :], iota_cap[:, :], cur[:, 0, t:t + 1], None, ALU.is_equal)
                ins.then_inc(sel_ready, 1)

            gain = c_of["ffn"] + (DEPTH - 1) * KD

            def rows_T(name, n, j, nth):
                b = full(dve, name, j)
                dve.wait_ge(rows_hi, nth)
                for c in range(4):
                    part = [v[:, n, c * CAP:(c + 1) * CAP] for v in hselT]
                    ins = V.scalar_tensor_tensor(out=part[1], in0=b[:, c * CAP:(c + 1) * CAP],
                                                 scalar=cols[:, gain + 4 * n + c:gain + 4 * n + c + 1],
                                                 in1=part[0].bitcast(F32), op0=ALU.mult, op1=ALU.subtract)
                free(ins, name)

            V.tensor_copy(cur[:, 0, :], rank[:, :, 0]).then_inc(cur_ready, 1)
            dve.wait_ge(cur_ready, 1)
            select(0)
            for n in range(2):
                rows_T(("gather0", l, n), n, 0, n + 1)

            def expert(j):
                n_lo = EARLY

                def lo_parts(i_end):
                    nonlocal n_lo
                    for i in range(n_lo, i_end):
                        s = (E0 + i) % SPLIT
                        dve.wait_ge(hi_ready, PER_E * j + (E0 + i + 1))
                        V.tensor_tensor(wlo[:, s, :], raw[:, i % RAW, :], whi[:, s, :].bitcast(F32),
                                        ALU.subtract).then_inc(lo_ready, 1)
                    n_lo = max(n_lo, i_end)

                def hidden_lo(b_):
                    lo_parts(job_room(("eT", b_)))
                    b = full(dve, ("eT", b_), j)
                    dve.wait_ge(g_hi, NM * j + (b_ + 1))
                    free(V.tensor_tensor(gated_m[1][:, b_ % 2, :], b[:, :], gated_m[0][:, b_ % 2, :].bitcast(F32),
                                         ALU.subtract), ("eT", b_))

                for b_ in range(NM):
                    lo_parts(job_room(("e1", b_)))
                    if b_:
                        hidden_lo(b_ - 1)
                    lo_parts(job_room(("e3", b_)))
                    b = full(dve, ("e3", b_), j)
                    read(dve, ("e1", b_), j)
                    free(V.tensor_tensor(g32_m[:, b_ % 2, :], silu_m[:, b_ % 2, :], b[:, :], ALU.mult), ("e3", b_))
                    if b_ == 1:
                        full(dve, ("selT", 0), j)
                        V.tensor_copy(cur[:, 0, :], rank[:, :, bass.ds(j + 1, 1)].rearrange("p t o -> p (t o)")).then_inc(cur_ready, 1)
                        V.tensor_copy(cur[:, 1, :], comb[:, :, bass.ds(j, 1)].rearrange("p t o -> p (t o)")).then_inc(cur_ready, 1)
                        dve.wait_ge(cur_ready, 2 * j + 3)
                        select(j + 1)
                hidden_lo(NM - 1)
                for n in range(2):
                    rows_T(("gather", n), n, j, 2 * j + (n + 3))
                lo_parts(job_room(("gather", 1)))
                for n in range(2):
                    b = full(dve, ("ey", n), j)
                    dve.wait_ge(ey_hi, 2 * j + (n + 1))
                    part = [v[:, n * HALF:(n + 1) * HALF] for v in y_part]
                    free(V.tensor_tensor(part[1], b[:, :], part[0].bitcast(F32), ALU.subtract), ("ey", n))
                for n in range(2):
                    for t in range(T):
                        if n + t == 1:
                            lo_parts(job_room(("scatter", 0)))
                        name = ("scatter", 2 * n + t)
                        read(dve, name, j - 1)
                        b = full(dve, name, j)
                        xs = x_sb[:, t, n * HALF:(n + 1) * HALF]
                        free(V.scalar_tensor_tensor(out=xs, in0=b[:, :], scalar=cur[:, 1, t:t + 1], in1=xs,
                                                    op0=ALU.mult, op1=ALU.add), name)
                lo_parts(PER_E + EARLY)

            with dve.Fori(0, NE) as j:
                expert(j)
            dve.wait_ge(flag_ready, 1)
            overflow = dve.value_load(more[0:1, 0:1], min_val=0, max_val=1)
            with dve.If(overflow > 0):
                with dve.Fori(NE, JOBS) as j:
                    expert(j)
            dve.wait_ge(gf_in, 16)
            row_scales(-1)
            for t in range(T):
                V.scalar_tensor_tensor(out=hn[:, t, :], in0=x_sb[:, t, :], scalar=rin[:, 6 + t:7 + t], in1=gf_row,
                                       op0=ALU.mult, op1=ALU.mult).then_inc(y_final, 1)


_INS = ['x', 'mem', 'positions', 'g_mix', 'w_in', 'g_q', 'g_kv', 'w_uq', 'w_uk', 'w_uv', 'g_sg', 'w_s',
        'b_s', 'g_mem', 'w_mkv', 'w_br', 'b_gate', 'w_out', 'g_ffn', 'dense_w1', 'dense_w3', 'dense_w2',
        'w_router', 'moe_w1', 'moe_w3', 'moe_w2', 'g_final']


def kernel(**inputs):
    from concourse import bacc
    from concourse.bass_utils import run_bass_kernel_spmd

    nc = bacc.Bacc("TRN2", target_bir_lowering=False, num_devices=1)
    arrays, args = {}, []
    for name in _INS:
        a = np.ascontiguousarray(inputs[name])
        arrays[f"in_{name}"] = a
        args.append(nc.dram_tensor(f"in_{name}", a.shape, mybir.dt.from_np(a.dtype), kind="ExternalInput").ap())
    args.append(nc.dram_tensor("out", inputs["x"].shape, F32, kind="ExternalOutput").ap())
    build(nc, *args)
    return run_bass_kernel_spmd(nc, [arrays], core_ids=[0]).results[0]["out"]
```
